# Optimizing a Trainium2 kernel written in Bass

```python
import math
import jax, jax.numpy as jnp
from jax import lax
import numpy as np

D_MODEL = 1024
BATCH = 1
SEQ = 512
DEPTH = 2

CONV_CH = D_MODEL // 2
CONV_WIDTH = 31
SGU_CH = D_MODEL // 2
SGU_GROUPS = 8
SGU_GROUP_CH = SGU_CH // SGU_GROUPS
SGU_CHUNK = 128
EVEN_IN = 2 * CONV_CH + 2 * SGU_CH
ATTN_GROUPS = ((128, 1), (512, 4), (2048, 16))
N_ATTN_GROUPS = len(ATTN_GROUPS)
HEADS_PER_GROUP = 8
HEAD_DIM = 128
ATTN_WIDTH = HEADS_PER_GROUP * HEAD_DIM
ODD_IN = N_ATTN_GROUPS * 3 * ATTN_WIDTH
ATTN_BLOCK = 128
ROT_DIM = HEAD_DIM // 4
ROPE_THETA = 500000.0
FFN_HIDDEN = ((-(-8 * D_MODEL // 3) + 255) // 256) * 256
N_EVEN = (DEPTH + 1) // 2
N_ODD = DEPTH // 2
DN_ALPHA = (2.0 * DEPTH) ** 0.25
DN_BETA = (8.0 * DEPTH) ** -0.25
LN_EPS = 1e-5

kernel_name = 'hybrid_conv_sgu_dilated_attn_deepnorm'

def layer_norm(x, g, b):
    xf = x.astype(jnp.float32)
    mu = jnp.mean(xf, axis=-1, keepdims=True)
    xc = xf - mu
    var = jnp.mean(xc * xc, axis=-1, keepdims=True)
    y = xc * lax.rsqrt(var + LN_EPS)
    return (y * g.astype(jnp.float32) + b.astype(jnp.float32)).astype(x.dtype)

def partial_rope(t, positions):
    half = ROT_DIM // 2
    inv_freq = ROPE_THETA ** (-jnp.arange(0, ROT_DIM, 2, dtype=jnp.float32) / ROT_DIM)
    ang = positions.astype(jnp.float32)[..., None] * inv_freq
    cos = jnp.cos(ang)[:, :, None, :]
    sin = jnp.sin(ang)[:, :, None, :]
    tf = t.astype(jnp.float32)
    r1, r2, rest = tf[..., :half], tf[..., half:ROT_DIM], tf[..., ROT_DIM:]
    out = jnp.concatenate([r1 * cos - r2 * sin, r2 * cos + r1 * sin, rest], axis=-1)
    return out.astype(t.dtype)

def dilated_window_attention(q, k, v, dilation, steps):
    B, S, H, Dh = q.shape
    Q = ATTN_BLOCK
    L = -(-S // dilation)
    L = -(-L // Q) * Q
    nb = L // Q
    S_pad = L * dilation
    pad = ((0, 0), (0, S_pad - S), (0, 0), (0, 0))

    def to_streams(t):
        t = jnp.pad(t, pad).reshape(B, L, dilation, H, Dh)
        return t.transpose(0, 2, 3, 1, 4).reshape(B, dilation, H, nb, Q, Dh)

    def with_prev(t):
        prev = jnp.pad(t, ((0, 0), (0, 0), (0, 0), (1, 0), (0, 0), (0, 0)))[:, :, :, :-1]
        return jnp.concatenate([prev, t], axis=4)

    qs = to_streams(q)
    kb = with_prev(to_streams(k))
    vb = with_prev(to_streams(v))
    s = jnp.einsum('brhnqd,brhnkd->brhnqk', qs, kb,
                   preferred_element_type=jnp.float32) * (Dh ** -0.5)
    qi = jnp.arange(Q)[:, None]
    kj = jnp.arange(2 * Q)[None, :]
    dist = Q + qi - kj
    band = (dist >= 0) & (dist <= steps)
    has_prev = (jnp.arange(nb)[:, None, None] > 0) | (kj[None] >= Q)
    valid = band[None] & has_prev
    s = jnp.where(valid, s, -jnp.inf)
    m = jnp.max(s, axis=-1, keepdims=True)
    p = jnp.exp(s - m)
    denom = jnp.sum(p, axis=-1, keepdims=True)
    o = jnp.einsum('brhnqk,brhnkd->brhnqd', p, vb.astype(jnp.float32)) / denom
    lse = (m + jnp.log(denom))[..., 0]
    o = o.reshape(B, dilation, H, L, Dh).transpose(0, 3, 1, 2, 4).reshape(B, S_pad, H, Dh)[:, :S]
    lse = lse.reshape(B, dilation, H, L).transpose(0, 3, 1, 2).reshape(B, S_pad, H)[:, :S]
    return o, lse

def conv_sgu_mixer(x, w_in, conv_w, conv_b, conv_ln_g, conv_ln_b,
                   sgu_ln_g, sgu_ln_b, w_spatial, b_spatial, w_out):
    B, S, _ = x.shape
    h = x @ w_in
    a_val = h[..., :CONV_CH]
    a_gate = h[..., CONV_CH:2 * CONV_CH]
    z = h[..., 2 * CONV_CH:]
    a = a_val * jax.nn.sigmoid(a_gate)
    a = lax.conv_general_dilated(a, conv_w[:, None, :].astype(a.dtype), window_strides=(1,),
                                 padding=[(CONV_WIDTH - 1, 0)],
                                 dimension_numbers=('NWC', 'WIO', 'NWC'),
                                 feature_group_count=CONV_CH) + conv_b
    a = jax.nn.silu(layer_norm(a, conv_ln_g, conv_ln_b))
    z = jax.nn.gelu(z, approximate=False)
    u, v = z[..., :SGU_CH], z[..., SGU_CH:]
    v = layer_norm(v, sgu_ln_g, sgu_ln_b).reshape(B, S // SGU_CHUNK, SGU_CHUNK, SGU_GROUPS, SGU_GROUP_CH)
    causal = jnp.tril(jnp.ones((SGU_CHUNK, SGU_CHUNK), dtype=w_spatial.dtype))
    sv = jnp.einsum('hts,bnshc->bnthc', w_spatial * causal, v) + b_spatial.T[None, None, :, :, None]
    g = u * sv.reshape(B, S, SGU_CH)
    return jnp.concatenate([a, g], axis=-1) @ w_out

def dilated_attention_mixer(x, positions, w_qkv, w_out):
    B, S, _ = x.shape
    qkv = (x @ w_qkv).reshape(B, S, N_ATTN_GROUPS, 3, HEADS_PER_GROUP, HEAD_DIM)
    outs, lses = [], []
    for gi, (window, dilation) in enumerate(ATTN_GROUPS):
        q = partial_rope(qkv[:, :, gi, 0], positions)
        k = partial_rope(qkv[:, :, gi, 1], positions)
        v = qkv[:, :, gi, 2]
        o, lse = dilated_window_attention(q, k, v, dilation, window // dilation)
        outs.append(o)
        lses.append(lse)
    wts = jax.nn.softmax(jnp.stack(lses, axis=0), axis=0)
    o = jnp.sum(wts[..., None] * jnp.stack(outs, axis=0), axis=0)
    return o.reshape(B, S, ATTN_WIDTH).astype(x.dtype) @ w_out

def swiglu(x, w_gate, w_up, w_down):
    return (jax.nn.silu(x @ w_gate) * (x @ w_up)) @ w_down

def setup_inputs(seed: int = 0) -> dict:
    key = jax.random.key(seed)
    ks = jax.random.split(key, 20)
    f32 = jnp.float32

    def nrm(k, shape, scale):
        return jax.random.normal(k, shape, f32) * scale

    x = jax.random.normal(ks[0], (BATCH, SEQ, D_MODEL), f32)
    positions = jnp.broadcast_to(jnp.arange(SEQ, dtype=jnp.int32), (BATCH, SEQ))
    ev_w_in = nrm(ks[1], (N_EVEN, D_MODEL, EVEN_IN), D_MODEL ** -0.5)
    ev_conv_w = nrm(ks[2], (N_EVEN, CONV_WIDTH, CONV_CH), CONV_WIDTH ** -0.5)
    ev_conv_b = nrm(ks[3], (N_EVEN, CONV_CH), 0.02)
    ev_conv_ln_g = 1.0 + nrm(ks[4], (N_EVEN, CONV_CH), 0.05)
    ev_conv_ln_b = nrm(ks[5], (N_EVEN, CONV_CH), 0.02)
    ev_sgu_ln_g = 1.0 + nrm(ks[6], (N_EVEN, SGU_CH), 0.05)
    ev_sgu_ln_b = nrm(ks[7], (N_EVEN, SGU_CH), 0.02)
    ev_w_spatial = nrm(ks[8], (N_EVEN, SGU_GROUPS, SGU_CHUNK, SGU_CHUNK), SGU_CHUNK ** -0.5)
    ev_b_spatial = 1.0 + nrm(ks[9], (N_EVEN, SGU_GROUPS, SGU_CHUNK), 0.1)
    ev_w_out = nrm(ks[10], (N_EVEN, CONV_CH + SGU_CH, D_MODEL), DN_BETA * (CONV_CH + SGU_CH) ** -0.5)
    od_w_qkv = nrm(ks[11], (N_ODD, D_MODEL, ODD_IN), D_MODEL ** -0.5)
    od_w_out = nrm(ks[12], (N_ODD, ATTN_WIDTH, D_MODEL), DN_BETA * ATTN_WIDTH ** -0.5)
    ffn_w_gate = nrm(ks[13], (DEPTH, D_MODEL, FFN_HIDDEN), D_MODEL ** -0.5)
    ffn_w_up = nrm(ks[14], (DEPTH, D_MODEL, FFN_HIDDEN), D_MODEL ** -0.5)
    ffn_w_down = nrm(ks[15], (DEPTH, FFN_HIDDEN, D_MODEL), DN_BETA * FFN_HIDDEN ** -0.5)
    ln_g = 1.0 + nrm(ks[16], (DEPTH, 2, D_MODEL), 0.05)
    ln_b = nrm(ks[17], (DEPTH, 2, D_MODEL), 0.02)
    return {'x': x, 'positions': positions,
            'ev_w_in': ev_w_in, 'ev_conv_w': ev_conv_w, 'ev_conv_b': ev_conv_b,
            'ev_conv_ln_g': ev_conv_ln_g, 'ev_conv_ln_b': ev_conv_ln_b,
            'ev_sgu_ln_g': ev_sgu_ln_g, 'ev_sgu_ln_b': ev_sgu_ln_b,
            'ev_w_spatial': ev_w_spatial, 'ev_b_spatial': ev_b_spatial, 'ev_w_out': ev_w_out,
            'od_w_qkv': od_w_qkv, 'od_w_out': od_w_out,
            'ffn_w_gate': ffn_w_gate, 'ffn_w_up': ffn_w_up, 'ffn_w_down': ffn_w_down,
            'ln_g': ln_g, 'ln_b': ln_b}

def reference(x, positions, ev_w_in, ev_conv_w, ev_conv_b, ev_conv_ln_g, ev_conv_ln_b,
              ev_sgu_ln_g, ev_sgu_ln_b, ev_w_spatial, ev_b_spatial, ev_w_out,
              od_w_qkv, od_w_out, ffn_w_gate, ffn_w_up, ffn_w_down, ln_g, ln_b):
    for layer in range(DEPTH):
        i = layer // 2
        if layer % 2 == 0:
            h = conv_sgu_mixer(x, ev_w_in[i], ev_conv_w[i], ev_conv_b[i], ev_conv_ln_g[i], ev_conv_ln_b[i],
                               ev_sgu_ln_g[i], ev_sgu_ln_b[i], ev_w_spatial[i], ev_b_spatial[i], ev_w_out[i])
        else:
            h = dilated_attention_mixer(x, positions, od_w_qkv[i], od_w_out[i])
        x = layer_norm(DN_ALPHA * x + h, ln_g[layer, 0], ln_b[layer, 0])
        x = layer_norm(DN_ALPHA * x + swiglu(x, ffn_w_gate[layer], ffn_w_up[layer], ffn_w_down[layer]),
                       ln_g[layer, 1], ln_b[layer, 1])
    return x


_drawn_inputs = setup_inputs


def setup_inputs(seed=0):
    import zlib

    import numpy as np

    out = dict(_drawn_inputs(seed))
    spreads = {}
    factors = {'ev_conv_b': 8.0,
     'ev_conv_ln_g': 6.241,
     'ev_conv_ln_b': 25.919,
     'ev_sgu_ln_g': 8.0,
     'ev_sgu_ln_b': 43.976,
     'ev_b_spatial': 3.469}
    for name, (base, spread) in spreads.items():
        noise = np.random.default_rng([zlib.crc32(name.encode()), seed]).standard_normal(out[name].shape)
        drawn = base * np.exp(spread * noise) if base else spread * noise
        out[name] = __import__('jax').numpy.asarray(drawn.astype(out[name].dtype))
    for name, factor in factors.items():
        out[name] = (out[name] * factor).astype(out[name].dtype)
    return out
```

```python
from contextlib import ExitStack

import numpy as np

import concourse.bass as bass
from concourse import mybir

F32 = mybir.dt.float32
F32R = mybir.dt.float32r
I32 = mybir.dt.int32
ACT = mybir.ActivationFunctionType
ALU = mybir.AluOpType
AXX = mybir.AxisListType.X

P = 128
D_MODEL = 1024
SEQ = 512
TILES = SEQ // P
KD = D_MODEL // P
CONV_CH = D_MODEL // 2
CONV_WIDTH = 31
PAD = CONV_WIDTH - 1
CC = CONV_CH // P
SGU_GROUPS = 8
GROUP_CH = CONV_CH // SGU_GROUPS
HEADS = 8
DH = 128
ROT = DH // 4
ROPE_THETA = 500000.0
NG = 3
DIL = 4
FFN = 2816
KF = FFN // P
ALPHA = 4.0 ** 0.25
EPS = 1e-5
SCALE = float(DH) ** -0.5
MASKED = -3.0e38
SLAB = 2048

N_IN, N_OUT, N_UP, N_DOWN, N_ATT = 8, 4, KF, KF // 2, 36
S_IN = 0
S_OUT0 = S_IN + N_IN
S_UP0 = S_OUT0 + N_OUT
S_DOWN0 = S_UP0 + N_UP
S_ATT = S_DOWN0 + N_DOWN
S_OUT1 = S_ATT + N_ATT
S_UP1 = S_OUT1 + N_OUT
S_DOWN1 = S_UP1 + N_UP
N_SLABS = S_DOWN1 + N_DOWN
HEADS_ROUND = 2
ROUND_SLABS = HEADS_ROUND * NG + NG
ROUNDS_BODY = 2
TURNS = HEADS // (HEADS_ROUND * ROUNDS_BODY)
BLOCKS_A = 2 * TILES - 1
BLOCKS = BLOCKS_A + 2 * TILES
C_MASKA, C_MASKB, C_L, C_LT, C_R, C_UT, C_FREQ, C_SIGN = 0, 512, 1024, 1536, 2048, 2052, 2180, 2181
N_CONST = 2182

TWO_PI = 2.0 * np.pi
BIG = 2048.0
PI_A = (6.25, 17.0 / 512.0)
PI_A += (float(np.float32(np.round((TWO_PI - sum(PI_A)) * 2.0 ** 22) / 2.0 ** 22)),)
PI_A4 = float(np.float32(TWO_PI - sum(PI_A)))
PI_B1 = float(np.round(TWO_PI * 2.0 ** 9) / 2.0 ** 9)
PI_B2 = float(np.round((TWO_PI - PI_B1) * 2.0 ** 21) / 2.0 ** 21)
PI_B3 = float(np.float32(TWO_PI - PI_B1 - PI_B2))
ROUND_MAGIC = 1.5 * 2.0 ** 23
PI_SAFE = 3.1415925


def constant_table():
    c = np.zeros((P, N_CONST), np.float32)
    row, col = np.arange(P)[:, None], np.arange(P)[None, :]
    own = np.where(row >= col, 0.0, MASKED)
    prev = np.where(col >= row, 0.0, MASKED)
    own_step4 = np.where((row >= col) & (row % 4 == col % 4), 0.0, MASKED)
    c[:, C_MASKA:C_MASKA + 512] = np.concatenate([prev, own, prev, own], 1)
    c[:, C_MASKB:C_MASKB + 512] = np.concatenate([own, own_step4, own, own_step4], 1)
    for i in range(TILES):
        c[:, C_L + i * P:C_L + (i + 1) * P] = col == 32 * i + row // DIL
        c[:, C_LT + i * P:C_LT + (i + 1) * P] = row == 32 * i + col // DIL
    c[:, C_R:C_R + DIL] = row % DIL == np.arange(DIL)[None, :]
    c[:, C_UT:C_UT + P] = col >= row
    half = ROT // 2
    freq = (ROPE_THETA ** (-np.arange(0, ROT, 2, dtype=np.float64) / ROT)).astype(np.float32)
    c[:ROT, C_FREQ] = np.concatenate([freq, freq])
    c[:ROT, C_SIGN] = np.concatenate([-np.ones(half), np.ones(half)])
    return c


def trunk(nc, x, positions, ev_w_in, ev_conv_w, ev_conv_b, ev_conv_ln_g, ev_conv_ln_b, ev_sgu_ln_g,
          ev_sgu_ln_b, ev_w_spatial, ev_b_spatial, ev_w_out, od_w_qkv, od_w_out, ffn_w_gate, ffn_w_up,
          ffn_w_down, ln_g, ln_b, ident_in, const_in, out):
    ctx = ExitStack()
    with ctx:
        def sb(name, shape, dt=F32, scope=ctx):
            return scope.enter_context(nc.sbuf_tensor(name, shape, dt))

        def sem(name):
            return ctx.enter_context(nc.semaphore(name))

        x_res = sb("x_res", [P, TILES, D_MODEL])
        xt_hi = sb("xt_hi", [P, KD, SEQ], F32R)
        xt_lo = sb("xt_lo", [P, KD, SEQ], F32R)
        w_stage = [sb(f"w_stage{j}", [P, SLAB]) for j in range(2)]
        w_hi = [sb(f"w_hi{j}", [P, SLAB], F32R) for j in range(2)]
        w_lo = [sb(f"w_lo{j}", [P, SLAB], F32R) for j in range(2)]
        ident = sb("ident", [P, P])
        ones = sb("ones", [P, P])
        cos_t = sb("cos_t", [ROT, SEQ])
        sin_t = sb("sin_t", [ROT, SEQ])
        cst = sb("cst", [P, N_CONST])
        norm_g = sb("norm_g", [P, D_MODEL])
        norm_b = sb("norm_b", [P, D_MODEL])
        stats = sb("stats", [P, 2 * 6])
        mean_var = sb("mean_var", [P, TILES, 2])
        std = sb("std", [P, TILES])
        rstd = sb("rstd", [P, TILES])
        eps = sb("eps", [P, 1])
        ps = [ctx.enter_context(nc.psum_tensor(f"ps{j}", [P, 512], F32)) for j in range(8)]

        with ExitStack() as s:
            mix_hi = sb("mix_hi", [P, KD, SEQ], F32R, s)
            mix_lo = sb("mix_lo", [P, KD, SEQ], F32R, s)
            a_pad = sb("a_pad", [P, CC, PAD + SEQ], F32, s)
            acc = sb("acc", [P, CC, SEQ], F32, s)
            u_t = sb("u_t", [P, CC, SEQ], F32, s)
            v_tok = sb("v_tok", [P, TILES, CONV_CH], F32, s)
            wsp_raw = sb("wsp_raw", [P, SGU_GROUPS, P], F32, s)
            wsp_t = sb("wsp_t", [P, SGU_GROUPS, P], F32, s)
            b_sp = sb("b_sp", [P, CC, P], F32, s)
            sgu_g = sb("sgu_g", [P, CONV_CH], F32, s)
            sgu_b = sb("sgu_b", [P, CONV_CH], F32, s)
            sig = sb("sig", [P, 2, SEQ], F32, s)
            mixed = sb("mixed", [P, 2, SEQ], F32, s)
            par_rows = sb("par_rows", [P, 512 + P], F32, s)
            par = sb("par", [P, CC * CONV_WIDTH + 12], F32, s)
            rot_tmp = u_t[0:ROT]
            pos_i = acc[0:ROT, 0, :].bitcast(I32)
        with ExitStack() as s:
            ht_hi = sb("ht_hi", [P, KF, SEQ], F32R, s)
            ht_lo = sb("ht_lo", [P, KF, SEQ], F32R, s)
            hidden = sb("hidden", [P, 1, SEQ], F32, s)
        with ExitStack() as s:
            ot_hi = sb("ot_hi", [P, HEADS, SEQ], F32R, s)
            ot_lo = sb("ot_lo", [P, HEADS, SEQ], F32R, s)
            probs = sb("probs", [P, HEADS_ROUND, BLOCKS * P], F32, s)
            probs_t = sb("probs_t", [P, 4 * 512], F32, s)
            v_att = sb("v_att", [P, NG, TILES, HEADS_ROUND * DH], F32, s)
            qk = sb("qk", [P, 2, 2, SEQ], F32, s)
            rot_a = sb("rot_a", [ROT, 2, SEQ], F32, s)
            rot_b = sb("rot_b", [ROT, 2, SEQ], F32, s)
            o_near = sb("o_near", [P, SEQ], F32, s)
            o_sum = sb("o_sum", [P, SEQ], F32, s)
            st_near = sb("st_near", [P, 2, HEADS_ROUND, TILES], F32, s)
            st_far = sb("st_far", [P, 2, HEADS_ROUND, TILES], F32, s)
            far_sel = sb("far_sel", [P, 16, 4], F32, s)
            far_nat = sb("far_nat", [P, TILES, 2, HEADS_ROUND], F32, s)
            m_low = sb("m_low", [P, HEADS_ROUND, TILES], F32, s)
            m_diff = sb("m_diff", [P, 2, HEADS_ROUND, TILES], F32, s)
            m_exp = sb("m_exp", [P, 2, HEADS_ROUND, TILES], F32, s)
            m_w = sb("m_w", [P, 2, HEADS_ROUND, TILES], F32, s)
            m_den = sb("m_den", [P, HEADS_ROUND, TILES], F32, s)
            m_fac = sb("m_fac", [P, 2, HEADS_ROUND, TILES], F32, s)
            fac_sel = sb("fac_sel", [P, TILES, HEADS_ROUND, DIL], F32, s)
            fac_far = sb("fac_far", [P, HEADS_ROUND, DIL], F32, s)

        w_loaded = [sem(f"w_loaded{j}") for j in range(2)]
        w_hi_ready = sem("w_hi_ready")
        w_lo_ready = sem("w_lo_ready")
        w_used = sem("w_used")
        x_loaded = [sem(f"x_loaded{i}") for i in range(TILES)]
        ident_loaded = sem("ident_loaded")
        rot_loaded = sem("rot_loaded")
        wsp_loaded = sem("wsp_loaded")
        par_loaded = sem("par_loaded")
        sgu_loaded = sem("sgu_loaded")
        ln_loaded = [sem(f"ln_loaded{e}") for e in range(4)]
        cst_loaded = sem("cst_loaded")
        out_stored = sem("out_stored")
        ones_set = sem("ones_set")
        pad_set = sem("pad_set")
        dve_link = sem("dve_link")
        act_link = sem("act_link")
        par_turned = sem("par_turned")
        par_set = sem("par_set")
        wsp_turned = sem("wsp_turned")
        wsp_set = sem("wsp_set")
        xt_turned = sem("xt_turned")
        xt_hi_set = sem("xt_hi_set")
        xt_set = sem("xt_set")
        sig_set = sem("sig_set")
        a_set = sem("a_set")
        acc_set = sem("acc_set")
        v_in = sem("v_in")
        v_gelu = sem("v_gelu")
        v_var = sem("v_var")
        v_std = sem("v_std")
        v_set = sem("v_set")
        u_in = sem("u_in")
        u_set = sem("u_set")
        sv_done = sem("sv_done")
        sv_read = sem("sv_read")
        g_set = sem("g_set")
        mixhi_set = sem("mixhi_set")
        mixlo_set = sem("mixlo_set")
        mean_done = sem("mean_done")
        xc_set = sem("xc_set")
        sq_set = sem("sq_set")
        var_done = sem("var_done")
        std_set = sem("std_set")
        y_set = sem("y_set")
        silu_set = sem("silu_set")
        acc_done = sem("acc_done")
        res_added = sem("res_added")
        ln_var = sem("ln_var")
        ln_std = sem("ln_std")
        x_normed = sem("x_normed")
        up_done = sem("up_done")
        gate_set = sem("gate_set")
        hid_set = sem("hid_set")
        hthi_set = sem("hthi_set")
        ht_set = sem("ht_set")
        qk_copied = sem("qk_copied")
        qk_set = sem("qk_set")
        near_done = sem("near_done")
        far_done = sem("far_done")
        max_set = sem("max_set")
        exp_set = sem("exp_set")
        v_copied = sem("v_copied")
        far_turned = sem("far_turned")
        angles_set = sem("angles_set")
        tables_set = sem("tables_set")
        diff_set = sem("diff_set")
        diff_exp = sem("diff_exp")
        fac_set = sem("fac_set")
        fac_turned = sem("fac_turned")
        fac_copied = sem("fac_copied")
        probs_set = sem("probs_set")
        pt_done = sem("pt_done")
        pt_copied = sem("pt_copied")
        o_done = sem("o_done")
        near_copied = sem("near_copied")
        o_set = sem("o_set")
        othi_set = sem("othi_set")
        ot_set = sem("ot_set")

        block = ctx.enter_context(nc.Block())

        class Link:

            def __init__(self, eng, which):
                self.eng, self.sem, self.n = eng, which, 0

            def mark(self, ins):
                ins.then_inc(self.sem, 1)
                self.n = self.n + 1
                return self.n

            def wait(self, value=None):
                self.eng.wait_ge(self.sem, self.n if value is None else value)

        def slab_views(slab):
            def up(layer, s):
                rows = lambda w: w[layer].rearrange("(k p) n -> p k n", p=P)[:, :, s * P:(s + 1) * P]
                return "cols", (rows(ffn_w_gate), rows(ffn_w_up))

            def square(w, k0, c0):
                rows = w.rearrange("(k p) n -> p k n", p=P)
                return "rows", tuple(rows[:, k:k + 2, c0:c0 + 512] for k in (k0, k0 + 2))

            def down(layer, s):
                rows = ffn_w_down[layer].rearrange("(k p) n -> p k n", p=P)
                return "rows", tuple(rows[:, k:k + 1, :] for k in (2 * s, 2 * s + 1))

            if slab < S_OUT0:
                s = slab - S_IN
                rows = ev_w_in[0].rearrange("(k p) n -> p k n", p=P)
                if s < 4:
                    return "cols", (rows[:, :, s * P:(s + 1) * P], rows[:, :, CONV_CH + s * P:CONV_CH + (s + 1) * P])
                if s < 6:
                    return square(ev_w_in[0], 4 * (s - 4), 3 * CONV_CH)
                c0 = 2 * CONV_CH + 2 * P * (s - 6)
                return "cols", (rows[:, :, c0:c0 + P], rows[:, :, c0 + P:c0 + 2 * P])
            if slab < S_UP0:
                s = slab - S_OUT0
                return square(ev_w_out[0], 4 * (1 - s // 2), 512 * (s % 2))
            if slab < S_DOWN0:
                return up(0, slab - S_UP0)
            if slab < S_ATT:
                return down(0, slab - S_DOWN0)
            if slab < S_OUT1 + 0:
                raise ValueError("attention slabs are addressed in their loop")
            if slab < S_UP1:
                s = slab - S_OUT1
                return square(od_w_out[0], 4 * (s // 2), 512 * (s % 2))
            if slab < S_DOWN1:
                return up(1, slab - S_UP1)
            return down(1, slab - S_DOWN1)

        @block.sync
        def _(sp):
            def load_halves(slab, turns, kind, halves):
                slot = slab % 2
                if slab >= 2:
                    sp.wait_ge(w_lo_ready, slab - 1 + 2 * turns)
                for j in range(2):
                    if kind == "cols":
                        dst = w_stage[slot][:, :].rearrange("p (k n) -> p k n", n=2 * P)[:, :, j * P:(j + 1) * P]
                    else:
                        k, n = halves[j].shape[1], halves[j].shape[2]
                        dst = w_stage[slot][:, j * 1024:(j + 1) * 1024].rearrange("p (k n) -> p k n", k=k)
                    sp.dma_start(dst, halves[j]).then_inc(w_loaded[slot], 16)

            def load(slab):
                load_halves(slab, 0, *slab_views(slab))

            def load_ln(e, layer, which):
                if e:
                    sp.wait_ge(x_normed, 2 * TILES * e)
                for dst, src in ((norm_g, ln_g), (norm_b, ln_b)):
                    sp.dma_start(dst[:, :], src[layer, which:which + 1, :].partition_broadcast(P)
                                 ).then_inc(ln_loaded[e], 16)

            sp.dma_start(ident[:, :], ident_in).then_inc(ident_loaded, 16)
            for i in range(TILES):
                sp.dma_start(x_res[:, i, :], x[0, i * P:(i + 1) * P, :]).then_inc(x_loaded[i], 16)
            load(0)
            load(1)
            sp.dma_start(cst[:, :], const_in).then_inc(cst_loaded, 16)
            sp.dma_start(pos_i, positions.partition_broadcast(ROT)).then_inc(rot_loaded, 16)
            sp.dma_start(par_rows[0:CONV_WIDTH, 0:CONV_CH], ev_conv_w[0]).then_inc(par_loaded, 16)
            for n, src in enumerate((ev_conv_b, ev_conv_ln_g, ev_conv_ln_b)):
                sp.dma_start(par_rows[4 * n:4 * n + 4, CONV_CH:CONV_CH + P],
                             src[0].rearrange("(c p) -> c p", p=P)).then_inc(par_loaded, 16)
            sp.dma_start(wsp_raw[:, :, :], ev_w_spatial[0].rearrange("h t s -> t h s")).then_inc(wsp_loaded, 16)
            sp.dma_start(sgu_g[:, :], ev_sgu_ln_g.partition_broadcast(P)).then_inc(sgu_loaded, 16)
            sp.dma_start(sgu_b[:, :], ev_sgu_ln_b.partition_broadcast(P)).then_inc(sgu_loaded, 16)
            for h in range(SGU_GROUPS):
                half = (h % 2) * GROUP_CH
                sp.dma_start(b_sp[half:half + GROUP_CH, h // 2, :],
                             ev_b_spatial[0, h:h + 1, :].partition_broadcast(GROUP_CH)).then_inc(sgu_loaded, 16)
            load_ln(0, 0, 0)
            for slab in range(2, S_UP0):
                load(slab)

            def load_up(first, layer):
                rows = [w[layer].rearrange("(k p) (s n) -> p k s n", p=P, n=P) for w in (ffn_w_gate, ffn_w_up)]
                with sp.Fori(0, N_UP // 2) as t:
                    for j in range(2):
                        load_halves(first + j, t, "cols", [r[:, :, 2 * t + j, :] for r in rows])

            def load_down(first, layer, e):
                rows = ffn_w_down[layer].rearrange("(k p) n -> p k n", p=P)
                load(first)
                load(first + 1)
                load_ln(e, layer, 1)
                with sp.Fori(1, N_DOWN // 2) as t:
                    for j in range(2):
                        load_halves(first + j, t, "rows",
                                    [rows[:, bass.ds(4 * t + 2 * j + c, 1), :] for c in range(2)])
                load(first + N_DOWN - 1)

            load_up(S_UP0, 0)
            load_down(S_DOWN0, 0, 1)
            qkv = od_w_qkv[0].rearrange("(k p) (g r y b h d) -> p k g r y b h d", p=P, g=NG, r=3, y=TURNS,
                                        b=ROUNDS_BODY, h=HEADS_ROUND)
            with sp.Fori(0, TURNS) as turn:
                for r in range(ROUNDS_BODY):
                    first = S_ATT + r * ROUND_SLABS
                    for s in range(HEADS_ROUND * NG):
                        load_halves(first + s, turn * (ROUNDS_BODY * ROUND_SLABS // 2), "cols",
                                    [qkv[:, :, s % NG, c, turn, r, s // NG, :] for c in range(2)])
                    for g in range(NG):
                        load_halves(first + HEADS_ROUND * NG + g, turn * (ROUNDS_BODY * ROUND_SLABS // 2), "cols",
                                    [qkv[:, :, g, 2, turn, r, h, :] for h in range(HEADS_ROUND)])
            load_ln(2, 1, 0)
            for slab in range(S_OUT1, S_UP1):
                load(slab)
            load_up(S_UP1, 1)
            load_down(S_DOWN1, 1, 3)
            for i in range(TILES):
                sp.wait_ge(x_normed, 6 * TILES + 2 * i + 2)
                sp.dma_start(out[0, i * P:(i + 1) * P, :], x_res[:, i, :]).then_inc(out_stored, 16)
            sp.wait_ge(out_stored, 16 * TILES)

        @block.gpsimd
        def _(pool):
            pool.memset(ones[:, :], 1.0 / CONV_CH).then_inc(ones_set, 1)
            pool.memset(eps[:, :], EPS).then_inc(ones_set, 1)
            pool.memset(a_pad[:, :, 0:PAD], 0.0).then_inc(pad_set, 1)

            def split_low(slab, turns=0):
                pool.wait_ge(w_hi_ready, slab + 1 + 2 * turns)
                pool.tensor_tensor(w_lo[slab % 2][:, :], w_stage[slab % 2][:, :],
                                   w_hi[slab % 2][:, :].bitcast(F32), ALU.subtract).then_inc(w_lo_ready, 1)

            for slab in range(S_UP0):
                split_low(slab)

            def feed_forward(up, down):
                with pool.Fori(0, N_UP // 2) as t:
                    for j in range(2):
                        split_low(up + j, t)
                with pool.Fori(0, N_DOWN // 2) as t:
                    for j in range(2):
                        split_low(down + j, t)
                split_low(down + N_DOWN - 1)

            feed_forward(S_UP0, S_DOWN0)
            with pool.Fori(0, N_ATT // 2) as t:
                for j in range(2):
                    split_low(S_ATT + j, t)
            for slab in range(S_OUT1, S_UP1):
                split_low(slab)
            feed_forward(S_UP1, S_DOWN1)

        @block.tensor
        def _(pe):
            def slab_ready(slab, turns=0):
                pe.wait_ge(w_lo_ready, slab + 1 + 2 * turns)

            def columns(slot, c, bank, x_hi=xt_hi, x_lo=xt_lo):
                hi, lo = (w[slot][:, :].rearrange("p (k n) -> p k n", n=2 * P)[:, :, c * P:(c + 1) * P]
                          for w in (w_hi, w_lo))
                for k in range(KD):
                    pe.matmul(ps[bank][:, :], hi[:, k, :], x_hi[:, k, :], start=(k == 0), stop=False)
                    pe.matmul(ps[bank][:, :], hi[:, k, :], x_lo[:, k, :], start=False, stop=False)
                    last = pe.matmul(ps[bank][:, :], lo[:, k, :], x_hi[:, k, :], start=False, stop=(k == KD - 1))
                return last

            def tokens(slot, base, width, bank, t_hi, t_lo, tile, first, end):
                hi, lo = (w[slot][:, base:base + width] for w in (w_hi, w_lo))
                o = ps[bank][:, 0:width]
                pe.matmul(o, t_hi[:, tile * P:(tile + 1) * P], hi, start=first, stop=False)
                pe.matmul(o, t_hi[:, tile * P:(tile + 1) * P], lo, start=False, stop=False)
                return pe.matmul(o, t_lo[:, tile * P:(tile + 1) * P], hi, start=False, stop=end)

            def turn_x(e, i):
                for half in range(2):
                    bank = ps[i + 4 * half]
                    if e:
                        pe.wait_ge(x_normed, 2 * TILES * (e - 1) + 2 * i + half + 1)
                    for c in range(4):
                        col = (4 * half + c) * P
                        last = pe.transpose(bank[:, c * P:(c + 1) * P], x_res[:, i, col:col + P], ident[:, :])
                    last.then_inc(xt_turned, 1)

            pe.wait_ge(ident_loaded, 16)
            for i in range(TILES):
                pe.wait_ge(x_loaded[i], 16)
                turn_x(0, i)
            def turn_parameters():
                pe.wait_ge(par_loaded, 16 * 4)
                for c in range(CC):
                    pe.transpose(ps[4][:, c * CONV_WIDTH:(c + 1) * CONV_WIDTH],
                                 par_rows[0:CONV_WIDTH, c * P:(c + 1) * P], ident[0:CONV_WIDTH, 0:CONV_WIDTH])
                pe.transpose(ps[4][:, CC * CONV_WIDTH:CC * CONV_WIDTH + 12], par_rows[0:12, CONV_CH:CONV_CH + P],
                             ident[0:12, 0:12]).then_inc(par_turned, 1)
                pe.wait_ge(wsp_loaded, 16)
                for half in range(2):
                    for h in range(4):
                        last = pe.transpose(ps[5 + half][:, h * P:(h + 1) * P], wsp_raw[:, 4 * half + h, :],
                                            ident[:, :])
                    last.then_inc(wsp_turned, 1)

            pe.wait_ge(xt_set, 2 * TILES)
            for s in range(CC):
                slab = S_IN + s
                slab_ready(slab)
                if s >= 2:
                    pe.wait_ge(a_set, s - 1)
                columns(slab % 2, 0, 2 * (s % 2))
                columns(slab % 2, 1, 2 * (s % 2) + 1).then_inc(w_used, 1)
                if s == 0:
                    turn_parameters()
            pe.wait_ge(par_set, 1)
            pe.wait_ge(wsp_set, 2)
            for s in range(2):
                slab = S_IN + 4 + s
                slab_ready(slab)
                for i in range(TILES):
                    for k in range(4):
                        last = tokens(slab % 2, 512 * k, 512, 4 + i, xt_hi[:, 4 * s + k, :], xt_lo[:, 4 * s + k, :],
                                      i, s == 0 and k == 0, s == 1 and k == 3)
                    if s == 1 and i < TILES - 1:
                        last.then_inc(v_in, 1)
                last.then_inc(w_used, 1)
            for s in range(2):
                slab = S_IN + 6 + s
                slab_ready(slab)
                pe.wait_ge(a_set, 3 + s)
                columns(slab % 2, 0, 2 * s).then_inc(u_in, 1)
                columns(slab % 2, 1, 2 * s + 1).then_inc(w_used, 1)
            pe.wait_ge(v_set, TILES)
            for pair in range(CC):
                for n in range(TILES):
                    for h in (2 * pair, 2 * pair + 1):
                        half = (h % 2) * GROUP_CH
                        last = pe.matmul(ps[4 + pair][half:half + GROUP_CH, n * P:(n + 1) * P],
                                         v_tok[:, n, h * GROUP_CH:(h + 1) * GROUP_CH], wsp_t[:, h, :],
                                         start=True, stop=True)
                last.then_inc(sv_done, 1)

            def mix_rows(slab, k0, half, i, first, end):
                for k in range(4):
                    last = tokens(slab % 2, 512 * k, 512, i + 4 * half, mix_hi[:, k0 + k, :], mix_lo[:, k0 + k, :],
                                  i, first and k == 0, end and k == 3)
                return last

            slab_ready(S_OUT0)
            pe.wait_ge(u_set, CC)
            pe.wait_ge(mixlo_set, CC)
            for i in range(TILES):
                last = mix_rows(S_OUT0, 4, 0, i, True, False)
            last.then_inc(w_used, 1)
            pe.wait_ge(ones_set, 1)
            for c in range(CC):
                pe.wait_ge(acc_set, c + 1)
                last = pe.matmul(ps[6][:, :], ones[:, :], acc[:, c, :], start=(c == 0), stop=(c == CC - 1))
            last.then_inc(mean_done, 1)
            for c in range(CC):
                pe.wait_ge(sq_set, c + 1)
                last = pe.matmul(ps[7][:, :], ones[:, :], acc[:, c, :], start=(c == 0), stop=(c == CC - 1))
            last.then_inc(var_done, 1)
            slab_ready(S_OUT0 + 1)
            pe.wait_ge(std_set, 1)
            for i in range(TILES):
                last = mix_rows(S_OUT0 + 1, 4, 1, i, True, False)
            last.then_inc(w_used, 1)

            def finish_tiles(e, slab_a, part_a, part_b):
                slab_ready(slab_a)
                slab_ready(slab_a + 1)
                for i in range(TILES):
                    last = part_a(i)
                    if i == TILES - 1:
                        last.then_inc(w_used, 1)
                    part_b(i).then_inc(w_used if i == TILES - 1 else acc_done, 1)
                    if i and e < 3:
                        turn_x(e + 1, i - 1)
                if e < 3:
                    turn_x(e + 1, TILES - 1)

            pe.wait_ge(mixlo_set, 2 * CC)
            finish_tiles(0, S_OUT0 + 2, lambda i: mix_rows(S_OUT0 + 2, 0, 0, i, False, True),
                         lambda i: mix_rows(S_OUT0 + 3, 0, 1, i, False, True))

            def feed_forward(layer, up, down, e):
                pe.wait_ge(xt_set, 2 * TILES * (e + 1))
                done = layer * KF

                def pair(t, j):
                    columns((up + j) % 2, 0, j).then_inc(up_done, 1)
                    columns((up + j) % 2, 1, 4 + j).then_inc(w_used, 1)

                for j in range(2):
                    slab_ready(up + j)
                    pair(0, j)
                with pe.Fori(1, N_UP // 2) as t:
                    for j in range(2):
                        slab_ready(up + j, t)
                        pe.wait_ge(hid_set, done + 2 * t + j - 1)
                        pair(t, j)

                def rows(slab, i, half, first, end, s):
                    for k in range(2):
                        last = tokens(slab % 2, 1024 * k + 512 * half, 512, i + 4 * half, ht_hi[:, 2 * s + k, :],
                                      ht_lo[:, 2 * s + k, :], i, first and k == 0, end and k == 1)
                    return last

                for s in range(N_DOWN - 2):
                    slab_ready(down + s)
                    pe.wait_ge(ht_set, done + 2 * s + 2)
                    if s == 0:
                        pe.wait_ge(hid_set, done + KF)
                    for i in range(TILES):
                        for half in range(2):
                            last = rows(down + s, i, half, s == 0, False, s)
                    last.then_inc(w_used, 1)
                pe.wait_ge(ht_set, done + KF)

                def both(s, end):
                    def part(i):
                        rows(down + s, i, 0, False, end, s)
                        return rows(down + s, i, 1, False, end, s)
                    return part

                finish_tiles(e, down + N_DOWN - 2, both(N_DOWN - 2, False), both(N_DOWN - 1, True))

            feed_forward(0, S_UP0, S_DOWN0, 1)

            pe.wait_ge(xt_set, 2 * TILES * 3)
            pe.wait_ge(cst_loaded, 16)
            lt = cst[:, C_LT:C_LT + TILES * P].rearrange("p (i n) -> p i n", i=TILES)
            lm = cst[:, C_L:C_L + TILES * P].rearrange("p (i n) -> p i n", i=TILES)
            with pe.Fori(0, TURNS) as turn:
                for r in range(ROUNDS_BODY):
                    rnd = turn * ROUNDS_BODY + r
                    first = S_ATT + r * ROUND_SLABS
                    passed = turn * (ROUNDS_BODY * ROUND_SLABS // 2)
                    n_qk = HEADS_ROUND * NG

                    def scores(s):
                        h, g = divmod(s, NG)
                        q, key = qk[:, s % 2, 0, :], qk[:, s % 2, 1, :]
                        pe.wait_ge(qk_set, rnd * n_qk + s + 1)
                        if h == 1 and g < 2:
                            pe.wait_ge(max_set, rnd * 2 * HEADS_ROUND + g + 1)
                        for i in range(TILES):
                            lhs = q[:, i * P:(i + 1) * P]
                            if g:
                                c = (i % 2) * 2 * P + (g - 1) * P
                                last = pe.matmul(ps[6 + i // 2][:, c:c + P], lhs, key[:, i * P:(i + 1) * P],
                                                 start=True, stop=True)
                            elif i == 0:
                                last = pe.matmul(ps[4][:, P:2 * P], lhs, key[:, 0:P], start=True, stop=True)
                            else:
                                c = (i % 2) * 2 * P
                                last = pe.matmul(ps[4 + i // 2][:, c:c + 2 * P], lhs,
                                                 key[:, (i - 1) * P:(i + 1) * P], start=True, stop=True)
                        last.then_inc(far_done if g else near_done, 1)

                    for s in range(n_qk):
                        slab_ready(first + s, passed)
                        if s >= 2:
                            pe.wait_ge(qk_copied, rnd * n_qk + s - 1)
                        columns((first + s) % 2, 0, 2 * (s % 2))
                        columns((first + s) % 2, 1, 2 * (s % 2) + 1).then_inc(w_used, 1)
                        if s:
                            scores(s - 1)
                    for g in range(NG):
                        slab = first + n_qk + g
                        slab_ready(slab, passed)
                        b0 = 2 * (g % 2)
                        if g == 0:
                            pe.wait_ge(qk_copied, rnd * n_qk + n_qk - 1)
                        if g == 1:
                            pe.wait_ge(qk_copied, rnd * n_qk + n_qk)
                        if g == 2:
                            pe.wait_ge(v_copied, rnd * NG + 1)
                        for i in range(TILES):
                            cols = slice(i * P, (i + 1) * P) if g == 0 else slice(i, SEQ, DIL)
                            o = ps[b0 + i // 2][:, (i % 2) * 256:(i % 2) * 256 + 256]
                            for k in range(KD):
                                hi, lo = (w[slab % 2][:, k * 256:(k + 1) * 256] for w in (w_hi, w_lo))
                                pe.matmul(o, xt_hi[:, k, cols], hi, start=(k == 0), stop=False)
                                pe.matmul(o, xt_hi[:, k, cols], lo, start=False, stop=False)
                                last = pe.matmul(o, xt_lo[:, k, cols], hi, start=False, stop=(k == KD - 1))
                        last.then_inc(w_used, 1)
                        if g == 0:
                            scores(n_qk - 1)
                        if g == 1:
                            pe.wait_ge(exp_set, (rnd + 1) * 2 * HEADS_ROUND)
                            for i in range(TILES):
                                last = pe.matmul(ps[4][:, i * 16:(i + 1) * 16], lt[:, i, :],
                                                 st_far[:, :, :, :].rearrange("p a b c -> p (a b c)"),
                                                 start=True, stop=True)
                            last.then_inc(far_turned, 1)
                    pe.wait_ge(fac_set, rnd + 1)
                    for i in range(TILES):
                        last = pe.matmul(ps[5][:, 0:2 * DIL], lm[:, i, :],
                                         fac_sel[:, i, :, :].rearrange("p a b -> p (a b)"),
                                         start=(i == 0), stop=(i == TILES - 1))
                    last.then_inc(fac_turned, 1)

                    def turn_probs(h):
                        for q in range(4):
                            if h == 0:
                                pe.wait_ge(probs_set, rnd * HEADS_ROUND + 1)
                            else:
                                pe.wait_ge(probs_set, rnd * HEADS_ROUND + 2)
                                pe.wait_ge(pt_copied, (rnd * HEADS_ROUND + h - 1) * 4 + q + 1)
                            for b in range(4 * q, min(4 * q + 4, BLOCKS)):
                                last = pe.transpose(ps[4 + q][:, (b % 4) * P:(b % 4 + 1) * P],
                                                    probs[:, h, b * P:(b + 1) * P], ident[:, :])
                            last.then_inc(pt_done, 1)

                    def values(h):
                        near, far = ps[2 * h], ps[2 * h + 1]
                        hd = slice(h * DH, (h + 1) * DH)
                        n = (rnd * HEADS_ROUND + h) * 4
                        if h == 0:
                            pe.wait_ge(v_copied, (rnd + 1) * NG)
                        for j in range(TILES):
                            w = min(2, TILES - j) * P
                            if j % 2 == 0:
                                pe.wait_ge(pt_copied, n + j // 2 + 1)
                            last = pe.matmul(near[:, j * P:j * P + w], v_att[:, 0, j, hd],
                                             probs_t[:, 2 * j * P:2 * j * P + w], start=(j == 0),
                                             stop=(j == TILES - 1), skip_group_check=True)
                        for j in range(TILES):
                            b = BLOCKS_A + 2 * j
                            pe.wait_ge(pt_copied, n + (b + 1) // 4 + 1)
                            for g in range(2):
                                last = pe.matmul(far[:, j * P:(j + 1) * P], v_att[:, 1 + g, j, hd],
                                                 probs_t[:, (b + g) * P:(b + g + 1) * P],
                                                 start=(j == 0 and g == 0), stop=(g == 1), skip_group_check=True)
                        last.then_inc(o_done, 1)

                    turn_probs(0)
                    values(0)
                    turn_probs(1)
                    values(1)
                    pe.wait_ge(o_set, (rnd + 1) * HEADS_ROUND)

            def out_rows(slab, k0, half, i, first, end):
                for k in range(4):
                    last = tokens(slab % 2, 512 * k, 512, i + 4 * half, ot_hi[:, k0 + k, :], ot_lo[:, k0 + k, :],
                                  i, first and k == 0, end and k == 3)
                return last

            pe.wait_ge(ot_set, HEADS)
            for half in range(2):
                slab_ready(S_OUT1 + half)
                for i in range(TILES):
                    last = out_rows(S_OUT1 + half, 0, half, i, True, False)
                last.then_inc(w_used, 1)
            finish_tiles(2, S_OUT1 + 2, lambda i: out_rows(S_OUT1 + 2, 4, 0, i, False, True),
                         lambda i: out_rows(S_OUT1 + 3, 4, 1, i, False, True))
            feed_forward(1, S_UP1, S_DOWN1, 3)

        @block.scalar
        def _(act):
            def split_high(slab, turns=0):
                act.wait_ge(w_loaded[slab % 2], 32 * (slab // 2 + 1) + 32 * turns)
                if slab >= 2:
                    act.wait_ge(w_used, slab - 1 + 2 * turns)
                act.activation(w_hi[slab % 2][:, :], w_stage[slab % 2][:, :], ACT.Copy).then_inc(w_hi_ready, 1)

            def x_high(e, i):
                for half in range(2):
                    act.wait_ge(xt_turned, 2 * TILES * e + 2 * i + half + 1)
                    act.activation(xt_hi[:, 4 * half:4 * half + 4, i * P:(i + 1) * P],
                                   ps[i + 4 * half][:, :].rearrange("p (c n) -> p c n", n=P), ACT.Copy
                                   ).then_inc(xt_hi_set, 1)

            def root(e, i):
                act.wait_ge(ln_var, e * TILES + i + 1)
                act.activation(std[:, i:i + 1], mean_var[:, i, 1:2], ACT.Sqrt, bias=eps[:, 0:1]).then_inc(ln_std, 1)

            def norm(e, next_slab):
                for i in range(TILES):
                    if i and e < 3:
                        x_high(e + 1, i - 1)
                    if i == TILES - 1 and e < 3:
                        split_high(next_slab)
                        split_high(next_slab + 1)
                    root(e, i)
                if e < 3:
                    x_high(e + 1, TILES - 1)

            act.wait_ge(ones_set, 2)
            for i in range(TILES):
                x_high(0, i)
                if i == 1:
                    split_high(0)
            split_high(1)
            for n, table in enumerate((sin_t, cos_t)):
                act.wait_ge(angles_set, n + 1)
                act.activation(table[:, :], rot_tmp[:, 3 - n, :], ACT.Sin).then_inc(tables_set, 1)
            for s in range(CC):
                act.wait_ge(w_used, S_IN + s + 1)
                if s >= 2:
                    act.wait_ge(a_set, s - 1)
                act.activation(sig[:, s % 2, :], ps[2 * (s % 2) + 1][:, :], ACT.Sigmoid).then_inc(sig_set, 1)
                if s == 0:
                    act.wait_ge(par_turned, 1)
                    act.activation(par[:, :], ps[4][:, 0:CC * CONV_WIDTH + 12], ACT.Copy).then_inc(par_set, 1)
                split_high(s + 2)
            split_high(6)
            for i in range(TILES):
                if i < TILES - 1:
                    act.wait_ge(v_in, i + 1)
                else:
                    act.wait_ge(w_used, S_IN + 6)
                act.activation(v_tok[:, i, :], ps[4 + i][:, :], ACT.Gelu).then_inc(v_gelu, 1)
            split_high(7)
            for i in range(TILES):
                act.wait_ge(v_var, i + 1)
                act.activation(std[:, i:i + 1], mean_var[:, i, 1:2], ACT.Sqrt, bias=eps[:, 0:1]).then_inc(v_std, 1)
            for s in range(2):
                act.wait_ge(u_in, s + 1)
                act.activation(u_t[:, 2 * s, :], ps[2 * s][:, :], ACT.Gelu).then_inc(u_set, 1)
                act.wait_ge(w_used, S_IN + 7 + s)
                act.activation(u_t[:, 2 * s + 1, :], ps[2 * s + 1][:, :], ACT.Gelu).then_inc(u_set, 1)
                split_high(8 + s)
            for c in range(CC):
                act.wait_ge(g_set, c + 1)
                act.activation(mix_hi[:, CC + c, :], mixed[:, c % 2, :], ACT.Copy).then_inc(mixhi_set, 1)
            split_high(10)
            for c in range(CC):
                act.wait_ge(xc_set, c + 1)
                act.activation(acc[:, c, :], a_pad[:, c, 0:SEQ], ACT.Square).then_inc(sq_set, 1)
            act.wait_ge(var_done, 1)
            act.activation(sig[:, 0, :], ps[7][:, :], ACT.Sqrt, bias=eps[:, 0:1]).then_inc(std_set, 1)
            gain, shift = CC * CONV_WIDTH + 4, CC * CONV_WIDTH + 8
            for c in range(CC):
                act.wait_ge(y_set, c + 1)
                if c >= 2:
                    act.wait_ge(mixlo_set, CC + c - 1)
                act.activation(mixed[:, c % 2, :], a_pad[:, c, 0:SEQ], ACT.Silu, bias=par[:, shift + c:shift + c + 1],
                               scale=par[:, gain + c:gain + c + 1]).then_inc(silu_set, 1)
                act.wait_ge(silu_set, c + 1)
                act.activation(mix_hi[:, c, :], mixed[:, c % 2, :], ACT.Copy).then_inc(mixhi_set, 1)
            split_high(11)
            norm(0, S_UP0)

            def feed_forward(layer, up, down, e):
                done = layer * KF

                def chunk(t, j):
                    n = done + 2 * t + j
                    act.wait_ge(up_done, n + 1)
                    if not (layer == 0 and isinstance(t, int) and t + j == 0):
                        act.wait_ge(ht_set, n)
                    act.activation(hidden[:, 0, :], ps[j][:, :], ACT.Silu).then_inc(gate_set, 1)
                    act.wait_ge(hid_set, n + 1)
                    act.activation(ht_hi[:, bass.ds(2 * t + j, 1), :], hidden[:, :, :], ACT.Copy).then_inc(hthi_set, 1)

                for j in range(2):
                    chunk(0, j)
                    split_high(up + 2 + j)
                with act.Fori(1, N_UP // 2) as t:
                    for j in range(2):
                        chunk(t, j)
                        split_high(up + 2 + j, t)
                with act.Fori(0, (N_DOWN - 3) // 2) as t:
                    for j in range(2):
                        split_high(down + 2 + j, t)
                split_high(down + N_DOWN - 1)
                norm(e, down + N_DOWN)

            feed_forward(0, S_UP0, S_DOWN0, 1)

            with act.Fori(0, TURNS) as turn:
                for r in range(ROUNDS_BODY):
                    rnd = turn * ROUNDS_BODY + r
                    first = S_ATT + r * ROUND_SLABS
                    passed = turn * (ROUNDS_BODY * ROUND_SLABS // 2)
                    n_qk = HEADS_ROUND * NG

                    def copy_qk(s):
                        g = s % NG
                        act.wait_ge(w_used, first + s + 1 + 2 * passed)
                        for c in range(2):
                            src = ps[2 * (s % 2) + c][:, :]
                            dst = qk[:, s % 2, c, :]
                            if g:
                                src = src.rearrange("p (m r) -> p r m", r=DIL)
                                dst = dst.rearrange("p (r m) -> p r m", r=DIL)
                            if s >= 2 and c == 0:
                                act.wait_ge(*((far_done, rnd * 2 * HEADS_ROUND + 2 * ((s - 2) // NG) + (s - 2) % NG)
                                              if (s - 2) % NG else
                                              (near_done, rnd * HEADS_ROUND + (s - 2) // NG + 1)))
                            last = act.activation(dst, src, ACT.Copy)
                        last.then_inc(qk_copied, 1)

                    def exps(h, far):
                        n = rnd * 2 * HEADS_ROUND + 2 * h + far
                        act.wait_ge(max_set, n + 1)
                        st = st_far if far else st_near
                        for i in range(TILES):
                            if far:
                                p = probs[:, h, (BLOCKS_A + 2 * i) * P:(BLOCKS_A + 2 * i + 2) * P]
                            else:
                                p = probs[:, h, max(0, 2 * i - 1) * P:(2 * i + 1) * P]
                            last = act.activation(p, p, ACT.Exp, bias=st[:, 0, h, i:i + 1], scale=SCALE,
                                                  accum_out=st[:, 1, h, i:i + 1])
                        last.then_inc(exp_set, 1)

                    for s in range(n_qk):
                        copy_qk(s)
                        split_high(first + s + 2, passed)
                        if s in (1, 4):
                            exps(s // NG, 0)
                        if s == 3:
                            exps(0, 1)
                    exps(1, 1)
                    for g in range(NG):
                        act.wait_ge(w_used, first + n_qk + g + 1 + 2 * passed)
                        for b in range(2):
                            last = act.activation(v_att[:, g, 2 * b:2 * b + 2, :],
                                                  ps[2 * (g % 2) + b][:, :].rearrange("p (t n) -> p t n", t=2), ACT.Copy)
                        last.then_inc(v_copied, 1)
                        split_high(first + n_qk + g + 2, passed)
                        if g == 1:
                            act.wait_ge(diff_set, rnd + 1)
                            act.activation(m_exp[:, :, :, :], m_diff[:, :, :, :], ACT.Exp).then_inc(diff_exp, 1)
                    for h in range(HEADS_ROUND):
                        n = (rnd * HEADS_ROUND + h) * 4
                        for q in range(0, 4, 2):
                            act.wait_ge(pt_done, n + q + 1)
                            if h or q:
                                act.wait_ge(pt_copied, n + q)
                            if h:
                                act.wait_ge(o_done, rnd * HEADS_ROUND + h)
                            act.activation(probs_t[:, q * 512:(q + 1) * 512], ps[4 + q][:, :], ACT.Copy
                                           ).then_inc(pt_copied, 1)
                        act.wait_ge(o_done, rnd * HEADS_ROUND + h + 1)
                        act.activation(o_near[:, :], ps[2 * h][:, :], ACT.Copy).then_inc(near_copied, 1)
                        act.wait_ge(o_set, rnd * HEADS_ROUND + h + 1)
                        act.activation(ot_hi[:, bass.ds(rnd * HEADS_ROUND + h, 1), :],
                                       o_sum[:, :].rearrange("p (a n) -> p a n", a=1), ACT.Copy).then_inc(othi_set, 1)
            split_high(S_OUT1 + 2)
            split_high(S_OUT1 + 3)
            norm(2, S_UP1)
            feed_forward(1, S_UP1, S_DOWN1, 3)

        @block.vector
        def _(dve):
            link = Link(dve, dve_link)

            def x_low(e, i):
                for half in range(2):
                    n = 2 * TILES * e + 2 * i + half + 1
                    dve.wait_ge(xt_hi_set, n)
                    hi = xt_hi[:, 4 * half:4 * half + 4, i * P:(i + 1) * P]
                    dve.tensor_tensor(xt_lo[:, 4 * half:4 * half + 4, i * P:(i + 1) * P],
                                      ps[i + 4 * half][:, :].rearrange("p (c n) -> p c n", n=P), hi.bitcast(F32),
                                      ALU.subtract).then_inc(xt_set, 1)

            def norm_in(e, i):
                if i < TILES - 1:
                    dve.wait_ge(acc_done, e * (TILES - 1) + i + 1)
                else:
                    dve.wait_ge(w_used, (S_UP0, S_ATT, S_UP1, N_SLABS)[e])
                for half in range(2):
                    xh = x_res[:, i, half * 512:(half + 1) * 512]
                    ins = dve.scalar_tensor_tensor(out=xh, in0=xh, scalar=ALPHA, in1=ps[i + 4 * half][:, :],
                                                   op0=ALU.mult, op1=ALU.add)
                    link.mark(ins)
                for half in range(2):
                    link.wait(link.n - 1 if half == 0 else link.n - 1)
                    link.mark(dve.bn_stats(stats[:, 6 * half:6 * half + 6], x_res[:, i, half * 512:(half + 1) * 512]))
                link.wait()
                dve.bn_aggr(mean_var[:, i, :], stats[:, :]).then_inc(ln_var, 1)

            def norm_out(e, i):
                g, b = norm_g, norm_b
                if i == 0:
                    dve.wait_ge(ln_loaded[e], 32)
                dve.wait_ge(ln_var, e * TILES + i + 1)
                for half in range(2):
                    xh, cols = x_res[:, i, half * 512:(half + 1) * 512], slice(half * 512, (half + 1) * 512)
                    link.mark(dve.scalar_tensor_tensor(out=xh, in0=xh, scalar=mean_var[:, i, 0:1], in1=g[:, cols],
                                                       op0=ALU.subtract, op1=ALU.mult))
                dve.wait_ge(ln_std, e * TILES + i + 1)
                link.mark(dve.reciprocal(rstd[:, i:i + 1], std[:, i:i + 1]))
                link.wait()
                for half in range(2):
                    xh, cols = x_res[:, i, half * 512:(half + 1) * 512], slice(half * 512, (half + 1) * 512)
                    dve.scalar_tensor_tensor(out=xh, in0=xh, scalar=rstd[:, i:i + 1], in1=b[:, cols],
                                             op0=ALU.mult, op1=ALU.add).then_inc(x_normed, 1)

            def norm(e):
                for i in range(TILES):
                    norm_in(e, i)
                    if i and e < 3:
                        x_low(e + 1, i - 1)
                    norm_out(e, i)
                if e < 3:
                    x_low(e + 1, TILES - 1)

            for i in range(TILES):
                x_low(0, i)
            dve.wait_ge(rot_loaded, 16)
            dve.wait_ge(cst_loaded, 16)
            ang, k, r_lo = rot_tmp[:, 0, :], rot_tmp[:, 1, :], rot_tmp[:, 2, :]

            def turns_of(src, scale, phase):
                link.mark(dve.tensor_scalar(k, src, scale, phase, ALU.mult, ALU.add))
                link.wait()
                link.mark(dve.tensor_scalar(k, k, ROUND_MAGIC, None, ALU.add))
                link.wait()
                link.mark(dve.tensor_scalar(k, k, -ROUND_MAGIC, None, ALU.add))
                link.wait()

            def take(dst, src, part):
                link.mark(dve.scalar_tensor_tensor(out=dst, in0=k, scalar=-part, in1=src, op0=ALU.mult, op1=ALU.add))
                link.wait()

            link.mark(dve.tensor_copy(ang, pos_i))
            link.wait()
            link.mark(dve.tensor_scalar(ang, ang, cst[0:ROT, C_FREQ:C_FREQ + 1], None, ALU.mult))
            link.wait()
            turns_of(ang, 1.0 / (BIG * TWO_PI), 0.0)
            for part in PI_A:
                take(ang, ang, BIG * part)
            link.mark(dve.tensor_scalar(r_lo, k, -BIG * PI_A4, None, ALU.mult))
            link.wait()
            turns_of(ang, 1.0 / TWO_PI, 0.0)
            for part in (PI_B1, PI_B2, PI_B3):
                take(ang, ang, part)
            link.mark(dve.tensor_tensor(ang, ang, r_lo, ALU.add))
            link.wait()
            for n, phase in enumerate((0.0, 0.25)):
                r = rot_tmp[:, 3 - n, :]
                turns_of(ang, 1.0 / TWO_PI, phase)
                take(r, ang, PI_B1)
                take(r, r, PI_B2)
                take(r, r, PI_B3)
                link.mark(dve.tensor_scalar(r, r, phase * TWO_PI, PI_SAFE, ALU.add, ALU.min))
                link.wait()
                dve.tensor_scalar(r, r, -PI_SAFE, None, ALU.max).then_inc(angles_set, 1)
            dve.wait_ge(tables_set, 2)
            link.mark(dve.tensor_scalar(sin_t[:, :], sin_t[:, :], cst[0:ROT, C_SIGN:C_SIGN + 1], None, ALU.mult))

            def gate_in(c):
                dve.wait_ge(sig_set, c + 1)
                dve.tensor_tensor(a_pad[:, c, PAD:PAD + SEQ], ps[2 * (c % 2)][:, :], sig[:, c % 2, :], ALU.mult
                                  ).then_inc(a_set, 1)

            def taps(chunks):
                for w in range(CONV_WIDTH):
                    for n, c in enumerate(chunks):
                        src = a_pad[:, c, w:w + SEQ]
                        weight = par[:, c * CONV_WIDTH + w:c * CONV_WIDTH + w + 1]
                        bias = par[:, CC * CONV_WIDTH + c:CC * CONV_WIDTH + c + 1]
                        if w == 0:
                            ins = dve.tensor_scalar(acc[:, c, :], src, weight, bias, ALU.mult, ALU.add)
                        else:
                            link.wait(link.n - len(chunks) + 1 + (n if w == CONV_WIDTH - 1 else 0))
                            ins = dve.scalar_tensor_tensor(out=acc[:, c, :], in0=src, scalar=weight, in1=acc[:, c, :],
                                                           op0=ALU.mult, op1=ALU.add)
                        if w < CONV_WIDTH - 1:
                            link.mark(ins)
                        else:
                            ins.then_inc(acc_set, 1)

            dve.wait_ge(pad_set, 1)
            gate_in(0)
            dve.wait_ge(wsp_loaded, 16)
            for half in range(2):
                dve.wait_ge(wsp_turned, half + 1)
                dve.tensor_tensor(wsp_t[:, 4 * half:4 * half + 4, :],
                                  ps[5 + half][:, :].rearrange("p (h n) -> p h n", n=P),
                                  cst[:, C_UT:C_UT + P].unsqueeze(1).broadcast_to([P, 4, P]), ALU.mult).then_inc(wsp_set, 1)
            dve.wait_ge(par_set, 1)
            gate_in(1)
            dve.wait_ge(a_set, 2)
            taps_plan = [(0, 1), (2, 3)]
            taps(taps_plan[0])
            gate_in(2)
            gate_in(3)

            dve.wait_ge(sgu_loaded, 16 * (2 + SGU_GROUPS))
            for i in range(TILES):
                dve.wait_ge(v_gelu, i + 1)
                link.mark(dve.bn_stats(stats[:, 0:6], v_tok[:, i, :]))
                link.wait()
                dve.bn_aggr(mean_var[:, i, :], stats[:, 0:6]).then_inc(v_var, 1)
                dve.wait_ge(v_var, i + 1)
                link.mark(dve.scalar_tensor_tensor(out=v_tok[:, i, :], in0=v_tok[:, i, :], scalar=mean_var[:, i, 0:1],
                                                   in1=sgu_g[:, :], op0=ALU.subtract, op1=ALU.mult))
                if i:
                    v_finish = i - 1
                    dve.wait_ge(v_std, v_finish + 1)
                    link.mark(dve.reciprocal(rstd[:, v_finish:v_finish + 1], std[:, v_finish:v_finish + 1]))
                    link.wait()
                    dve.scalar_tensor_tensor(out=v_tok[:, v_finish, :], in0=v_tok[:, v_finish, :],
                                             scalar=rstd[:, v_finish:v_finish + 1], in1=sgu_b[:, :], op0=ALU.mult,
                                             op1=ALU.add).then_inc(v_set, 1)
            dve.wait_ge(v_std, TILES)
            link.mark(dve.reciprocal(rstd[:, TILES - 1:TILES], std[:, TILES - 1:TILES]))
            link.wait()
            dve.scalar_tensor_tensor(out=v_tok[:, TILES - 1, :], in0=v_tok[:, TILES - 1, :],
                                     scalar=rstd[:, TILES - 1:TILES], in1=sgu_b[:, :], op0=ALU.mult, op1=ALU.add
                                     ).then_inc(v_set, 1)
            dve.wait_ge(a_set, 4)
            taps(taps_plan[1])

            for c in range(CC):
                dve.wait_ge(sv_done, c + 1)
                dve.wait_ge(u_set, c + 1)
                if c >= 2:
                    dve.wait_ge(mixhi_set, c - 1)
                    dve.wait_ge(mixlo_set, c - 1)
                link.mark(dve.tensor_tensor(mixed[:, c % 2, :].rearrange("p (n t) -> p n t", t=P),
                                            ps[4 + c][:, :].rearrange("p (n t) -> p n t", t=P),
                                            b_sp[:, c, :].unsqueeze(1).broadcast_to([P, TILES, P]), ALU.add))
                link.wait()
                dve.tensor_tensor(mixed[:, c % 2, :], mixed[:, c % 2, :], u_t[:, c, :], ALU.mult).then_inc(g_set, 1)
                dve.wait_ge(mixhi_set, c + 1)
                dve.tensor_tensor(mix_lo[:, CC + c, :], mixed[:, c % 2, :], mix_hi[:, CC + c, :].bitcast(F32),
                                  ALU.subtract).then_inc(mixlo_set, 1)

            dve.wait_ge(mean_done, 1)
            for c in range(CC):
                dve.tensor_tensor(a_pad[:, c, 0:SEQ], acc[:, c, :], ps[6][:, :], ALU.subtract).then_inc(xc_set, 1)
            dve.wait_ge(std_set, 1)
            link.mark(dve.reciprocal(sig[:, 0, :], sig[:, 0, :]))
            link.wait()
            dve.wait_ge(sq_set, CC)
            for c in range(CC):
                dve.tensor_tensor(a_pad[:, c, 0:SEQ], a_pad[:, c, 0:SEQ], sig[:, 0, :], ALU.mult).then_inc(y_set, 1)
            for c in range(CC):
                dve.wait_ge(mixhi_set, CC + c + 1)
                dve.tensor_tensor(mix_lo[:, c, :], mixed[:, c % 2, :], mix_hi[:, c, :].bitcast(F32), ALU.subtract
                                  ).then_inc(mixlo_set, 1)
            norm(0)

            def feed_forward(layer, e):
                done = layer * KF
                with dve.Fori(0, N_UP // 2) as t:
                    for j in range(2):
                        n = done + 2 * t + j
                        dve.wait_ge(gate_set, n + 1)
                        dve.wait_ge(w_used, (S_UP1 if layer else S_UP0) + 2 * t + j + 1)
                        dve.tensor_tensor(hidden[:, 0, :], ps[4 + j][:, :], hidden[:, 0, :], ALU.mult
                                          ).then_inc(hid_set, 1)
                        dve.wait_ge(hthi_set, n + 1)
                        dve.tensor_tensor(ht_lo[:, bass.ds(2 * t + j, 1), :], hidden[:, :, :],
                                          ht_hi[:, bass.ds(2 * t + j, 1), :].bitcast(F32), ALU.subtract
                                          ).then_inc(ht_set, 1)
                norm(e)

            feed_forward(0, 1)

            rot_links = HEADS_ROUND * NG * 3
            max_links = HEADS_ROUND * 2 * 2
            merge_links = 7
            round_links = rot_links + max_links + merge_links
            base = link.n
            with dve.Fori(0, TURNS) as turn:
                for r in range(ROUNDS_BODY):
                    rnd = turn * ROUNDS_BODY + r
                    n_qk = HEADS_ROUND * NG
                    link.n = base + rnd * round_links

                    def rotate(s):
                        g = s % NG
                        if s:
                            dve.wait_ge(qk_set, rnd * n_qk + s)
                        dve.wait_ge(qk_copied, rnd * n_qk + s + 1)
                        x3 = qk[0:ROT, s % 2, :, :]
                        cosv, sinv = cos_t[:, :], sin_t[:, :]

                        def order(a):
                            return a.rearrange("p (m r) -> p r m", r=DIL) if g else a

                        def dst(a):
                            return a.rearrange("p (r m) -> p r m", r=DIL) if g else a

                        for c in range(2):
                            ins = dve.tensor_tensor(dst(rot_a[:, c, :]), dst(qk[0:ROT, s % 2, c, :]), order(cosv), ALU.mult)
                        ins = dve.stream_shuffle(rot_b[:, :, :].rearrange("p a b -> p (a b)"),
                                                 x3.rearrange("p a b -> p (a b)"),
                                                 [(p + ROT // 2) % ROT for p in range(ROT)])
                        link.mark(ins)
                        link.wait()
                        for c in range(2):
                            ins = dve.tensor_tensor(dst(rot_b[:, c, :]), dst(rot_b[:, c, :]), order(sinv), ALU.mult)
                            link.mark(ins)
                        link.wait()
                        dve.tensor_tensor(x3, rot_a[:, :, :], rot_b[:, :, :], ALU.add).then_inc(qk_set, 1)

                    def maxima(h, far):
                        st = st_far if far else st_near
                        if far:
                            dve.wait_ge(far_done, rnd * 2 * HEADS_ROUND + 2 * (h + 1))
                            dst = probs[:, h, BLOCKS_A * P:BLOCKS * P]
                            ins = dve.tensor_tensor(dst[:, 0:512], ps[6][:, :], cst[:, C_MASKB:C_MASKB + 512], ALU.add)
                            ins = dve.tensor_tensor(dst[:, 512:1024], ps[7][:, :], cst[:, C_MASKB:C_MASKB + 512], ALU.add)
                            link.mark(ins)
                            link.wait()
                            ins = dve.tensor_reduce(st[:, 0, h, :], dst.rearrange("p (t n) -> p t n", n=2 * P), AXX, ALU.max)
                            link.mark(ins)
                        else:
                            dve.wait_ge(near_done, rnd * HEADS_ROUND + h + 1)
                            dst = probs[:, h, 0:BLOCKS_A * P]
                            dve.tensor_tensor(dst[:, 0:384], ps[4][:, P:512], cst[:, C_MASKA + P:C_MASKA + 512], ALU.add)
                            ins = dve.tensor_tensor(dst[:, 384:896], ps[5][:, :], cst[:, C_MASKA:C_MASKA + 512], ALU.add)
                            link.mark(ins)
                            link.wait()
                            dve.tensor_reduce(st[:, 0, h, 0:1], dst[:, 0:P], AXX, ALU.max)
                            ins = dve.tensor_reduce(st[:, 0, h, 1:4], dst[:, P:7 * P].rearrange("p (t n) -> p t n", n=2 * P),
                                                    AXX, ALU.max)
                            link.mark(ins)
                        link.wait()
                        dve.tensor_scalar(st[:, 0, h, :], st[:, 0, h, :], -SCALE, None, ALU.mult).then_inc(max_set, 1)

                    rotate(0)
                    rotate(1)
                    maxima(0, 0)
                    rotate(2)
                    rotate(3)
                    maxima(0, 1)
                    rotate(4)
                    maxima(1, 0)
                    rotate(5)
                    maxima(1, 1)

                    dve.wait_ge(far_turned, rnd + 1)
                    rsel = cst[:, C_R:C_R + DIL]
                    link.mark(dve.tensor_tensor(far_sel[:, :, :], ps[4][:, 0:64].rearrange("p (a r) -> p a r", r=DIL),
                                                rsel.unsqueeze(1).broadcast_to([P, 16, DIL]), ALU.mult))
                    link.wait()
                    link.mark(dve.tensor_reduce(far_nat[:, :, :, :].rearrange("p a b c -> p (a b c)"), far_sel[:, :, :],
                                                AXX, ALU.add))
                    link.wait()
                    far_m, far_d = (far_nat[:, :, kind, :].rearrange("p i h -> p h i") for kind in range(2))
                    link.mark(dve.tensor_tensor(m_low[:, :, :], st_near[:, 0, :, :], far_m, ALU.min))
                    link.wait()
                    dve.tensor_tensor(m_diff[:, 0, :, :], m_low[:, :, :], st_near[:, 0, :, :], ALU.subtract)
                    dve.tensor_tensor(m_diff[:, 1, :, :], m_low[:, :, :], far_m, ALU.subtract).then_inc(diff_set, 1)
                    dve.wait_ge(diff_exp, rnd + 1)
                    dve.tensor_tensor(m_w[:, 0, :, :], m_exp[:, 0, :, :], st_near[:, 1, :, :], ALU.mult)
                    link.mark(dve.tensor_tensor(m_w[:, 1, :, :], m_exp[:, 1, :, :], far_d, ALU.mult))
                    link.wait()
                    link.mark(dve.tensor_tensor(m_den[:, :, :], m_w[:, 0, :, :], m_w[:, 1, :, :], ALU.add))
                    link.wait()
                    link.mark(dve.reciprocal(m_den[:, :, :], m_den[:, :, :]))
                    link.wait()
                    dve.tensor_tensor(m_fac[:, 0, :, :], m_exp[:, 0, :, :], m_den[:, :, :], ALU.mult)
                    link.mark(dve.tensor_tensor(m_fac[:, 1, :, :], m_exp[:, 1, :, :], m_den[:, :, :], ALU.mult))
                    link.wait()
                    for h in range(HEADS_ROUND):
                        ins = dve.tensor_tensor(fac_sel[:, :, h, :],
                                                m_fac[:, 1, h, :].unsqueeze(2).broadcast_to([P, TILES, DIL]),
                                                rsel.unsqueeze(1).broadcast_to([P, TILES, DIL]), ALU.mult)
                    ins.then_inc(fac_set, 1)
                    dve.wait_ge(fac_turned, rnd + 1)
                    link_done = dve.tensor_copy(fac_far[:, :, :], ps[5][:, 0:2 * DIL].rearrange("p (h r) -> p h r", h=2))
                    link_done.then_inc(fac_copied, 1)
                    dve.wait_ge(fac_copied, rnd + 1)
                    for h in range(HEADS_ROUND):
                        for i in range(TILES):
                            near = probs[:, h, max(0, 2 * i - 1) * P:(2 * i + 1) * P]
                            far = probs[:, h, (BLOCKS_A + 2 * i) * P:(BLOCKS_A + 2 * i + 2) * P]
                            dve.tensor_scalar(near, near, m_fac[:, 0, h, i:i + 1], None, ALU.mult)
                            ins = dve.tensor_scalar(far, far, fac_far[:, h, i:i + 1], None, ALU.mult)
                        ins.then_inc(probs_set, 1)
                    for h in range(HEADS_ROUND):
                        n = (rnd * HEADS_ROUND + h) * 4
                        for q in range(1, 4, 2):
                            width = 512 if q < 3 else BLOCKS * P - 3 * 512
                            dve.wait_ge(pt_done, n + q + 1)
                            dve.wait_ge(pt_copied, n + q)
                            if h:
                                dve.wait_ge(o_done, rnd * HEADS_ROUND + h)
                            dve.tensor_copy(probs_t[:, q * 512:q * 512 + width], ps[4 + q][:, 0:width]
                                            ).then_inc(pt_copied, 1)
                        dve.wait_ge(near_copied, rnd * HEADS_ROUND + h + 1)
                        dve.tensor_tensor(o_sum[:, :].rearrange("p (m r) -> p m r", r=DIL),
                                          ps[2 * h + 1][:, :].rearrange("p (r m) -> p m r", r=DIL),
                                          o_near[:, :].rearrange("p (m r) -> p m r", r=DIL), ALU.add).then_inc(o_set, 1)
                        dve.wait_ge(othi_set, rnd * HEADS_ROUND + h + 1)
                        at = bass.ds(rnd * HEADS_ROUND + h, 1)
                        dve.tensor_tensor(ot_lo[:, at, :], o_sum[:, :].rearrange("p (a n) -> p a n", a=1),
                                          ot_hi[:, at, :].bitcast(F32), ALU.subtract).then_inc(ot_set, 1)
            link.n = base + TURNS * ROUNDS_BODY * round_links
            norm(2)
            feed_forward(1, 3)


_INS = ["x", "positions", "ev_w_in", "ev_conv_w", "ev_conv_b", "ev_conv_ln_g", "ev_conv_ln_b", "ev_sgu_ln_g",
        "ev_sgu_ln_b", "ev_w_spatial", "ev_b_spatial", "ev_w_out", "od_w_qkv", "od_w_out", "ffn_w_gate",
        "ffn_w_up", "ffn_w_down", "ln_g", "ln_b"]


def kernel(**inputs):
    import concourse.bacc as _bacc
    from concourse.bass_utils import run_bass_kernel_spmd as _run

    nc = _bacc.Bacc("TRN2", target_bir_lowering=False, num_devices=1)
    arrays, args = {}, []
    given = [(n, inputs[n]) for n in _INS] + [("ident", np.eye(P, dtype=np.float32)), ("const", constant_table())]
    for name, value in given:
        a = np.ascontiguousarray(value)
        arrays[f"in_{name}_dram"] = a
        args.append(nc.dram_tensor(f"in_{name}_dram", a.shape, mybir.dt.from_np(a.dtype), kind="ExternalInput").ap())
    args.append(nc.dram_tensor("out_0_dram", (1, SEQ, D_MODEL), F32, kind="ExternalOutput").ap())
    trunk(nc, *args)
    r = _run(nc, [arrays], core_ids=[0])
    return r.results[0]["out_0_dram"]
```

```python
from contextlib import ExitStack

import numpy as np

import concourse.bass as bass
from concourse import mybir

F32 = mybir.dt.float32
F32R = mybir.dt.float32r
I32 = mybir.dt.int32
ACT = mybir.ActivationFunctionType
ALU = mybir.AluOpType
AXX = mybir.AxisListType.X

P = 128
D_MODEL = 1024
SEQ = 512
TILES = SEQ // P
KD = D_MODEL // P
CONV_CH = D_MODEL // 2
CONV_WIDTH = 31
PAD = CONV_WIDTH - 1
CC = CONV_CH // P
SGU_GROUPS = 8
GROUP_CH = CONV_CH // SGU_GROUPS
HEADS = 8
DH = 128
ROT = DH // 4
ROPE_THETA = 500000.0
NG = 3
DIL = 4
FFN = 2816
KF = FFN // P
ALPHA = 4.0 ** 0.25
EPS = 1e-5
SCALE = float(DH) ** -0.5
MASKED = -3.0e38
SLAB = 1024
RING = 4

N_IN, N_OUT, N_UP, N_DOWN, N_ATT = 16, 8, 2 * KF, KF, 72
S_IN = 0
S_OUT0 = S_IN + N_IN
S_UP0 = S_OUT0 + N_OUT
S_DOWN0 = S_UP0 + N_UP
S_ATT = S_DOWN0 + N_DOWN
S_OUT1 = S_ATT + N_ATT
S_UP1 = S_OUT1 + N_OUT
S_DOWN1 = S_UP1 + N_UP
N_SLABS = S_DOWN1 + N_DOWN
HEADS_ROUND = 2
ROUND_SLABS = 2 * (HEADS_ROUND * NG + NG)
ROUNDS_BODY = 2
TURNS = HEADS // (HEADS_ROUND * ROUNDS_BODY)
BLOCKS_A = 2 * TILES - 1
BLOCKS = BLOCKS_A + 2 * TILES
C_MASKA, C_MASKB, C_L, C_LT, C_R, C_UT, C_FREQ, C_SIGN = 0, 512, 1024, 1536, 2048, 2052, 2180, 2181
N_CONST = 2182

TWO_PI = 2.0 * np.pi
BIG = 2048.0
PI_A = (6.25, 17.0 / 512.0)
PI_A += (float(np.float32(np.round((TWO_PI - sum(PI_A)) * 2.0 ** 22) / 2.0 ** 22)),)
PI_A4 = float(np.float32(TWO_PI - sum(PI_A)))
PI_B1 = float(np.round(TWO_PI * 2.0 ** 9) / 2.0 ** 9)
PI_B2 = float(np.round((TWO_PI - PI_B1) * 2.0 ** 21) / 2.0 ** 21)
PI_B3 = float(np.float32(TWO_PI - PI_B1 - PI_B2))
ROUND_MAGIC = 1.5 * 2.0 ** 23
PI_SAFE = 3.1415925


def constant_table():
    c = np.zeros((P, N_CONST), np.float32)
    row, col = np.arange(P)[:, None], np.arange(P)[None, :]
    own = np.where(row >= col, 0.0, MASKED)
    prev = np.where(col >= row, 0.0, MASKED)
    own_step4 = np.where((row >= col) & (row % 4 == col % 4), 0.0, MASKED)
    c[:, C_MASKA:C_MASKA + 512] = np.concatenate([prev, own, prev, own], 1)
    c[:, C_MASKB:C_MASKB + 512] = np.concatenate([own, own_step4, own, own_step4], 1)
    for i in range(TILES):
        c[:, C_L + i * P:C_L + (i + 1) * P] = col == 32 * i + row // DIL
        c[:, C_LT + i * P:C_LT + (i + 1) * P] = row == 32 * i + col // DIL
    c[:, C_R:C_R + DIL] = row % DIL == np.arange(DIL)[None, :]
    c[:, C_UT:C_UT + P] = col >= row
    half = ROT // 2
    freq = (ROPE_THETA ** (-np.arange(0, ROT, 2, dtype=np.float64) / ROT)).astype(np.float32)
    c[:, C_FREQ] = np.tile(freq, P // half)
    c[:, C_SIGN] = np.tile(np.concatenate([-np.ones(half), np.ones(half)]), P // ROT)
    return c


def trunk(nc, x, positions, ev_w_in, ev_conv_w, ev_conv_b, ev_conv_ln_g, ev_conv_ln_b, ev_sgu_ln_g,
          ev_sgu_ln_b, ev_w_spatial, ev_b_spatial, ev_w_out, od_w_qkv, od_w_out, ffn_w_gate, ffn_w_up,
          ffn_w_down, ln_g, ln_b, ident_in, const_in, out):
    ctx = ExitStack()
    with ctx:
        def sb(name, shape, dt=F32, scope=ctx):
            return scope.enter_context(nc.sbuf_tensor(name, shape, dt))

        def sem(name):
            return ctx.enter_context(nc.semaphore(name))

        x_res = sb("x_res", [P, TILES, D_MODEL])
        xt_hi = sb("xt_hi", [P, KD, SEQ], F32R)
        xt_lo = sb("xt_lo", [P, KD, SEQ], F32R)
        w_stage = [sb(f"w_stage{j}", [P, SLAB]) for j in range(RING)]
        w_hi = [sb(f"w_hi{j}", [P, SLAB], F32R) for j in range(RING)]
        w_lo = [sb(f"w_lo{j}", [P, SLAB], F32R) for j in range(RING)]
        ident = sb("ident", [P, P])
        ones = sb("ones", [P, P])
        cos_t = sb("cos_t", [ROT, SEQ])
        sin_t = sb("sin_t", [ROT, SEQ])
        cst = sb("cst", [P, N_CONST])
        norm_g = sb("norm_g", [P, D_MODEL])
        norm_b = sb("norm_b", [P, D_MODEL])
        stats = sb("stats", [P, 2 * 6])
        mean_var = sb("mean_var", [P, TILES, 2])
        row_sum = sb("row_sum", [P, TILES, 2])
        neg_mean = sb("neg_mean", [P, TILES])
        sq_sum = sb("sq_sum", [P, TILES])
        shift = sb("shift", [P, TILES])
        std = sb("std", [P, TILES])
        rstd = sb("rstd", [P, TILES])
        eps = sb("eps", [P, 1])
        ps = [ctx.enter_context(nc.psum_tensor(f"ps{j}", [P, 512], F32)) for j in range(8)]

        with ExitStack() as s:
            mix_hi = sb("mix_hi", [P, KD, SEQ], F32R, s)
            mix_lo = sb("mix_lo", [P, KD, SEQ], F32R, s)
            a_pad = sb("a_pad", [P, CC, PAD + SEQ], F32, s)
            acc = sb("acc", [P, CC, SEQ], F32, s)
            u_t = sb("u_t", [P, CC, SEQ], F32, s)
            v_tok = sb("v_tok", [P, TILES, CONV_CH], F32, s)
            wsp_raw = sb("wsp_raw", [P, SGU_GROUPS, P], F32, s)
            wsp_t = sb("wsp_t", [P, SGU_GROUPS, P], F32, s)
            b_sp = sb("b_sp", [P, CC, P], F32, s)
            sgu_g = sb("sgu_g", [P, CONV_CH], F32, s)
            sgu_b = sb("sgu_b", [P, CONV_CH], F32, s)
            sig = sb("sig", [P, 2, SEQ], F32, s)
            mixed = sb("mixed", [P, 2, SEQ], F32, s)
            par_rows = sb("par_rows", [P, 512 + P], F32, s)
            par = sb("par", [P, CC * CONV_WIDTH + 12], F32, s)
            rot_tmp = u_t[:, :, 0:P]
            pos_i = acc[:, 0, 0:P].bitcast(I32)
        with ExitStack() as s:
            ht_hi = sb("ht_hi", [P, KF, SEQ], F32R, s)
            ht_lo = sb("ht_lo", [P, KF, SEQ], F32R, s)
            hidden = sb("hidden", [P, 1, SEQ], F32, s)
        with ExitStack() as s:
            ot_hi = sb("ot_hi", [P, HEADS, SEQ], F32R, s)
            ot_lo = sb("ot_lo", [P, HEADS, SEQ], F32R, s)
            probs = sb("probs", [P, HEADS_ROUND, BLOCKS * P], F32, s)
            probs_t = sb("probs_t", [P, 4 * 512], F32, s)
            v_att = sb("v_att", [P, NG, TILES, HEADS_ROUND * DH], F32, s)
            qk = sb("qk", [P, 2, 2, SEQ], F32, s)
            rot_a = sb("rot_a", [ROT, 2, SEQ], F32, s)
            rot_b = sb("rot_b", [ROT, 2, SEQ], F32, s)
            o_near = sb("o_near", [P, SEQ], F32, s)
            o_sum = sb("o_sum", [P, SEQ], F32, s)
            st_near = sb("st_near", [P, 2, HEADS_ROUND, TILES], F32, s)
            st_far = sb("st_far", [P, 2, HEADS_ROUND, TILES], F32, s)
            far_sel = sb("far_sel", [P, 16, 4], F32, s)
            far_nat = sb("far_nat", [P, TILES, 2, HEADS_ROUND], F32, s)
            m_low = sb("m_low", [P, HEADS_ROUND, TILES], F32, s)
            m_diff = sb("m_diff", [P, 2, HEADS_ROUND, TILES], F32, s)
            m_exp = sb("m_exp", [P, 2, HEADS_ROUND, TILES], F32, s)
            m_w = sb("m_w", [P, 2, HEADS_ROUND, TILES], F32, s)
            m_den = sb("m_den", [P, HEADS_ROUND, TILES], F32, s)
            m_fac = sb("m_fac", [P, 2, HEADS_ROUND, TILES], F32, s)
            fac_sel = sb("fac_sel", [P, TILES, HEADS_ROUND, DIL], F32, s)
            fac_far = sb("fac_far", [P, HEADS_ROUND, DIL], F32, s)

        w_loaded = [sem(f"w_loaded{j}") for j in range(RING)]
        w_hi_ready = sem("w_hi_ready")
        w_lo_ready = sem("w_lo_ready")
        w_used = sem("w_used")
        x_loaded = [sem(f"x_loaded{i}") for i in range(TILES)]
        ident_loaded = sem("ident_loaded")
        rot_loaded = sem("rot_loaded")
        wsp_loaded = sem("wsp_loaded")
        par_loaded = sem("par_loaded")
        sgu_loaded = sem("sgu_loaded")
        ln_loaded = [sem(f"ln_loaded{e}") for e in range(4)]
        cst_loaded = sem("cst_loaded")
        out_stored = sem("out_stored")
        ones_set = sem("ones_set")
        pad_set = sem("pad_set")
        dve_link = sem("dve_link")
        act_link = sem("act_link")
        par_turned = sem("par_turned")
        par_set = sem("par_set")
        wsp_turned = sem("wsp_turned")
        wsp_set = sem("wsp_set")
        xt_turned = sem("xt_turned")
        xt_hi_set = sem("xt_hi_set")
        xt_set = sem("xt_set")
        sig_set = sem("sig_set")
        a_set = sem("a_set")
        acc_set = sem("acc_set")
        v_in = sem("v_in")
        v_gelu = sem("v_gelu")
        v_var = sem("v_var")
        v_std = sem("v_std")
        v_set = sem("v_set")
        u_in = sem("u_in")
        u_set = sem("u_set")
        sv_done = sem("sv_done")
        sv_read = sem("sv_read")
        g_set = sem("g_set")
        mixhi_set = sem("mixhi_set")
        mixlo_set = sem("mixlo_set")
        mean_done = sem("mean_done")
        xc_set = sem("xc_set")
        sq_set = sem("sq_set")
        var_done = sem("var_done")
        std_set = sem("std_set")
        y_set = sem("y_set")
        silu_set = sem("silu_set")
        acc_done = sem("acc_done")
        ln_std = sem("ln_std")
        row_summed = sem("row_summed")
        ln_sq = sem("ln_sq")
        ln_scale = sem("ln_scale")
        x_scaled = sem("x_scaled")
        x_gained = sem("x_gained")
        x_normed = sem("x_normed")
        x_normed_end = sem("x_normed_end")
        tap_product = sem("tap_product")
        tap_added = sem("tap_added")
        gate_set = sem("gate_set")
        hid_set = sem("hid_set")
        hthi_set = sem("hthi_set")
        ht_set = sem("ht_set")
        qk_copied = sem("qk_copied")
        qk_set = sem("qk_set")
        near_done = sem("near_done")
        far_done = sem("far_done")
        max_set = sem("max_set")
        exp_set = sem("exp_set")
        v_done = sem("v_done")
        v_copied = sem("v_copied")
        far_turned = sem("far_turned")
        angles_set = sem("angles_set")
        tables_set = sem("tables_set")
        diff_set = sem("diff_set")
        diff_exp = sem("diff_exp")
        fac_set = sem("fac_set")
        fac_turned = sem("fac_turned")
        fac_copied = sem("fac_copied")
        probs_set = sem("probs_set")
        pt_done = sem("pt_done")
        pt_copied = sem("pt_copied")
        o_done = sem("o_done")
        near_copied = sem("near_copied")
        o_set = sem("o_set")
        othi_set = sem("othi_set")
        ot_set = sem("ot_set")

        block = ctx.enter_context(nc.Block())

        def conv_taps(slab):
            start = 1 + 3 * (slab - 6)
            return range(max(1, start), min(CONV_WIDTH, start + 3)) if slab >= 6 else range(0)

        class Link:

            def __init__(self, eng, which):
                self.eng, self.sem, self.n = eng, which, 0

            def mark(self, ins):
                ins.then_inc(self.sem, 1)
                self.n = self.n + 1
                return self.n

            def wait(self, value=None):
                self.eng.wait_ge(self.sem, self.n if value is None else value)

        def slab_view(slab):
            def chunks(w):
                return w.rearrange("(k p) n -> p k n", p=P)

            def cols(w, c):
                return chunks(w)[:, :, c * P:(c + 1) * P]

            def square(w, k, c0):
                return chunks(w)[:, k:k + 2, c0:c0 + 512]

            def rows(w, k):
                return chunks(w)[:, k:k + 1, :]

            if slab < S_OUT0:
                s = slab - S_IN
                if s < 8:
                    return cols(ev_w_in[0], CC * (s % 2) + s // 2)
                if s < 12:
                    return square(ev_w_in[0], 2 * (s - 8), 3 * CONV_CH)
                return cols(ev_w_in[0], 2 * CC + s - 12)
            if slab < S_UP0:
                s = slab - S_OUT0
                if s < 4:
                    return square(ev_w_out[0], CC + 2 * (s % 2), 512 * (s // 2))
                return rows(ev_w_out[0], s - 4)
            if S_DOWN0 <= slab < S_ATT:
                return rows(ffn_w_down[0], slab - S_DOWN0)
            if S_OUT1 <= slab < S_UP1:
                return rows(od_w_out[0], slab - S_OUT1)
            if slab >= S_DOWN1:
                return rows(ffn_w_down[1], slab - S_DOWN1)
            raise ValueError("this slab is addressed in its loop")

        @block.sync
        def _(sp):
            def load_view(slab, turns, view):
                slot = slab % RING
                if slab >= RING:
                    sp.wait_ge(w_lo_ready, slab - RING + 1 + RING * turns)
                dst = w_stage[slot][:, :].rearrange("p (k n) -> p k n", k=view.shape[1])
                sp.dma_start(dst, view).then_inc(w_loaded[slot], 16)

            def load(slab):
                load_view(slab, 0, slab_view(slab))

            def load_ln(e, layer, which):
                if e:
                    sp.wait_ge(x_normed, 2 * (TILES - 1) * e)
                    sp.wait_ge(x_normed_end, 2 * e)
                for dst, src in ((norm_g, ln_g), (norm_b, ln_b)):
                    sp.dma_start(dst[:, :], src[layer, which:which + 1, :].partition_broadcast(P)
                                 ).then_inc(ln_loaded[e], 16)

            sp.dma_start(ident[:, :], ident_in).then_inc(ident_loaded, 16)
            for i in range(TILES):
                sp.dma_start(x_res[:, i, :], x[0, i * P:(i + 1) * P, :]).then_inc(x_loaded[i], 16)
            for slab in range(RING):
                load(slab)
            sp.dma_start(cst[:, :], const_in).then_inc(cst_loaded, 16)
            for q in range(TILES):
                sp.dma_start(pos_i[q * ROT:(q + 1) * ROT], positions[:, q * P:(q + 1) * P].partition_broadcast(ROT)
                             ).then_inc(rot_loaded, 16)
            sp.dma_start(par_rows[0:CONV_WIDTH, 0:CONV_CH], ev_conv_w[0]).then_inc(par_loaded, 16)
            for n, src in enumerate((ev_conv_b, ev_conv_ln_g, ev_conv_ln_b)):
                sp.dma_start(par_rows[4 * n:4 * n + 4, CONV_CH:CONV_CH + P],
                             src[0].rearrange("(c p) -> c p", p=P)).then_inc(par_loaded, 16)
            sp.dma_start(wsp_raw[:, :, :], ev_w_spatial[0].rearrange("h t s -> t h s")).then_inc(wsp_loaded, 16)
            sp.dma_start(sgu_g[:, :], ev_sgu_ln_g.partition_broadcast(P)).then_inc(sgu_loaded, 16)
            sp.dma_start(sgu_b[:, :], ev_sgu_ln_b.partition_broadcast(P)).then_inc(sgu_loaded, 16)
            for h in range(SGU_GROUPS):
                half = (h % 2) * GROUP_CH
                sp.dma_start(b_sp[half:half + GROUP_CH, h // 2, :],
                             ev_b_spatial[0, h:h + 1, :].partition_broadcast(GROUP_CH)).then_inc(sgu_loaded, 16)
            load_ln(0, 0, 0)
            for slab in range(RING, S_UP0):
                load(slab)

            def load_up(first, layer):
                gate_up = [w[layer].rearrange("(k p) (s n) -> p k s n", p=P, n=P) for w in (ffn_w_gate, ffn_w_up)]
                with sp.Fori(0, N_UP // RING) as t:
                    for j in range(RING):
                        load_view(first + j, t, gate_up[j % 2][:, :, 2 * t + j // 2, :])

            def load_down(first, layer, e):
                rows = ffn_w_down[layer].rearrange("(k p) n -> p k n", p=P)
                load(first)
                load(first + 1)
                load_ln(e, layer, 1)
                with sp.Fori(0, (N_DOWN - 2) // RING) as t:
                    for j in range(RING):
                        load_view(first + 2 + j, t, rows[:, bass.ds(RING * t + 2 + j, 1), :])

            load_up(S_UP0, 0)
            load_down(S_DOWN0, 0, 1)
            qkv = od_w_qkv[0].rearrange("(k p) (g r y b h d) -> p k g r y b h d", p=P, g=NG, r=3, y=TURNS,
                                        b=ROUNDS_BODY, h=HEADS_ROUND)
            values = od_w_qkv[0].rearrange("(a k p) (g r y b d) -> a p k g r y b d", a=2, p=P, g=NG, r=3, y=TURNS,
                                           b=ROUNDS_BODY)
            with sp.Fori(0, TURNS) as turn:
                passed = turn * (ROUNDS_BODY * ROUND_SLABS // RING)
                for r in range(ROUNDS_BODY):
                    slab = S_ATT + r * ROUND_SLABS
                    for h in range(HEADS_ROUND):
                        for g in range(NG):
                            for c in range(2):
                                load_view(slab, passed, qkv[:, :, g, c, turn, r, h, :])
                                slab += 1
                    for g in range(NG):
                        for a in range(2):
                            load_view(slab, passed, values[a, :, :, g, 2, turn, r, :])
                            slab += 1
            load_ln(2, 1, 0)
            for slab in range(S_OUT1, S_UP1):
                load(slab)
            load_up(S_UP1, 1)
            load_down(S_DOWN1, 1, 3)
            for i in range(TILES):
                if i < TILES - 1:
                    sp.wait_ge(x_normed, 2 * (3 * (TILES - 1) + i + 1))
                else:
                    sp.wait_ge(x_normed_end, 2 * 4)
                sp.dma_start(out[0, i * P:(i + 1) * P, :], x_res[:, i, :]).then_inc(out_stored, 16)
            sp.wait_ge(out_stored, 16 * TILES)

        @block.gpsimd
        def _(pool):
            pool.memset(ones[:, :], 1.0 / CONV_CH).then_inc(ones_set, 1)
            pool.memset(eps[:, :], EPS).then_inc(ones_set, 1)
            pool.memset(a_pad[:, :, 0:PAD], 0.0).then_inc(pad_set, 1)

            def split_low(slab, turns=0):
                pool.wait_ge(w_hi_ready, slab + 1 + RING * turns)
                pool.tensor_tensor(w_lo[slab % RING][:, :], w_stage[slab % RING][:, :],
                                   w_hi[slab % RING][:, :].bitcast(F32), ALU.subtract).then_inc(w_lo_ready, 1)

            def add_shift(e, i):
                for half in range(2):
                    xh = x_res[:, i, half * 512:(half + 1) * 512]
                    pool.wait_ge(x_gained, 2 * (e * (TILES - 1) + i) + half + 1)
                    pool.tensor_tensor(xh, xh, norm_b[:, half * 512:(half + 1) * 512], ALU.add).then_inc(x_normed, 1)

            def norm(e, following):
                if e < 3:
                    split_low(following)
                add_shift(e, 0)
                add_shift(e, 1)
                if e < 3:
                    split_low(following + 1)
                add_shift(e, 2)
                if e < 3:
                    split_low(following + 2)
                    split_low(following + 3)

            for slab in range(S_UP0):
                split_low(slab)
                for w in conv_taps(slab):
                    pool.wait_ge(tap_product, w)
                    if w > 1:
                        pool.wait_ge(tap_added, w - 1)
                    pool.tensor_tensor(acc[:, 0, :], acc[:, 0, :], mixed[:, w % 2, :], ALU.add).then_inc(tap_added, 1)
            norm(0, S_UP0)

            def feed_forward(up, down, e):
                with pool.Fori(1, N_UP // RING) as t:
                    for j in range(RING):
                        split_low(up + j, t)
                with pool.Fori(0, N_DOWN // RING) as t:
                    for j in range(RING):
                        split_low(down + j, t)
                for slab in range(down + N_DOWN // RING * RING, down + N_DOWN):
                    split_low(slab)
                norm(e, down + N_DOWN)

            feed_forward(S_UP0, S_DOWN0, 1)
            with pool.Fori(0, N_ATT // RING - 1) as t:
                for j in range(RING):
                    split_low(S_ATT + RING + j, t)
            for slab in range(S_OUT1, S_UP1):
                split_low(slab)
            norm(2, S_UP1)
            feed_forward(S_UP1, S_DOWN1, 3)

        @block.tensor
        def _(pe):
            def slab_ready(slab, turns=0):
                pe.wait_ge(w_lo_ready, slab + 1 + RING * turns)

            def columns(slab, bank, tiles=(0, TILES)):
                hi, lo = (w[slab % RING][:, :].rearrange("p (k n) -> p k n", n=P) for w in (w_hi, w_lo))
                at = slice(tiles[0] * P, tiles[1] * P)
                for k in range(KD):
                    pe.matmul(ps[bank][:, at], hi[:, k, :], xt_hi[:, k, at], start=(k == 0), stop=False)
                    pe.matmul(ps[bank][:, at], hi[:, k, :], xt_lo[:, k, at], start=False, stop=False)
                    last = pe.matmul(ps[bank][:, at], lo[:, k, :], xt_hi[:, k, at], start=False, stop=(k == KD - 1))
                return last

            def columns_behind_norm(slab, bank, e):
                pe.wait_ge(xt_set, 2 * TILES * (e + 2) - 2)
                columns(slab, bank, (0, TILES - 1))
                pe.wait_ge(xt_set, 2 * TILES * (e + 2))
                return columns(slab, bank, (TILES - 1, TILES))

            def tokens(slab, base, width, bank, t_hi, t_lo, tile, first, end):
                hi, lo = (w[slab % RING][:, base:base + width] for w in (w_hi, w_lo))
                o = ps[bank][:, 0:width]
                pe.matmul(o, t_hi[:, tile * P:(tile + 1) * P], hi, start=first, stop=False)
                pe.matmul(o, t_hi[:, tile * P:(tile + 1) * P], lo, start=False, stop=False)
                return pe.matmul(o, t_lo[:, tile * P:(tile + 1) * P], hi, start=False, stop=end)

            def turn_x(e, i):
                for half in range(2):
                    bank = ps[i + 4 * half]
                    if e and i < TILES - 1:
                        pe.wait_ge(x_normed, 2 * ((e - 1) * (TILES - 1) + i) + half + 1)
                    elif e:
                        pe.wait_ge(x_normed_end, 2 * (e - 1) + half + 1)
                    for c in range(4):
                        col = (4 * half + c) * P
                        last = pe.transpose(bank[:, c * P:(c + 1) * P], x_res[:, i, col:col + P], ident[:, :])
                    last.then_inc(xt_turned, 1)

            pe.wait_ge(ident_loaded, 16)
            for i in range(TILES):
                pe.wait_ge(x_loaded[i], 16)
                turn_x(0, i)
            def turn_parameters():
                pe.wait_ge(par_loaded, 16 * 4)
                for c in range(CC):
                    pe.transpose(ps[4][:, c * CONV_WIDTH:(c + 1) * CONV_WIDTH],
                                 par_rows[0:CONV_WIDTH, c * P:(c + 1) * P], ident[0:CONV_WIDTH, 0:CONV_WIDTH])
                pe.transpose(ps[4][:, CC * CONV_WIDTH:CC * CONV_WIDTH + 12], par_rows[0:12, CONV_CH:CONV_CH + P],
                             ident[0:12, 0:12]).then_inc(par_turned, 1)
                pe.wait_ge(wsp_loaded, 16)
                for half in range(2):
                    for h in range(4):
                        last = pe.transpose(ps[5 + half][:, h * P:(h + 1) * P], wsp_raw[:, 4 * half + h, :],
                                            ident[:, :])
                    last.then_inc(wsp_turned, 1)

            pe.wait_ge(xt_set, 2 * TILES)
            for c in range(CC):
                slab = S_IN + 2 * c
                if c >= 2:
                    pe.wait_ge(a_set, c - 1)
                for j in range(2):
                    slab_ready(slab + j)
                    columns(slab + j, 2 * (c % 2) + j).then_inc(w_used, 1)
                if c == 0:
                    turn_parameters()
            pe.wait_ge(par_set, 1)
            pe.wait_ge(wsp_set, 2)
            for s in range(4):
                slab = S_IN + 8 + s
                slab_ready(slab)
                for i in range(TILES):
                    for k in range(2):
                        last = tokens(slab, 512 * k, 512, 4 + i, xt_hi[:, 2 * s + k, :], xt_lo[:, 2 * s + k, :],
                                      i, s == 0 and k == 0, s == 3 and k == 1)
                    if s == 3 and i < TILES - 1:
                        last.then_inc(v_in, 1)
                last.then_inc(w_used, 1)
            for c in range(CC):
                slab = S_IN + 12 + c
                slab_ready(slab)
                if c % 2 == 0:
                    pe.wait_ge(a_set, 3 + c // 2)
                columns(slab, c).then_inc(w_used, 1)
            pe.wait_ge(v_set, TILES)
            for pair in range(CC):
                for n in range(TILES):
                    for h in (2 * pair, 2 * pair + 1):
                        half = (h % 2) * GROUP_CH
                        last = pe.matmul(ps[4 + pair][half:half + GROUP_CH, n * P:(n + 1) * P],
                                         v_tok[:, n, h * GROUP_CH:(h + 1) * GROUP_CH], wsp_t[:, h, :],
                                         start=True, stop=True)
                last.then_inc(sv_done, 1)

            def gating_rows(half):
                for s in range(2):
                    slab = S_OUT0 + 2 * half + s
                    slab_ready(slab)
                    for i in range(TILES):
                        for k in range(2):
                            row = CC + 2 * s + k
                            last = tokens(slab, 512 * k, 512, i + 4 * half, mix_hi[:, row, :], mix_lo[:, row, :],
                                          i, s == 0 and k == 0, False)
                    last.then_inc(w_used, 1)

            def both_halves(slab, t_hi, t_lo, row, i, first, end):
                for half in range(2):
                    last = tokens(slab, 512 * half, 512, i + 4 * half, t_hi[:, row, :], t_lo[:, row, :], i, first, end)
                return last

            def whole_rows(slab, t_hi, t_lo, row, first=False):
                slab_ready(slab)
                for i in range(TILES):
                    last = both_halves(slab, t_hi, t_lo, row, i, first, False)
                last.then_inc(w_used, 1)

            pe.wait_ge(u_set, CC)
            pe.wait_ge(mixlo_set, CC)
            gating_rows(0)
            pe.wait_ge(ones_set, 1)
            for c in range(CC):
                if c == 0:
                    pe.wait_ge(tap_added, CONV_WIDTH - 1)
                else:
                    pe.wait_ge(acc_set, c)
                last = pe.matmul(ps[6][:, :], ones[:, :], acc[:, c, :], start=(c == 0), stop=(c == CC - 1))
            last.then_inc(mean_done, 1)
            for c in range(CC):
                pe.wait_ge(sq_set, c + 1)
                last = pe.matmul(ps[7][:, :], ones[:, :], acc[:, c, :], start=(c == 0), stop=(c == CC - 1))
            last.then_inc(var_done, 1)
            pe.wait_ge(std_set, 1)
            gating_rows(1)

            def finish_tiles(e, slab, t_hi, t_lo, row):
                for j in range(3):
                    slab_ready(slab + j)
                for i in range(TILES):
                    for j in range(3):
                        last = both_halves(slab + j, t_hi, t_lo, row + j, i, False, j == 2)
                        if i == TILES - 1:
                            last.then_inc(w_used, 1)
                    if i < TILES - 1:
                        last.then_inc(acc_done, 1)
                    if i >= 2 and e < 3:
                        turn_x(e + 1, i - 2)
                if e < 3:
                    turn_x(e + 1, 2)
                    turn_x(e + 1, 3)

            for k in range(CC):
                pe.wait_ge(mixlo_set, CC + k + 1)
                if k == 0:
                    whole_rows(S_OUT0 + 4, mix_hi, mix_lo, 0)
            finish_tiles(0, S_OUT0 + 5, mix_hi, mix_lo, 1)

            def feed_forward(layer, up, down, e):
                done = layer * KF

                def chunk(slab, t, j, first):
                    slab_ready(slab, t)
                    if first:
                        last = columns_behind_norm(slab, j, e - 1)
                    else:
                        last = columns(slab, j)
                    last.then_inc(w_used, 1)
                    slab_ready(slab + 1, t)
                    columns(slab + 1, 4 + j).then_inc(w_used, 1)

                for j in range(2):
                    chunk(up + 2 * j, 0, j, j == 0)
                with pe.Fori(1, N_UP // RING) as t:
                    for j in range(2):
                        pe.wait_ge(hid_set, done + 2 * t + j - 1)
                        chunk(up + 2 * j, t, j, False)
                for k in range(KF - 3):
                    pe.wait_ge(ht_set, done + k + 1)
                    if k == 0:
                        pe.wait_ge(hid_set, done + KF)
                    whole_rows(down + k, ht_hi, ht_lo, k, k == 0)
                pe.wait_ge(ht_set, done + KF)
                finish_tiles(e, down + KF - 3, ht_hi, ht_lo, KF - 3)

            feed_forward(0, S_UP0, S_DOWN0, 1)

            pe.wait_ge(cst_loaded, 16)
            lt = cst[:, C_LT:C_LT + TILES * P].rearrange("p (i n) -> p i n", i=TILES)
            lm = cst[:, C_L:C_L + TILES * P].rearrange("p (i n) -> p i n", i=TILES)
            with pe.Fori(0, TURNS) as turn:
                for r in range(ROUNDS_BODY):
                    rnd = turn * ROUNDS_BODY + r
                    first = S_ATT + r * ROUND_SLABS
                    passed = turn * (ROUNDS_BODY * ROUND_SLABS // RING)
                    n_qk = HEADS_ROUND * NG

                    def scores(s):
                        h, g = divmod(s, NG)
                        q, key = qk[:, s % 2, 0, :], qk[:, s % 2, 1, :]
                        pe.wait_ge(qk_set, rnd * n_qk + s + 1)
                        if h == 1 and g < 2:
                            pe.wait_ge(max_set, rnd * 2 * HEADS_ROUND + g + 1)
                        for i in range(TILES):
                            lhs = q[:, i * P:(i + 1) * P]
                            if g:
                                c = (i % 2) * 2 * P + (g - 1) * P
                                last = pe.matmul(ps[6 + i // 2][:, c:c + P], lhs, key[:, i * P:(i + 1) * P],
                                                 start=True, stop=True)
                            elif i == 0:
                                last = pe.matmul(ps[4][:, P:2 * P], lhs, key[:, 0:P], start=True, stop=True)
                            else:
                                c = (i % 2) * 2 * P
                                last = pe.matmul(ps[4 + i // 2][:, c:c + 2 * P], lhs,
                                                 key[:, (i - 1) * P:(i + 1) * P], start=True, stop=True)
                        last.then_inc(far_done if g else near_done, 1)

                    for s in range(n_qk):
                        if s >= 2:
                            pe.wait_ge(qk_copied, rnd * n_qk + s - 1)
                        for c in range(2):
                            slab = first + 2 * s + c
                            slab_ready(slab, passed)
                            if r == 0 and s == 0 and c == 0:
                                last = columns_behind_norm(slab, 0, 1)
                            else:
                                last = columns(slab, 2 * (s % 2) + c)
                            last.then_inc(w_used, 1)
                        if s:
                            scores(s - 1)
                    for g in range(NG):
                        for a in range(2):
                            slab = first + 2 * n_qk + 2 * g + a
                            slab_ready(slab, passed)
                            for i in range(TILES):
                                if a == 0 and g == 0 and i % 2 == 0:
                                    pe.wait_ge(qk_copied, rnd * n_qk + n_qk - 1 + i // 2)
                                elif a == 0 and g:
                                    pe.wait_ge(v_copied, (rnd * NG + g - 1) * TILES + i + 1)
                                cols = slice(i * P, (i + 1) * P) if g == 0 else slice(i, SEQ, DIL)
                                o = ps[i][:, 0:HEADS_ROUND * DH]
                                for k in range(4):
                                    hi, lo = (w[slab % RING][:, k * 256:(k + 1) * 256] for w in (w_hi, w_lo))
                                    t_hi, t_lo = (t[:, 4 * a + k, cols] for t in (xt_hi, xt_lo))
                                    pe.matmul(o, t_hi, hi, start=(a == 0 and k == 0), stop=False)
                                    pe.matmul(o, t_hi, lo, start=False, stop=False)
                                    last = pe.matmul(o, t_lo, hi, start=False, stop=(a == 1 and k == 3))
                                if a == 1 and i < TILES - 1:
                                    last.then_inc(v_done, 1)
                            last.then_inc(w_used, 1)
                            if g == 0 and a == 0:
                                scores(n_qk - 1)
                        if g == 1:
                            pe.wait_ge(exp_set, (rnd + 1) * 2 * HEADS_ROUND)
                            for i in range(TILES):
                                last = pe.matmul(ps[4][:, i * 16:(i + 1) * 16], lt[:, i, :],
                                                 st_far[:, :, :, :].rearrange("p a b c -> p (a b c)"),
                                                 start=True, stop=True)
                            last.then_inc(far_turned, 1)
                    pe.wait_ge(fac_set, rnd + 1)
                    for i in range(TILES):
                        last = pe.matmul(ps[5][:, 0:2 * DIL], lm[:, i, :],
                                         fac_sel[:, i, :, :].rearrange("p a b -> p (a b)"),
                                         start=(i == 0), stop=(i == TILES - 1))
                    last.then_inc(fac_turned, 1)

                    def turn_probs(h):
                        for q in range(4):
                            if h == 0:
                                pe.wait_ge(probs_set, rnd * HEADS_ROUND + 1)
                            else:
                                pe.wait_ge(probs_set, rnd * HEADS_ROUND + 2)
                                pe.wait_ge(pt_copied, (rnd * HEADS_ROUND + h - 1) * 4 + q + 1)
                            for b in range(4 * q, min(4 * q + 4, BLOCKS)):
                                last = pe.transpose(ps[4 + q][:, (b % 4) * P:(b % 4 + 1) * P],
                                                    probs[:, h, b * P:(b + 1) * P], ident[:, :])
                            last.then_inc(pt_done, 1)

                    def values(h):
                        near, far = ps[2 * h], ps[2 * h + 1]
                        hd = slice(h * DH, (h + 1) * DH)
                        n = (rnd * HEADS_ROUND + h) * 4
                        if h == 0:
                            pe.wait_ge(v_copied, (rnd + 1) * NG * TILES)
                        for j in range(TILES):
                            w = min(2, TILES - j) * P
                            if j % 2 == 0:
                                pe.wait_ge(pt_copied, n + j // 2 + 1)
                            last = pe.matmul(near[:, j * P:j * P + w], v_att[:, 0, j, hd],
                                             probs_t[:, 2 * j * P:2 * j * P + w], start=(j == 0),
                                             stop=(j == TILES - 1), skip_group_check=True)
                        for j in range(TILES):
                            b = BLOCKS_A + 2 * j
                            pe.wait_ge(pt_copied, n + (b + 1) // 4 + 1)
                            for g in range(2):
                                last = pe.matmul(far[:, j * P:(j + 1) * P], v_att[:, 1 + g, j, hd],
                                                 probs_t[:, (b + g) * P:(b + g + 1) * P],
                                                 start=(j == 0 and g == 0), stop=(g == 1), skip_group_check=True)
                        last.then_inc(o_done, 1)

                    turn_probs(0)
                    values(0)
                    turn_probs(1)
                    values(1)
                    pe.wait_ge(o_set, (rnd + 1) * HEADS_ROUND)

            pe.wait_ge(ot_set, HEADS)
            for k in range(HEADS - 3):
                whole_rows(S_OUT1 + k, ot_hi, ot_lo, k, k == 0)
            finish_tiles(2, S_OUT1 + HEADS - 3, ot_hi, ot_lo, HEADS - 3)
            feed_forward(1, S_UP1, S_DOWN1, 3)

        @block.scalar
        def _(act):
            def split_high(slab, turns=0):
                act.wait_ge(w_loaded[slab % RING], 16 * (slab // RING + 1) + 16 * turns)
                if slab >= RING:
                    act.wait_ge(w_used, slab - RING + 1 + RING * turns)
                act.activation(w_hi[slab % RING][:, :], w_stage[slab % RING][:, :], ACT.Copy).then_inc(w_hi_ready, 1)

            def x_high(e, i):
                for half in range(2):
                    act.wait_ge(xt_turned, 2 * TILES * e + 2 * i + half + 1)
                    act.activation(xt_hi[:, 4 * half:4 * half + 4, i * P:(i + 1) * P],
                                   ps[i + 4 * half][:, :].rearrange("p (c n) -> p c n", n=P), ACT.Copy
                                   ).then_inc(xt_hi_set, 1)

            def norm(e, following):
                if e < 3:
                    split_high(following)
                for i in range(TILES):
                    n = e * TILES + i
                    if i == TILES - 1 and e < 3:
                        for j in range(1, RING):
                            split_high(following + j)
                    act.wait_ge(row_summed, n + 1)
                    act.activation(xt_lo[:, :, i * P:(i + 1) * P], x_res[:, i, :].rearrange("p (c n) -> p c n", n=P),
                                   ACT.Square, bias=neg_mean[:, i:i + 1], accum_out=sq_sum[:, i:i + 1]
                                   ).then_inc(ln_sq, 1)
                    act.wait_ge(ln_sq, n + 1)
                    act.activation(std[:, i:i + 1], sq_sum[:, i:i + 1], ACT.Sqrt, bias=eps[:, 0:1],
                                   scale=1.0 / D_MODEL).then_inc(ln_std, 1)
                    if i and e < 3:
                        x_high(e + 1, i - 1)
                    act.wait_ge(ln_scale, n + 1)
                    act.activation(x_res[:, i, :], x_res[:, i, :], ACT.Identity, bias=shift[:, i:i + 1],
                                   scale=rstd[:, i:i + 1]).then_inc(x_scaled, 1)
                if e < 3:
                    x_high(e + 1, TILES - 1)

            act.wait_ge(ones_set, 2)
            for i in range(TILES):
                x_high(0, i)
                if i == 1:
                    split_high(0)
            for slab in range(1, RING):
                split_high(slab)
            for n, table in enumerate((sin_t, cos_t)):
                act.wait_ge(angles_set, n + 1)
                for q in range(TILES):
                    last = act.activation(table[:, q * P:(q + 1) * P], rot_tmp[ROT * q:ROT * (q + 1), 3 - n, :], ACT.Sin)
                last.then_inc(tables_set, 1)

            def multiply_taps(slab):
                for w in conv_taps(slab):
                    if w == 1:
                        act.wait_ge(a_set, 1)
                        act.activation(acc[:, 0, :], a_pad[:, 0, 0:SEQ], ACT.Identity, scale=par[:, 0:1],
                                       bias=par[:, CC * CONV_WIDTH:CC * CONV_WIDTH + 1])
                    if w > 2:
                        act.wait_ge(tap_added, w - 2)
                    act.activation(mixed[:, w % 2, :], a_pad[:, 0, w:w + SEQ], ACT.Copy, scale=par[:, w:w + 1]
                                   ).then_inc(tap_product, 1)

            def split_and_taps(slab):
                split_high(slab)
                multiply_taps(slab)

            for c in range(CC):
                act.wait_ge(w_used, S_IN + 2 * c + 2)
                if c >= 2:
                    act.wait_ge(a_set, c - 1)
                act.activation(sig[:, c % 2, :], ps[2 * (c % 2) + 1][:, :], ACT.Sigmoid).then_inc(sig_set, 1)
                if c == 0:
                    act.wait_ge(par_turned, 1)
                    act.activation(par[:, :], ps[4][:, 0:CC * CONV_WIDTH + 12], ACT.Copy).then_inc(par_set, 1)
                    act.wait_ge(par_set, 1)
                split_and_taps(2 * c + 4)
                split_and_taps(2 * c + 5)
            split_and_taps(12)
            split_and_taps(13)
            for i in range(TILES):
                if i < TILES - 1:
                    act.wait_ge(v_in, i + 1)
                else:
                    act.wait_ge(w_used, S_IN + 12)
                act.activation(v_tok[:, i, :], ps[4 + i][:, :], ACT.Gelu).then_inc(v_gelu, 1)
            split_and_taps(14)
            split_and_taps(15)
            for i in range(TILES):
                act.wait_ge(v_var, i + 1)
                act.activation(std[:, i:i + 1], mean_var[:, i, 1:2], ACT.Sqrt, bias=eps[:, 0:1]).then_inc(v_std, 1)
            for c in range(CC):
                act.wait_ge(w_used, S_IN + 12 + c + 1)
                act.activation(u_t[:, c, :], ps[c][:, :], ACT.Gelu).then_inc(u_set, 1)
                split_high(16 + c)
            for c in range(CC):
                act.wait_ge(g_set, c + 1)
                act.activation(mix_hi[:, CC + c, :], mixed[:, c % 2, :], ACT.Copy).then_inc(mixhi_set, 1)
            split_high(20)
            split_high(21)
            for c in range(CC):
                act.wait_ge(xc_set, c + 1)
                act.activation(acc[:, c, :], a_pad[:, c, 0:SEQ], ACT.Square).then_inc(sq_set, 1)
            act.wait_ge(var_done, 1)
            act.activation(sig[:, 0, :], ps[7][:, :], ACT.Sqrt, bias=eps[:, 0:1]).then_inc(std_set, 1)
            gain, offset = CC * CONV_WIDTH + 4, CC * CONV_WIDTH + 8
            for c in range(CC):
                act.wait_ge(y_set, c + 1)
                if c >= 2:
                    act.wait_ge(mixlo_set, CC + c - 1)
                act.activation(mixed[:, c % 2, :], a_pad[:, c, 0:SEQ], ACT.Silu, scale=par[:, gain + c:gain + c + 1],
                               bias=par[:, offset + c:offset + c + 1]).then_inc(silu_set, 1)
                act.wait_ge(silu_set, c + 1)
                act.activation(mix_hi[:, c, :], mixed[:, c % 2, :], ACT.Copy).then_inc(mixhi_set, 1)
            split_high(22)
            split_high(23)
            norm(0, S_UP0)

            def feed_forward(layer, up, down, e):
                done = layer * KF

                def chunk(t, j):
                    n = done + 2 * t + j
                    act.wait_ge(w_used, up + 4 * t + 2 * j + 1)
                    if not (layer == 0 and isinstance(t, int) and t + j == 0):
                        act.wait_ge(ht_set, n)
                    act.activation(hidden[:, 0, :], ps[j][:, :], ACT.Silu).then_inc(gate_set, 1)
                    split_high(up + 4 + 2 * j, t)
                    act.wait_ge(hid_set, n + 1)
                    act.activation(ht_hi[:, bass.ds(2 * t + j, 1), :], hidden[:, :, :], ACT.Copy).then_inc(hthi_set, 1)
                    split_high(up + 5 + 2 * j, t)

                for j in range(2):
                    chunk(0, j)
                with act.Fori(1, N_UP // RING) as t:
                    for j in range(2):
                        chunk(t, j)
                with act.Fori(0, (N_DOWN - RING) // RING) as t:
                    for j in range(RING):
                        split_high(down + RING + j, t)
                for slab in range(down + N_DOWN // RING * RING, down + N_DOWN):
                    split_high(slab)
                norm(e, down + N_DOWN)

            feed_forward(0, S_UP0, S_DOWN0, 1)

            with act.Fori(0, TURNS) as turn:
                for r in range(ROUNDS_BODY):
                    rnd = turn * ROUNDS_BODY + r
                    first = S_ATT + r * ROUND_SLABS
                    passed = turn * (ROUNDS_BODY * ROUND_SLABS // RING)
                    n_qk = HEADS_ROUND * NG

                    def copy_qk(s):
                        g = s % NG
                        act.wait_ge(w_used, first + 2 * s + 2 + RING * passed)
                        for c in range(2):
                            src = ps[2 * (s % 2) + c][:, :]
                            dst = qk[:, s % 2, c, :]
                            if g:
                                src = src.rearrange("p (m r) -> p r m", r=DIL)
                                dst = dst.rearrange("p (r m) -> p r m", r=DIL)
                            if s >= 2 and c == 0:
                                act.wait_ge(*((far_done, rnd * 2 * HEADS_ROUND + 2 * ((s - 2) // NG) + (s - 2) % NG)
                                              if (s - 2) % NG else
                                              (near_done, rnd * HEADS_ROUND + (s - 2) // NG + 1)))
                            last = act.activation(dst, src, ACT.Copy)
                        last.then_inc(qk_copied, 1)

                    def exps(h, far):
                        n = rnd * 2 * HEADS_ROUND + 2 * h + far
                        act.wait_ge(max_set, n + 1)
                        st = st_far if far else st_near
                        for i in range(TILES):
                            if far:
                                p = probs[:, h, (BLOCKS_A + 2 * i) * P:(BLOCKS_A + 2 * i + 2) * P]
                            else:
                                p = probs[:, h, max(0, 2 * i - 1) * P:(2 * i + 1) * P]
                            last = act.activation(p, p, ACT.Exp, bias=st[:, 0, h, i:i + 1], scale=SCALE,
                                                  accum_out=st[:, 1, h, i:i + 1])
                        last.then_inc(exp_set, 1)

                    for s in range(n_qk):
                        copy_qk(s)
                        split_high(first + 2 * s + 4, passed)
                        split_high(first + 2 * s + 5, passed)
                        if s in (1, 4):
                            exps(s // NG, 0)
                        if s == 3:
                            exps(0, 1)
                    exps(1, 1)
                    for g in range(NG):
                        slab = first + 2 * n_qk + 2 * g
                        if g:
                            split_high(slab + 4, passed)
                        for i in range(TILES):
                            if i < TILES - 1:
                                act.wait_ge(v_done, (rnd * NG + g) * (TILES - 1) + i + 1)
                            else:
                                act.wait_ge(w_used, slab + 2 + RING * passed)
                            act.activation(v_att[:, g, i, :], ps[i][:, 0:HEADS_ROUND * DH], ACT.Copy
                                           ).then_inc(v_copied, 1)
                        if g == 0:
                            split_high(slab + 4, passed)
                        split_high(slab + 5, passed)
                        if g == 1:
                            act.wait_ge(diff_set, rnd + 1)
                            act.activation(m_exp[:, :, :, :], m_diff[:, :, :, :], ACT.Exp).then_inc(diff_exp, 1)
                    for h in range(HEADS_ROUND):
                        n = (rnd * HEADS_ROUND + h) * 4
                        for q in range(0, 4, 2):
                            act.wait_ge(pt_done, n + q + 1)
                            if h or q:
                                act.wait_ge(pt_copied, n + q)
                            if h:
                                act.wait_ge(o_done, rnd * HEADS_ROUND + h)
                            act.activation(probs_t[:, q * 512:(q + 1) * 512], ps[4 + q][:, :], ACT.Copy
                                           ).then_inc(pt_copied, 1)
                        act.wait_ge(o_done, rnd * HEADS_ROUND + h + 1)
                        act.activation(o_near[:, :], ps[2 * h][:, :], ACT.Copy).then_inc(near_copied, 1)
                        act.wait_ge(o_set, rnd * HEADS_ROUND + h + 1)
                        act.activation(ot_hi[:, bass.ds(rnd * HEADS_ROUND + h, 1), :],
                                       o_sum[:, :].rearrange("p (a n) -> p a n", a=1), ACT.Copy).then_inc(othi_set, 1)
            for slab in range(S_OUT1 + RING, S_UP1):
                split_high(slab)
            norm(2, S_UP1)
            feed_forward(1, S_UP1, S_DOWN1, 3)

        @block.vector
        def _(dve):
            link = Link(dve, dve_link)

            def x_low(e, i):
                for half in range(2):
                    n = 2 * TILES * e + 2 * i + half + 1
                    dve.wait_ge(xt_hi_set, n)
                    hi = xt_hi[:, 4 * half:4 * half + 4, i * P:(i + 1) * P]
                    dve.tensor_tensor(xt_lo[:, 4 * half:4 * half + 4, i * P:(i + 1) * P],
                                      ps[i + 4 * half][:, :].rearrange("p (c n) -> p c n", n=P), hi.bitcast(F32),
                                      ALU.subtract).then_inc(xt_set, 1)

            def norm_in(e, i):
                if i < TILES - 1:
                    dve.wait_ge(acc_done, e * (TILES - 1) + i + 1)
                else:
                    dve.wait_ge(w_used, (S_UP0, S_ATT, S_UP1, N_SLABS)[e])
                for half in range(2):
                    xh = x_res[:, i, half * 512:(half + 1) * 512]
                    link.mark(dve.scalar_tensor_tensor(out=xh, in0=xh, scalar=ALPHA, in1=ps[i + 4 * half][:, :],
                                                       op0=ALU.mult, op1=ALU.add, accum_out=row_sum[:, i, half:half + 1]))
                link.wait()
                dve.tensor_scalar(neg_mean[:, i:i + 1], row_sum[:, i, 0:1], row_sum[:, i, 1:2], -1.0 / D_MODEL,
                                  ALU.add, ALU.mult).then_inc(row_summed, 1)

            def norm_scale(e, i):
                dve.wait_ge(ln_std, e * TILES + i + 1)
                link.mark(dve.reciprocal(rstd[:, i:i + 1], std[:, i:i + 1]))
                link.wait()
                dve.tensor_tensor(shift[:, i:i + 1], neg_mean[:, i:i + 1], rstd[:, i:i + 1], ALU.mult
                                  ).then_inc(ln_scale, 1)

            def norm_gain(e, i):
                if i == 0:
                    dve.wait_ge(ln_loaded[e], 32)
                dve.wait_ge(x_scaled, e * TILES + i + 1)
                for half in range(2):
                    xh, cols = x_res[:, i, half * 512:(half + 1) * 512], slice(half * 512, (half + 1) * 512)
                    ins = dve.tensor_tensor(xh, xh, norm_g[:, cols], ALU.mult)
                    if i < TILES - 1:
                        ins.then_inc(x_gained, 1)
                    else:
                        link.mark(ins)
                        link.wait()
                        dve.tensor_tensor(xh, xh, norm_b[:, cols], ALU.add).then_inc(x_normed_end, 1)

            def norm(e):
                for i in range(TILES):
                    norm_in(e, i)
                    if i:
                        norm_gain(e, i - 1)
                    norm_scale(e, i)
                    if i and e < 3:
                        x_low(e + 1, i - 1)
                norm_gain(e, TILES - 1)
                if e < 3:
                    x_low(e + 1, TILES - 1)

            for i in range(TILES):
                x_low(0, i)
            dve.wait_ge(rot_loaded, 16 * TILES)
            dve.wait_ge(cst_loaded, 16)
            ang, k, r_lo = rot_tmp[:, 0, :], rot_tmp[:, 1, :], rot_tmp[:, 2, :]

            def turns_of(src, scale, phase):
                link.mark(dve.tensor_scalar(k, src, scale, phase, ALU.mult, ALU.add))
                link.wait()
                link.mark(dve.tensor_scalar(k, k, ROUND_MAGIC, None, ALU.add))
                link.wait()
                link.mark(dve.tensor_scalar(k, k, -ROUND_MAGIC, None, ALU.add))
                link.wait()

            def take(dst, src, part):
                link.mark(dve.scalar_tensor_tensor(out=dst, in0=k, scalar=-part, in1=src, op0=ALU.mult, op1=ALU.add))
                link.wait()

            link.mark(dve.tensor_copy(ang, pos_i))
            link.wait()
            link.mark(dve.tensor_scalar(ang, ang, cst[:, C_FREQ:C_FREQ + 1], None, ALU.mult))
            link.wait()
            turns_of(ang, 1.0 / (BIG * TWO_PI), 0.0)
            for part in PI_A:
                take(ang, ang, BIG * part)
            link.mark(dve.tensor_scalar(r_lo, k, -BIG * PI_A4, None, ALU.mult))
            link.wait()
            turns_of(ang, 1.0 / TWO_PI, 0.0)
            for part in (PI_B1, PI_B2, PI_B3):
                take(ang, ang, part)
            link.mark(dve.tensor_tensor(ang, ang, r_lo, ALU.add))
            link.wait()
            for n, phase in enumerate((0.0, 0.25)):
                r = rot_tmp[:, 3 - n, :]
                turns_of(ang, 1.0 / TWO_PI, phase)
                take(r, ang, PI_B1)
                take(r, r, PI_B2)
                take(r, r, PI_B3)
                link.mark(dve.tensor_scalar(r, r, phase * TWO_PI, PI_SAFE, ALU.add, ALU.min))
                link.wait()
                dve.tensor_scalar(r, r, -PI_SAFE, None, ALU.max).then_inc(angles_set, 1)
            dve.wait_ge(tables_set, 2)
            link.mark(dve.tensor_scalar(sin_t[:, :], sin_t[:, :], cst[0:ROT, C_SIGN:C_SIGN + 1], None, ALU.mult))

            def gate_in(c):
                dve.wait_ge(sig_set, c + 1)
                dve.tensor_tensor(a_pad[:, c, PAD:PAD + SEQ], ps[2 * (c % 2)][:, :], sig[:, c % 2, :], ALU.mult
                                  ).then_inc(a_set, 1)

            self_tap = {}

            def taps(chunks, start=0, end=CONV_WIDTH):
                for w in range(start, end):
                    for n, c in enumerate(chunks):
                        src = a_pad[:, c, w:w + SEQ]
                        weight = par[:, c * CONV_WIDTH + w:c * CONV_WIDTH + w + 1]
                        bias = par[:, CC * CONV_WIDTH + c:CC * CONV_WIDTH + c + 1]
                        if w == 0:
                            ins = dve.tensor_scalar(acc[:, c, :], src, weight, bias, ALU.mult, ALU.add)
                        else:
                            link.wait(self_tap[c])
                            ins = dve.scalar_tensor_tensor(out=acc[:, c, :], in0=src, scalar=weight, in1=acc[:, c, :],
                                                           op0=ALU.mult, op1=ALU.add)
                        if w < CONV_WIDTH - 1:
                            self_tap[c] = link.mark(ins)
                        else:
                            ins.then_inc(acc_set, 1)

            dve.wait_ge(pad_set, 1)
            gate_in(0)
            dve.wait_ge(wsp_loaded, 16)
            for half in range(2):
                dve.wait_ge(wsp_turned, half + 1)
                dve.tensor_tensor(wsp_t[:, 4 * half:4 * half + 4, :],
                                  ps[5 + half][:, :].rearrange("p (h n) -> p h n", n=P),
                                  cst[:, C_UT:C_UT + P].unsqueeze(1).broadcast_to([P, 4, P]), ALU.mult).then_inc(wsp_set, 1)
            gate_in(1)
            dve.wait_ge(a_set, 2)
            dve.wait_ge(par_set, 1)
            taps((1,))
            gate_in(2)
            gate_in(3)
            dve.wait_ge(a_set, 4)
            taps((2, 3), 0, 12)
            dve.wait_ge(sgu_loaded, 16 * (2 + SGU_GROUPS))
            for i in range(TILES):
                dve.wait_ge(v_gelu, i + 1)
                link.mark(dve.bn_stats(stats[:, 0:6], v_tok[:, i, :]))
                link.wait()
                dve.bn_aggr(mean_var[:, i, :], stats[:, 0:6]).then_inc(v_var, 1)
                dve.wait_ge(v_var, i + 1)
                link.mark(dve.scalar_tensor_tensor(out=v_tok[:, i, :], in0=v_tok[:, i, :], scalar=mean_var[:, i, 0:1],
                                                   in1=sgu_g[:, :], op0=ALU.subtract, op1=ALU.mult))
                if i:
                    v_finish = i - 1
                    dve.wait_ge(v_std, v_finish + 1)
                    link.mark(dve.reciprocal(rstd[:, v_finish:v_finish + 1], std[:, v_finish:v_finish + 1]))
                    link.wait()
                    dve.scalar_tensor_tensor(out=v_tok[:, v_finish, :], in0=v_tok[:, v_finish, :],
                                             scalar=rstd[:, v_finish:v_finish + 1], in1=sgu_b[:, :], op0=ALU.mult,
                                             op1=ALU.add).then_inc(v_set, 1)
            dve.wait_ge(v_std, TILES)
            link.mark(dve.reciprocal(rstd[:, TILES - 1:TILES], std[:, TILES - 1:TILES]))
            link.wait()
            dve.scalar_tensor_tensor(out=v_tok[:, TILES - 1, :], in0=v_tok[:, TILES - 1, :],
                                     scalar=rstd[:, TILES - 1:TILES], in1=sgu_b[:, :], op0=ALU.mult, op1=ALU.add
                                     ).then_inc(v_set, 1)
            taps((2, 3), 12, CONV_WIDTH)
            dve.wait_ge(tap_added, CONV_WIDTH - 1)

            for c in range(CC):
                dve.wait_ge(sv_done, c + 1)
                dve.wait_ge(u_set, c + 1)
                if c >= 2:
                    dve.wait_ge(mixhi_set, c - 1)
                    dve.wait_ge(mixlo_set, c - 1)
                link.mark(dve.tensor_tensor(mixed[:, c % 2, :].rearrange("p (n t) -> p n t", t=P),
                                            ps[4 + c][:, :].rearrange("p (n t) -> p n t", t=P),
                                            b_sp[:, c, :].unsqueeze(1).broadcast_to([P, TILES, P]), ALU.add))
                link.wait()
                dve.tensor_tensor(mixed[:, c % 2, :], mixed[:, c % 2, :], u_t[:, c, :], ALU.mult).then_inc(g_set, 1)
                dve.wait_ge(mixhi_set, c + 1)
                dve.tensor_tensor(mix_lo[:, CC + c, :], mixed[:, c % 2, :], mix_hi[:, CC + c, :].bitcast(F32),
                                  ALU.subtract).then_inc(mixlo_set, 1)

            dve.wait_ge(mean_done, 1)
            for c in range(CC):
                dve.tensor_tensor(a_pad[:, c, 0:SEQ], acc[:, c, :], ps[6][:, :], ALU.subtract).then_inc(xc_set, 1)
            dve.wait_ge(std_set, 1)
            link.mark(dve.reciprocal(sig[:, 0, :], sig[:, 0, :]))
            link.wait()
            dve.wait_ge(sq_set, CC)
            for c in range(CC):
                dve.tensor_tensor(a_pad[:, c, 0:SEQ], a_pad[:, c, 0:SEQ], sig[:, 0, :], ALU.mult).then_inc(y_set, 1)
            for c in range(CC):
                dve.wait_ge(mixhi_set, CC + c + 1)
                dve.tensor_tensor(mix_lo[:, c, :], mixed[:, c % 2, :], mix_hi[:, c, :].bitcast(F32), ALU.subtract
                                  ).then_inc(mixlo_set, 1)
            norm(0)

            def feed_forward(layer, e):
                done = layer * KF
                with dve.Fori(0, N_UP // RING) as t:
                    for j in range(2):
                        n = done + 2 * t + j
                        dve.wait_ge(gate_set, n + 1)
                        dve.wait_ge(w_used, (S_UP1 if layer else S_UP0) + 4 * t + 2 * j + 2)
                        dve.tensor_tensor(hidden[:, 0, :], ps[4 + j][:, :], hidden[:, 0, :], ALU.mult
                                          ).then_inc(hid_set, 1)
                        dve.wait_ge(hthi_set, n + 1)
                        dve.tensor_tensor(ht_lo[:, bass.ds(2 * t + j, 1), :], hidden[:, :, :],
                                          ht_hi[:, bass.ds(2 * t + j, 1), :].bitcast(F32), ALU.subtract
                                          ).then_inc(ht_set, 1)
                norm(e)

            feed_forward(0, 1)

            rot_links = HEADS_ROUND * NG * 3
            max_links = HEADS_ROUND * 2 * 2
            merge_links = 7
            round_links = rot_links + max_links + merge_links
            base = link.n
            with dve.Fori(0, TURNS) as turn:
                for r in range(ROUNDS_BODY):
                    rnd = turn * ROUNDS_BODY + r
                    n_qk = HEADS_ROUND * NG
                    link.n = base + rnd * round_links

                    def rotate(s):
                        g = s % NG
                        if s:
                            dve.wait_ge(qk_set, rnd * n_qk + s)
                        dve.wait_ge(qk_copied, rnd * n_qk + s + 1)
                        x3 = qk[0:ROT, s % 2, :, :]
                        cosv, sinv = cos_t[:, :], sin_t[:, :]

                        def order(a):
                            return a.rearrange("p (m r) -> p r m", r=DIL) if g else a

                        def dst(a):
                            return a.rearrange("p (r m) -> p r m", r=DIL) if g else a

                        for c in range(2):
                            ins = dve.tensor_tensor(dst(rot_a[:, c, :]), dst(qk[0:ROT, s % 2, c, :]), order(cosv), ALU.mult)
                        ins = dve.stream_shuffle(rot_b[:, :, :].rearrange("p a b -> p (a b)"),
                                                 x3.rearrange("p a b -> p (a b)"),
                                                 [(p + ROT // 2) % ROT for p in range(ROT)])
                        link.mark(ins)
                        link.wait()
                        for c in range(2):
                            ins = dve.tensor_tensor(dst(rot_b[:, c, :]), dst(rot_b[:, c, :]), order(sinv), ALU.mult)
                            link.mark(ins)
                        link.wait()
                        dve.tensor_tensor(x3, rot_a[:, :, :], rot_b[:, :, :], ALU.add).then_inc(qk_set, 1)

                    def maxima(h, far):
                        st = st_far if far else st_near
                        if far:
                            dve.wait_ge(far_done, rnd * 2 * HEADS_ROUND + 2 * (h + 1))
                            dst = probs[:, h, BLOCKS_A * P:BLOCKS * P]
                            ins = dve.tensor_tensor(dst[:, 0:512], ps[6][:, :], cst[:, C_MASKB:C_MASKB + 512], ALU.add)
                            ins = dve.tensor_tensor(dst[:, 512:1024], ps[7][:, :], cst[:, C_MASKB:C_MASKB + 512], ALU.add)
                            link.mark(ins)
                            link.wait()
                            ins = dve.tensor_reduce(st[:, 0, h, :], dst.rearrange("p (t n) -> p t n", n=2 * P), AXX, ALU.max)
                            link.mark(ins)
                        else:
                            dve.wait_ge(near_done, rnd * HEADS_ROUND + h + 1)
                            dst = probs[:, h, 0:BLOCKS_A * P]
                            dve.tensor_tensor(dst[:, 0:384], ps[4][:, P:512], cst[:, C_MASKA + P:C_MASKA + 512], ALU.add)
                            ins = dve.tensor_tensor(dst[:, 384:896], ps[5][:, :], cst[:, C_MASKA:C_MASKA + 512], ALU.add)
                            link.mark(ins)
                            link.wait()
                            dve.tensor_reduce(st[:, 0, h, 0:1], dst[:, 0:P], AXX, ALU.max)
                            ins = dve.tensor_reduce(st[:, 0, h, 1:4], dst[:, P:7 * P].rearrange("p (t n) -> p t n", n=2 * P),
                                                    AXX, ALU.max)
                            link.mark(ins)
                        link.wait()
                        dve.tensor_scalar(st[:, 0, h, :], st[:, 0, h, :], -SCALE, None, ALU.mult).then_inc(max_set, 1)

                    rotate(0)
                    rotate(1)
                    maxima(0, 0)
                    rotate(2)
                    rotate(3)
                    maxima(0, 1)
                    rotate(4)
                    maxima(1, 0)
                    rotate(5)
                    maxima(1, 1)

                    dve.wait_ge(far_turned, rnd + 1)
                    rsel = cst[:, C_R:C_R + DIL]
                    link.mark(dve.tensor_tensor(far_sel[:, :, :], ps[4][:, 0:64].rearrange("p (a r) -> p a r", r=DIL),
                                                rsel.unsqueeze(1).broadcast_to([P, 16, DIL]), ALU.mult))
                    link.wait()
                    link.mark(dve.tensor_reduce(far_nat[:, :, :, :].rearrange("p a b c -> p (a b c)"), far_sel[:, :, :],
                                                AXX, ALU.add))
                    link.wait()
                    far_m, far_d = (far_nat[:, :, kind, :].rearrange("p i h -> p h i") for kind in range(2))
                    link.mark(dve.tensor_tensor(m_low[:, :, :], st_near[:, 0, :, :], far_m, ALU.min))
                    link.wait()
                    dve.tensor_tensor(m_diff[:, 0, :, :], m_low[:, :, :], st_near[:, 0, :, :], ALU.subtract)
                    dve.tensor_tensor(m_diff[:, 1, :, :], m_low[:, :, :], far_m, ALU.subtract).then_inc(diff_set, 1)
                    dve.wait_ge(diff_exp, rnd + 1)
                    dve.tensor_tensor(m_w[:, 0, :, :], m_exp[:, 0, :, :], st_near[:, 1, :, :], ALU.mult)
                    link.mark(dve.tensor_tensor(m_w[:, 1, :, :], m_exp[:, 1, :, :], far_d, ALU.mult))
                    link.wait()
                    link.mark(dve.tensor_tensor(m_den[:, :, :], m_w[:, 0, :, :], m_w[:, 1, :, :], ALU.add))
                    link.wait()
                    link.mark(dve.reciprocal(m_den[:, :, :], m_den[:, :, :]))
                    link.wait()
                    dve.tensor_tensor(m_fac[:, 0, :, :], m_exp[:, 0, :, :], m_den[:, :, :], ALU.mult)
                    link.mark(dve.tensor_tensor(m_fac[:, 1, :, :], m_exp[:, 1, :, :], m_den[:, :, :], ALU.mult))
                    link.wait()
                    for h in range(HEADS_ROUND):
                        ins = dve.tensor_tensor(fac_sel[:, :, h, :],
                                                m_fac[:, 1, h, :].unsqueeze(2).broadcast_to([P, TILES, DIL]),
                                                rsel.unsqueeze(1).broadcast_to([P, TILES, DIL]), ALU.mult)
                    ins.then_inc(fac_set, 1)
                    dve.wait_ge(fac_turned, rnd + 1)
                    link_done = dve.tensor_copy(fac_far[:, :, :], ps[5][:, 0:2 * DIL].rearrange("p (h r) -> p h r", h=2))
                    link_done.then_inc(fac_copied, 1)
                    dve.wait_ge(fac_copied, rnd + 1)
                    for h in range(HEADS_ROUND):
                        for i in range(TILES):
                            near = probs[:, h, max(0, 2 * i - 1) * P:(2 * i + 1) * P]
                            far = probs[:, h, (BLOCKS_A + 2 * i) * P:(BLOCKS_A + 2 * i + 2) * P]
                            dve.tensor_scalar(near, near, m_fac[:, 0, h, i:i + 1], None, ALU.mult)
                            ins = dve.tensor_scalar(far, far, fac_far[:, h, i:i + 1], None, ALU.mult)
                        ins.then_inc(probs_set, 1)
                    for h in range(HEADS_ROUND):
                        n = (rnd * HEADS_ROUND + h) * 4
                        for q in range(1, 4, 2):
                            width = 512 if q < 3 else BLOCKS * P - 3 * 512
                            dve.wait_ge(pt_done, n + q + 1)
                            dve.wait_ge(pt_copied, n + q)
                            if h:
                                dve.wait_ge(o_done, rnd * HEADS_ROUND + h)
                            dve.tensor_copy(probs_t[:, q * 512:q * 512 + width], ps[4 + q][:, 0:width]
                                            ).then_inc(pt_copied, 1)
                        dve.wait_ge(near_copied, rnd * HEADS_ROUND + h + 1)
                        dve.tensor_tensor(o_sum[:, :].rearrange("p (m r) -> p m r", r=DIL),
                                          ps[2 * h + 1][:, :].rearrange("p (r m) -> p m r", r=DIL),
                                          o_near[:, :].rearrange("p (m r) -> p m r", r=DIL), ALU.add).then_inc(o_set, 1)
                        dve.wait_ge(othi_set, rnd * HEADS_ROUND + h + 1)
                        at = bass.ds(rnd * HEADS_ROUND + h, 1)
                        dve.tensor_tensor(ot_lo[:, at, :], o_sum[:, :].rearrange("p (a n) -> p a n", a=1),
                                          ot_hi[:, at, :].bitcast(F32), ALU.subtract).then_inc(ot_set, 1)
            link.n = base + TURNS * ROUNDS_BODY * round_links
            norm(2)
            feed_forward(1, 3)


_INS = ["x", "positions", "ev_w_in", "ev_conv_w", "ev_conv_b", "ev_conv_ln_g", "ev_conv_ln_b", "ev_sgu_ln_g",
        "ev_sgu_ln_b", "ev_w_spatial", "ev_b_spatial", "ev_w_out", "od_w_qkv", "od_w_out", "ffn_w_gate",
        "ffn_w_up", "ffn_w_down", "ln_g", "ln_b"]


def kernel(**inputs):
    import concourse.bacc as _bacc
    from concourse.bass_utils import run_bass_kernel_spmd as _run

    nc = _bacc.Bacc("TRN2", target_bir_lowering=False, num_devices=1)
    arrays, args = {}, []
    given = [(n, inputs[n]) for n in _INS] + [("ident", np.eye(P, dtype=np.float32)), ("const", constant_table())]
    for name, value in given:
        a = np.ascontiguousarray(value)
        arrays[f"in_{name}_dram"] = a
        args.append(nc.dram_tensor(f"in_{name}_dram", a.shape, mybir.dt.from_np(a.dtype), kind="ExternalInput").ap())
    args.append(nc.dram_tensor("out_0_dram", (1, SEQ, D_MODEL), F32, kind="ExternalOutput").ap())
    trunk(nc, *args)
    r = _run(nc, [arrays], core_ids=[0])
    return r.results[0]["out_0_dram"]
```

```python
from contextlib import ExitStack

import numpy as np

import concourse.bass as bass
from concourse import mybir

F32 = mybir.dt.float32
F32R = mybir.dt.float32r
I32 = mybir.dt.int32
ACT = mybir.ActivationFunctionType
ALU = mybir.AluOpType
AXX = mybir.AxisListType.X

P = 128
D_MODEL = 1024
SEQ = 512
TILES = SEQ // P
KD = D_MODEL // P
CONV_CH = D_MODEL // 2
CONV_WIDTH = 31
PAD = CONV_WIDTH - 1
CC = CONV_CH // P
SGU_GROUPS = 8
GROUP_CH = CONV_CH // SGU_GROUPS
HEADS = 8
DH = 128
ROT = DH // 4
ROPE_THETA = 500000.0
NG = 3
DIL = 4
FFN = 2816
KF = FFN // P
ALPHA = 4.0 ** 0.25
EPS = 1e-5
SCALE = float(DH) ** -0.5
MASKED = -3.0e38
SHIFT_TILES = TILES - 1
SLAB = 1024
RING = 4

N_IN, N_OUT, N_UP, N_DOWN, N_ATT = 16, 8, 2 * KF, KF, 72
S_IN = 0
S_OUT0 = S_IN + N_IN
S_UP0 = S_OUT0 + N_OUT
S_DOWN0 = S_UP0 + N_UP
S_ATT = S_DOWN0 + N_DOWN
S_OUT1 = S_ATT + N_ATT
S_UP1 = S_OUT1 + N_OUT
S_DOWN1 = S_UP1 + N_UP
N_SLABS = S_DOWN1 + N_DOWN
HEADS_ROUND = 2
ROUND_SLABS = 2 * (HEADS_ROUND * NG + NG)
ROUNDS_BODY = 2
TURNS = HEADS // (HEADS_ROUND * ROUNDS_BODY)
BLOCKS_A = 2 * TILES - 1
BLOCKS = BLOCKS_A + 2 * TILES
C_MASKA, C_MASKB, C_L, C_LT, C_R, C_UT, C_FREQ, C_SIGN = 0, 512, 1024, 1536, 2048, 2052, 2180, 2181
N_CONST = 2182

TWO_PI = 2.0 * np.pi
BIG = 2048.0
PI_A = (6.25, 17.0 / 512.0)
PI_A += (float(np.float32(np.round((TWO_PI - sum(PI_A)) * 2.0 ** 22) / 2.0 ** 22)),)
PI_A4 = float(np.float32(TWO_PI - sum(PI_A)))
PI_B1 = float(np.round(TWO_PI * 2.0 ** 9) / 2.0 ** 9)
PI_B2 = float(np.round((TWO_PI - PI_B1) * 2.0 ** 21) / 2.0 ** 21)
PI_B3 = float(np.float32(TWO_PI - PI_B1 - PI_B2))
ROUND_MAGIC = 1.5 * 2.0 ** 23
PI_SAFE = 3.1415925


def constant_table():
    c = np.zeros((P, N_CONST), np.float32)
    row, col = np.arange(P)[:, None], np.arange(P)[None, :]
    own = np.where(row >= col, 0.0, MASKED)
    prev = np.where(col >= row, 0.0, MASKED)
    own_step4 = np.where((row >= col) & (row % 4 == col % 4), 0.0, MASKED)
    c[:, C_MASKA:C_MASKA + 512] = np.concatenate([prev, own, prev, own], 1)
    c[:, C_MASKB:C_MASKB + 512] = np.concatenate([own, own_step4, own, own_step4], 1)
    for i in range(TILES):
        c[:, C_L + i * P:C_L + (i + 1) * P] = col == 32 * i + row // DIL
        c[:, C_LT + i * P:C_LT + (i + 1) * P] = row == 32 * i + col // DIL
    c[:, C_R:C_R + DIL] = row % DIL == np.arange(DIL)[None, :]
    c[:, C_UT:C_UT + P] = col >= row
    half = ROT // 2
    freq = (ROPE_THETA ** (-np.arange(0, ROT, 2, dtype=np.float64) / ROT)).astype(np.float32)
    c[:, C_FREQ] = np.tile(freq, P // half)
    c[:, C_SIGN] = np.tile(np.concatenate([-np.ones(half), np.ones(half)]), P // ROT)
    return c


def trunk(nc, x, positions, ev_w_in, ev_conv_w, ev_conv_b, ev_conv_ln_g, ev_conv_ln_b, ev_sgu_ln_g,
          ev_sgu_ln_b, ev_w_spatial, ev_b_spatial, ev_w_out, od_w_qkv, od_w_out, ffn_w_gate, ffn_w_up,
          ffn_w_down, ln_g, ln_b, ident_in, const_in, out):
    ctx = ExitStack()
    with ctx:
        def sb(name, shape, dt=F32, scope=ctx):
            return scope.enter_context(nc.sbuf_tensor(name, shape, dt))

        def sem(name):
            return ctx.enter_context(nc.semaphore(name))

        x_res = sb("x_res", [P, TILES, D_MODEL])
        xt_hi = sb("xt_hi", [P, KD, SEQ], F32R)
        xt_lo = sb("xt_lo", [P, KD, SEQ], F32R)
        w_stage = [sb(f"w_stage{j}", [P, SLAB]) for j in range(RING)]
        w_hi = [sb(f"w_hi{j}", [P, SLAB], F32R) for j in range(RING)]
        w_lo = [sb(f"w_lo{j}", [P, SLAB], F32R) for j in range(RING)]
        ident = sb("ident", [P, P])
        ones = sb("ones", [P, P])
        cos_t = sb("cos_t", [ROT, SEQ])
        sin_t = sb("sin_t", [ROT, SEQ])
        cst = sb("cst", [P, N_CONST])
        norm_g = sb("norm_g", [P, D_MODEL])
        norm_b = sb("norm_b", [P, D_MODEL])
        stats = sb("stats", [P, 2 * 6])
        mean_var = sb("mean_var", [P, TILES, 2])
        row_sum = sb("row_sum", [P, TILES, 2])
        neg_mean = sb("neg_mean", [P, TILES])
        sq_sum = sb("sq_sum", [P, TILES])
        shift = sb("shift", [P, TILES])
        std = sb("std", [P, TILES])
        rstd = sb("rstd", [P, TILES])
        eps = sb("eps", [P, 1])
        ps = [ctx.enter_context(nc.psum_tensor(f"ps{j}", [P, 512], F32)) for j in range(8)]

        with ExitStack() as s:
            mix_hi = sb("mix_hi", [P, KD, SEQ], F32R, s)
            mix_lo = sb("mix_lo", [P, KD, SEQ], F32R, s)
            a_pad = sb("a_pad", [P, CC, PAD + SEQ], F32, s)
            acc = sb("acc", [P, CC, SEQ], F32, s)
            u_t = sb("u_t", [P, CC, SEQ], F32, s)
            v_tok = sb("v_tok", [P, TILES, CONV_CH], F32, s)
            wsp_raw = sb("wsp_raw", [P, SGU_GROUPS, P], F32, s)
            wsp_t = sb("wsp_t", [P, SGU_GROUPS, P], F32, s)
            b_sp = sb("b_sp", [P, CC, P], F32, s)
            sgu_g = sb("sgu_g", [P, CONV_CH], F32, s)
            sgu_b = sb("sgu_b", [P, CONV_CH], F32, s)
            sig = sb("sig", [P, 2, SEQ], F32, s)
            mixed = sb("mixed", [P, 2, SEQ], F32, s)
            par_rows = sb("par_rows", [P, 512 + P], F32, s)
            par = sb("par", [P, CC * CONV_WIDTH + 12], F32, s)
        with ExitStack() as s:
            ht_hi = sb("ht_hi", [P, KF, SEQ], F32R, s)
            ht_lo = sb("ht_lo", [P, KF, SEQ], F32R, s)
            hidden = sb("hidden", [P, 1, SEQ], F32, s)
            rot_tmp = hidden[:, 0, :].rearrange("p (n t) -> p n t", n=4)
            pos_i = ones[:, :].bitcast(I32)
        with ExitStack() as s:
            ot_hi = sb("ot_hi", [P, HEADS, SEQ], F32R, s)
            ot_lo = sb("ot_lo", [P, HEADS, SEQ], F32R, s)
            probs = sb("probs", [P, HEADS_ROUND, BLOCKS * P], F32, s)
            probs_t = sb("probs_t", [P, HEADS_ROUND, 4 * 512], F32, s)
            v_att = sb("v_att", [P, NG, TILES, HEADS_ROUND * DH], F32, s)
            qk = sb("qk", [P, 2, 2, SEQ], F32, s)
            rot_a, rot_b = (probs_t[0:ROT, HEADS_ROUND - 1, n * 2 * SEQ:(n + 1) * 2 * SEQ].rearrange(
                "p (c t) -> p c t", c=2) for n in range(2))
            o_near = sb("o_near", [P, SEQ], F32, s)
            o_sum = sb("o_sum", [P, SEQ], F32, s)
            st_near = sb("st_near", [P, 2, HEADS_ROUND, TILES], F32, s)
            st_far = sb("st_far", [P, 2, HEADS_ROUND, TILES], F32, s)
            far_sel = sb("far_sel", [P, 16, 4], F32, s)
            far_nat = sb("far_nat", [P, TILES, 2, HEADS_ROUND], F32, s)
            m_low = sb("m_low", [P, HEADS_ROUND, TILES], F32, s)
            m_diff = sb("m_diff", [P, 2, HEADS_ROUND, TILES], F32, s)
            m_exp = sb("m_exp", [P, 2, HEADS_ROUND, TILES], F32, s)
            m_w = sb("m_w", [P, 2, HEADS_ROUND, TILES], F32, s)
            m_den = sb("m_den", [P, HEADS_ROUND, TILES], F32, s)
            m_fac = sb("m_fac", [P, 2, HEADS_ROUND, TILES], F32, s)
            fac_sel = sb("fac_sel", [P, TILES, HEADS_ROUND, DIL], F32, s)
            fac_far = sb("fac_far", [P, HEADS_ROUND, DIL], F32, s)

        w_loaded = [sem(f"w_loaded{j}") for j in range(RING)]
        w_hi_ready = sem("w_hi_ready")
        w_lo_ready = sem("w_lo_ready")
        w_used = sem("w_used")
        x_loaded = [sem(f"x_loaded{i}") for i in range(TILES)]
        ident_loaded = sem("ident_loaded")
        rot_loaded = sem("rot_loaded")
        wsp_loaded = sem("wsp_loaded")
        par_loaded = sem("par_loaded")
        sgu_loaded = sem("sgu_loaded")
        ln_loaded = [sem(f"ln_loaded{e}") for e in range(4)]
        cst_loaded = sem("cst_loaded")
        out_stored = sem("out_stored")
        ones_set = sem("ones_set")
        pad_set = sem("pad_set")
        dve_link = sem("dve_link")
        par_turned = sem("par_turned")
        par_set = sem("par_set")
        wsp_turned = sem("wsp_turned")
        wsp_set = sem("wsp_set")
        xt_turned = sem("xt_turned")
        xt_hi_set = sem("xt_hi_set")
        xt_set = sem("xt_set")
        sig_set = sem("sig_set")
        a_set = sem("a_set")
        acc_set = sem("acc_set")
        v_in = sem("v_in")
        v_gelu = sem("v_gelu")
        v_var = sem("v_var")
        v_std = sem("v_std")
        v_set = sem("v_set")
        u_set = sem("u_set")
        sv_done = sem("sv_done")
        g_set = sem("g_set")
        mixhi_set = sem("mixhi_set")
        mixlo_set = sem("mixlo_set")
        mean_done = sem("mean_done")
        xc_set = sem("xc_set")
        sq_set = sem("sq_set")
        sq_sum_set = sem("sq_sum_set")
        var_done = sem("var_done")
        std_set = sem("std_set")
        y_set = sem("y_set")
        silu_set = sem("silu_set")
        acc_done = sem("acc_done")
        ln_std = sem("ln_std")
        row_summed = sem("row_summed")
        ln_sq = sem("ln_sq")
        ln_scale = sem("ln_scale")
        x_scaled = sem("x_scaled")
        x_gained = sem("x_gained")
        x_normed = sem("x_normed")
        x_normed_end = sem("x_normed_end")
        sum_begun = sem("sum_begun")
        tap_product = sem("tap_product")
        tap_added = sem("tap_added")
        gate_set = sem("gate_set")
        hid_set = sem("hid_set")
        hthi_set = sem("hthi_set")
        ht_set = sem("ht_set")
        qk_copied = sem("qk_copied")
        qk_set = sem("qk_set")
        near_done = sem("near_done")
        far_done = sem("far_done")
        max_set = sem("max_set")
        exp_set = sem("exp_set")
        v_done = sem("v_done")
        v_copied = sem("v_copied")
        far_turned = sem("far_turned")
        angles_set = sem("angles_set")
        tables_set = sem("tables_set")
        diff_set = sem("diff_set")
        diff_exp = sem("diff_exp")
        fac_set = sem("fac_set")
        fac_turned = sem("fac_turned")
        fac_copied = sem("fac_copied")
        probs_set = sem("probs_set")
        pt_done = sem("pt_done")
        pt_act = sem("pt_act")
        pt_dve = sem("pt_dve")
        o_done = sem("o_done")
        near_copied = sem("near_copied")
        o_set = sem("o_set")
        othi_set = sem("othi_set")
        ot_set = sem("ot_set")

        block = ctx.enter_context(nc.Block())

        dve_taps = (8, 22)
        pool_taps = [(c, w) for c in range(2) for w in range(dve_taps[c], CONV_WIDTH)]
        chunk_taps = [CONV_WIDTH - n for n in dve_taps]
        after_slab = {5: 3, 6: 3, 7: 3, 8: 3, 9: 3, 10: 3, 11: 3, 12: 2, 13: 2, 14: 2, 15: 5}

        def conv_taps(slab):
            start = sum(count for s, count in after_slab.items() if s < slab)
            return [(n, *pool_taps[n]) for n in range(start, start + after_slab.get(slab, 0))]

        def quarter_copied(head, q):
            return (pt_dve if q % 2 else pt_act), head * 2 + q // 2 + 1

        class Link:

            def __init__(self, eng, which):
                self.eng, self.sem, self.n = eng, which, 0

            def mark(self, ins):
                ins.then_inc(self.sem, 1)
                self.n = self.n + 1
                return self.n

            def wait(self, value=None):
                self.eng.wait_ge(self.sem, self.n if value is None else value)

        def slab_view(slab):
            def chunks(w):
                return w.rearrange("(k p) n -> p k n", p=P)

            def cols(w, c):
                return chunks(w)[:, :, c * P:(c + 1) * P]

            def square(w, k, c0):
                return chunks(w)[:, k:k + 2, c0:c0 + 512]

            def rows(w, k):
                return chunks(w)[:, k:k + 1, :]

            if slab < S_OUT0:
                s = slab - S_IN
                if s < 8:
                    return cols(ev_w_in[0], CC * (s % 2) + s // 2)
                if s < 12:
                    return square(ev_w_in[0], 2 * (s - 8), 3 * CONV_CH)
                return cols(ev_w_in[0], 2 * CC + s - 12)
            if slab < S_UP0:
                s = slab - S_OUT0
                if s < 4:
                    return square(ev_w_out[0], CC + 2 * (s % 2), 512 * (s // 2))
                return rows(ev_w_out[0], s - 4)
            if S_DOWN0 <= slab < S_ATT:
                return rows(ffn_w_down[0], slab - S_DOWN0)
            if S_OUT1 <= slab < S_UP1:
                return rows(od_w_out[0], slab - S_OUT1)
            if slab >= S_DOWN1:
                return rows(ffn_w_down[1], slab - S_DOWN1)
            raise ValueError("this slab is addressed in its loop")

        @block.sync
        def _(sp):
            def load_view(slab, turns, view):
                slot = slab % RING
                if slab >= RING:
                    sp.wait_ge(w_lo_ready, slab - RING + 1 + RING * turns)
                dst = w_stage[slot][:, :].rearrange("p (k n) -> p k n", k=view.shape[1])
                sp.dma_start(dst, view).then_inc(w_loaded[slot], 16)

            def load(slab):
                load_view(slab, 0, slab_view(slab))

            def load_ln(e, layer, which):
                if e:
                    sp.wait_ge(x_normed, 2 * SHIFT_TILES * e)
                    sp.wait_ge(x_normed_end, 2 * e)
                for dst, src in ((norm_g, ln_g), (norm_b, ln_b)):
                    sp.dma_start(dst[:, :], src[layer, which:which + 1, :].partition_broadcast(P)
                                 ).then_inc(ln_loaded[e], 16)

            sp.dma_start(ident[:, :], ident_in).then_inc(ident_loaded, 16)
            for i in range(TILES):
                sp.dma_start(x_res[:, i, :], x[0, i * P:(i + 1) * P, :]).then_inc(x_loaded[i], 16)
                if i == 1:
                    load(0)
            for slab in range(1, RING):
                load(slab)
            sp.dma_start(cst[:, :], const_in).then_inc(cst_loaded, 16)
            sp.dma_start(par_rows[0:CONV_WIDTH, 0:CONV_CH], ev_conv_w[0]).then_inc(par_loaded, 16)
            for n, src in enumerate((ev_conv_b, ev_conv_ln_g, ev_conv_ln_b)):
                sp.dma_start(par_rows[4 * n:4 * n + 4, CONV_CH:CONV_CH + P],
                             src[0].rearrange("(c p) -> c p", p=P)).then_inc(par_loaded, 16)
            sp.dma_start(wsp_raw[:, :, :], ev_w_spatial[0].rearrange("h t s -> t h s")).then_inc(wsp_loaded, 16)
            sp.dma_start(sgu_g[:, :], ev_sgu_ln_g.partition_broadcast(P)).then_inc(sgu_loaded, 16)
            sp.dma_start(sgu_b[:, :], ev_sgu_ln_b.partition_broadcast(P)).then_inc(sgu_loaded, 16)
            for h in range(SGU_GROUPS):
                half = (h % 2) * GROUP_CH
                sp.dma_start(b_sp[half:half + GROUP_CH, h // 2, :],
                             ev_b_spatial[0, h:h + 1, :].partition_broadcast(GROUP_CH)).then_inc(sgu_loaded, 16)
            load_ln(0, 0, 0)
            for slab in range(RING, S_UP0):
                load(slab)

            def load_up(first, layer):
                gate_up = [w[layer].rearrange("(k p) (s n) -> p k s n", p=P, n=P) for w in (ffn_w_gate, ffn_w_up)]
                with sp.Fori(0, N_UP // RING) as t:
                    for j in range(RING):
                        load_view(first + j, t, gate_up[j % 2][:, :, 2 * t + j // 2, :])

            def load_down(first, layer, e):
                rows = ffn_w_down[layer].rearrange("(k p) n -> p k n", p=P)
                load(first)
                load(first + 1)
                load_ln(e, layer, 1)
                with sp.Fori(0, (N_DOWN - 2) // RING) as t:
                    for j in range(RING):
                        load_view(first + 2 + j, t, rows[:, bass.ds(RING * t + 2 + j, 1), :])

            load_up(S_UP0, 0)
            for q in range(TILES):
                sp.dma_start(pos_i[q * ROT:(q + 1) * ROT], positions[:, q * P:(q + 1) * P].partition_broadcast(ROT)
                             ).then_inc(rot_loaded, 16)
            load_down(S_DOWN0, 0, 1)
            qkv = od_w_qkv[0].rearrange("(k p) (g r y b h d) -> p k g r y b h d", p=P, g=NG, r=3, y=TURNS,
                                        b=ROUNDS_BODY, h=HEADS_ROUND)
            values = od_w_qkv[0].rearrange("(a k p) (g r y b d) -> a p k g r y b d", a=2, p=P, g=NG, r=3, y=TURNS,
                                           b=ROUNDS_BODY)
            with sp.Fori(0, TURNS) as turn:
                passed = turn * (ROUNDS_BODY * ROUND_SLABS // RING)
                for r in range(ROUNDS_BODY):
                    slab = S_ATT + r * ROUND_SLABS
                    for h in range(HEADS_ROUND):
                        for g in range(NG):
                            for c in range(2):
                                load_view(slab, passed, qkv[:, :, g, c, turn, r, h, :])
                                slab += 1
                    for g in range(NG):
                        for a in range(2):
                            load_view(slab, passed, values[a, :, :, g, 2, turn, r, :])
                            slab += 1
            load_ln(2, 1, 0)
            for slab in range(S_OUT1, S_UP1):
                load(slab)
            load_up(S_UP1, 1)
            load_down(S_DOWN1, 1, 3)
            for i in range(TILES):
                if i < 2:
                    sp.wait_ge(x_normed, 2 * (3 * SHIFT_TILES + i + 1))
                else:
                    sp.wait_ge(x_normed_end, 2 * (3 + i - 1))
                sp.dma_start(out[0, i * P:(i + 1) * P, :], x_res[:, i, :]).then_inc(out_stored, 16)
            sp.wait_ge(out_stored, 16 * TILES)

        @block.gpsimd
        def _(pool):
            pool.memset(ones[:, :], 1.0 / CONV_CH).then_inc(ones_set, 1)
            pool.memset(eps[:, :], EPS).then_inc(ones_set, 1)
            pool.memset(a_pad[:, :, 0:PAD], 0.0).then_inc(pad_set, 1)

            def split_low(slab, turns=0):
                pool.wait_ge(w_hi_ready, slab + 1 + RING * turns)
                pool.tensor_tensor(w_lo[slab % RING][:, :], w_stage[slab % RING][:, :],
                                   w_hi[slab % RING][:, :].bitcast(F32), ALU.subtract).then_inc(w_lo_ready, 1)

            def add_shift(e, i):
                for half in range(2):
                    xh = x_res[:, i, half * 512:(half + 1) * 512]
                    pool.wait_ge(x_gained, 2 * (e * SHIFT_TILES + i) + half + 1)
                    pool.tensor_tensor(xh, xh, norm_b[:, half * 512:(half + 1) * 512], ALU.add).then_inc(x_normed, 1)

            def norm(e, following):
                if e < 3:
                    split_low(following)
                add_shift(e, 0)
                add_shift(e, 1)
                if e < 3:
                    split_low(following + 1)
                    add_shift(e, 2)
                    split_low(following + 2)
                    split_low(following + 3)

            for slab in range(S_UP0):
                split_low(slab)
                for n, c, w in conv_taps(slab):
                    if w == dve_taps[c]:
                        pool.wait_ge(sum_begun, c + 1)
                    pool.wait_ge(tap_product, n + 1)
                    if n:
                        pool.wait_ge(tap_added, n)
                    pool.tensor_tensor(acc[:, c, :], acc[:, c, :], mixed[:, n % 2, :], ALU.add).then_inc(tap_added, 1)
            norm(0, S_UP0)

            def feed_forward(up, down, e):
                with pool.Fori(1, N_UP // RING) as t:
                    for j in range(RING):
                        split_low(up + j, t)
                with pool.Fori(0, N_DOWN // RING) as t:
                    for j in range(RING):
                        split_low(down + j, t)
                for slab in range(down + N_DOWN // RING * RING, down + N_DOWN):
                    split_low(slab)
                norm(e, down + N_DOWN)

            feed_forward(S_UP0, S_DOWN0, 1)
            with pool.Fori(0, N_ATT // RING - 1) as t:
                for j in range(RING):
                    split_low(S_ATT + RING + j, t)
            for slab in range(S_OUT1, S_UP1):
                split_low(slab)
            norm(2, S_UP1)
            feed_forward(S_UP1, S_DOWN1, 3)

        @block.tensor
        def _(pe):
            def slab_ready(slab, turns=0):
                pe.wait_ge(w_lo_ready, slab + 1 + RING * turns)

            def columns(slab, bank, tiles=(0, TILES)):
                hi, lo = (w[slab % RING][:, :].rearrange("p (k n) -> p k n", n=P) for w in (w_hi, w_lo))
                at = slice(tiles[0] * P, tiles[1] * P)
                for k in range(KD):
                    pe.matmul(ps[bank][:, at], hi[:, k, :], xt_hi[:, k, at], start=(k == 0), stop=False)
                    pe.matmul(ps[bank][:, at], hi[:, k, :], xt_lo[:, k, at], start=False, stop=False)
                    last = pe.matmul(ps[bank][:, at], lo[:, k, :], xt_hi[:, k, at], start=False, stop=(k == KD - 1))
                return last

            def columns_behind_norm(first, banks, e, turn=True, turns=0):
                pe.wait_ge(xt_set, 2 * TILES * (e + 1) + 4)
                for j, bank in enumerate(banks):
                    slab_ready(first + j, turns)
                    columns(first + j, bank, (0, 2))
                    if turn and j == 1:
                        turn_x(e + 1, 2)
                        turn_x(e + 1, 3)
                pe.wait_ge(xt_set, 2 * TILES * (e + 2))
                for j, bank in enumerate(banks):
                    columns(first + j, bank, (2, TILES)).then_inc(w_used, 1)

            def tokens(slab, base, width, bank, t_hi, t_lo, tile, first, end):
                hi, lo = (w[slab % RING][:, base:base + width] for w in (w_hi, w_lo))
                o = ps[bank][:, 0:width]
                pe.matmul(o, t_hi[:, tile * P:(tile + 1) * P], hi, start=first, stop=False)
                pe.matmul(o, t_hi[:, tile * P:(tile + 1) * P], lo, start=False, stop=False)
                return pe.matmul(o, t_lo[:, tile * P:(tile + 1) * P], hi, start=False, stop=end)

            def turn_x(e, i):
                for half in range(2):
                    bank = ps[i + 4 * half]
                    if e and i < SHIFT_TILES:
                        pe.wait_ge(x_normed, 2 * ((e - 1) * SHIFT_TILES + i) + half + 1)
                    elif e:
                        pe.wait_ge(x_normed_end, 2 * (e - 1) + half + 1)
                    for c in range(4):
                        col = (4 * half + c) * P
                        last = pe.transpose(bank[:, c * P:(c + 1) * P], x_res[:, i, col:col + P], ident[:, :])
                    last.then_inc(xt_turned, 1)

            pe.wait_ge(ident_loaded, 16)
            for i in range(TILES):
                pe.wait_ge(x_loaded[i], 16)
                turn_x(0, i)
            pe.wait_ge(xt_set, 4)
            slab_ready(0)
            columns(0, 0, (0, 2))

            def turn_parameters():
                pe.wait_ge(par_loaded, 16 * 4)
                for c in range(CC):
                    pe.transpose(ps[4][:, c * CONV_WIDTH:(c + 1) * CONV_WIDTH],
                                 par_rows[0:CONV_WIDTH, c * P:(c + 1) * P], ident[0:CONV_WIDTH, 0:CONV_WIDTH])
                pe.transpose(ps[4][:, CC * CONV_WIDTH:CC * CONV_WIDTH + 12], par_rows[0:12, CONV_CH:CONV_CH + P],
                             ident[0:12, 0:12]).then_inc(par_turned, 1)
                pe.wait_ge(wsp_loaded, 16)
                for half in range(2):
                    for h in range(4):
                        last = pe.transpose(ps[5 + half][:, h * P:(h + 1) * P], wsp_raw[:, 4 * half + h, :],
                                            ident[:, :])
                    last.then_inc(wsp_turned, 1)

            pe.wait_ge(xt_set, 2 * TILES)
            for c in range(CC):
                slab = S_IN + 2 * c
                if c >= 2:
                    pe.wait_ge(a_set, c - 1)
                for j in range(2):
                    slab_ready(slab + j)
                    columns(slab + j, 2 * (c % 2) + j, (2 if c + j == 0 else 0, TILES)).then_inc(w_used, 1)
                if c == 0:
                    turn_parameters()
            pe.wait_ge(par_set, 1)
            pe.wait_ge(wsp_set, 2)
            for s in range(4):
                slab = S_IN + 8 + s
                slab_ready(slab)
                for i in range(TILES):
                    for k in range(2):
                        last = tokens(slab, 512 * k, 512, 4 + i, xt_hi[:, 2 * s + k, :], xt_lo[:, 2 * s + k, :],
                                      i, s == 0 and k == 0, s == 3 and k == 1)
                    if s == 3 and i < TILES - 1:
                        last.then_inc(v_in, 1)
                last.then_inc(w_used, 1)
            for c in range(CC):
                slab = S_IN + 12 + c
                slab_ready(slab)
                if c % 2 == 0:
                    pe.wait_ge(a_set, 3 + c // 2)
                columns(slab, c).then_inc(w_used, 1)
            pe.wait_ge(ones_set, 1)
            pe.wait_ge(v_gelu, TILES)
            for c, (which, count) in enumerate(((tap_added, chunk_taps[0]), (tap_added, len(pool_taps)),
                                                (acc_set, 1), (acc_set, 2))):
                pe.wait_ge(which, count)
                last = pe.matmul(ps[7][:, :], ones[:, :], acc[:, c, :], start=(c == 0), stop=(c == CC - 1))
            last.then_inc(mean_done, 1)
            def spatial(pair):
                for n in range(TILES):
                    for h in (2 * pair, 2 * pair + 1):
                        half = (h % 2) * GROUP_CH
                        last = pe.matmul(ps[4 + pair][half:half + GROUP_CH, n * P:(n + 1) * P],
                                         v_tok[:, n, h * GROUP_CH:(h + 1) * GROUP_CH], wsp_t[:, h, :],
                                         start=True, stop=True)
                last.then_inc(sv_done, 1)

            pe.wait_ge(v_set, TILES)
            for pair in range(CC - 1):
                spatial(pair)

            def gating_rows(half):
                for s in range(2):
                    slab = S_OUT0 + 2 * half + s
                    slab_ready(slab)
                    if half == 0:
                        pe.wait_ge(mixlo_set, 2 * s + 2)
                    for i in range(TILES):
                        for k in range(2):
                            row = CC + 2 * s + k
                            last = tokens(slab, 512 * k, 512, i + 4 * half, mix_hi[:, row, :], mix_lo[:, row, :],
                                          i, s == 0 and k == 0, False)
                        if half == 0 and s == 0 and i == 1:
                            pe.wait_ge(xc_set, CC)
                            spatial(CC - 1)
                        if half == 0 and s == 1 and i == 1:
                            pe.wait_ge(sq_sum_set, 1)
                            pe.matmul(ps[4][:, :], ones[:, :], acc[:, 0, :], start=True, stop=True
                                      ).then_inc(var_done, 1)
                    last.then_inc(w_used, 1)

            def both_halves(slab, t_hi, t_lo, row, i, first, end):
                for half in range(2):
                    last = tokens(slab, 512 * half, 512, i + 4 * half, t_hi[:, row, :], t_lo[:, row, :], i, first, end)
                return last

            def whole_rows(slab, t_hi, t_lo, row, order=range(TILES), first=False, banks_read=None):
                slab_ready(slab)
                for n, i in enumerate(order):
                    if n == 2 and banks_read:
                        pe.wait_ge(*banks_read)
                    last = both_halves(slab, t_hi, t_lo, row, i, first, False)
                last.then_inc(w_used, 1)

            pe.wait_ge(u_set, CC)
            gating_rows(0)
            pe.wait_ge(std_set, 1)
            gating_rows(1)

            def finish_tiles(e, slab, t_hi, t_lo, row):
                for j in range(3):
                    slab_ready(slab + j)
                for i in range(TILES):
                    for j in range(3):
                        last = both_halves(slab + j, t_hi, t_lo, row + j, i, False, j == 2)
                        if i == TILES - 1:
                            last.then_inc(w_used, 1)
                            if j == 1 and e < 3:
                                turn_x(e + 1, 0)
                    if i < TILES - 1:
                        last.then_inc(acc_done, 1)
                if e < 3:
                    turn_x(e + 1, 1)

            for k in range(CC):
                pe.wait_ge(mixlo_set, CC + k + 1)
                if k == 0:
                    whole_rows(S_OUT0 + 4, mix_hi, mix_lo, 0)
            finish_tiles(0, S_OUT0 + 5, mix_hi, mix_lo, 1)

            def feed_forward(layer, up, down, e):
                done = layer * KF

                def product(slab, t, bank):
                    slab_ready(slab, t)
                    columns(slab, bank).then_inc(w_used, 1)

                columns_behind_norm(up, (0, 4, 1), e - 1)
                product(up + 3, 0, 5)
                with pe.Fori(1, N_UP // RING) as t:
                    for j in range(2):
                        pe.wait_ge(hid_set, done + 2 * t + j - 1)
                        product(up + 2 * j, t, j)
                        product(up + 2 * j + 1, t, 4 + j)
                for k in range(KF - 3):
                    pe.wait_ge(ht_set, done + k + 1)
                    if k == 0:
                        pe.wait_ge(hid_set, done + KF - 1)
                        whole_rows(down, ht_hi, ht_lo, 0, (2, 0, 3, 1), True, (hid_set, done + KF))
                    else:
                        whole_rows(down + k, ht_hi, ht_lo, k)
                pe.wait_ge(ht_set, done + KF)
                finish_tiles(e, down + KF - 3, ht_hi, ht_lo, KF - 3)

            feed_forward(0, S_UP0, S_DOWN0, 1)

            turn_x(2, 2)
            turn_x(2, 3)
            pe.wait_ge(cst_loaded, 16)
            lt = cst[:, C_LT:C_LT + TILES * P].rearrange("p (i n) -> p i n", i=TILES)
            lm = cst[:, C_L:C_L + TILES * P].rearrange("p (i n) -> p i n", i=TILES)
            with pe.Fori(0, TURNS) as turn:
                for r in range(ROUNDS_BODY):
                    rnd = turn * ROUNDS_BODY + r
                    first = S_ATT + r * ROUND_SLABS
                    passed = turn * (ROUNDS_BODY * ROUND_SLABS // RING)
                    n_qk = HEADS_ROUND * NG

                    def scores(s):
                        h, g = divmod(s, NG)
                        q, key = qk[:, s % 2, 0, :], qk[:, s % 2, 1, :]
                        pe.wait_ge(qk_set, rnd * n_qk + s + 1)
                        if h == 1 and g < 2:
                            pe.wait_ge(max_set, rnd * 2 * HEADS_ROUND + g + 1)
                        for i in range(TILES):
                            lhs = q[:, i * P:(i + 1) * P]
                            if g:
                                c = (i % 2) * 2 * P + (g - 1) * P
                                last = pe.matmul(ps[6 + i // 2][:, c:c + P], lhs, key[:, i * P:(i + 1) * P],
                                                 start=True, stop=True)
                            elif i == 0:
                                last = pe.matmul(ps[4][:, P:2 * P], lhs, key[:, 0:P], start=True, stop=True)
                            else:
                                c = (i % 2) * 2 * P
                                last = pe.matmul(ps[4 + i // 2][:, c:c + 2 * P], lhs,
                                                 key[:, (i - 1) * P:(i + 1) * P], start=True, stop=True)
                        last.then_inc(far_done if g else near_done, 1)

                    for s in range(n_qk):
                        if s >= 2:
                            pe.wait_ge(qk_copied, rnd * n_qk + s - 1)
                        if r == 0 and s == 0:
                            columns_behind_norm(first, (0, 1), 1, False, passed)
                        else:
                            if s == 1:
                                pe.wait_ge(o_set, rnd * HEADS_ROUND + 1)
                            for c in range(2):
                                slab = first + 2 * s + c
                                slab_ready(slab, passed)
                                columns(slab, 2 * (s % 2) + c).then_inc(w_used, 1)
                        if s:
                            scores(s - 1)
                    def value_tile(g, a, i):
                        slab = first + 2 * n_qk + 2 * g + a
                        if a == 0 and g == 0 and i % 2 == 0:
                            pe.wait_ge(qk_copied, rnd * n_qk + n_qk - 1 + i // 2)
                        elif a == 0 and g:
                            pe.wait_ge(v_copied, (rnd * NG + g - 1) * TILES + i + 1)
                        cols = slice(i * P, (i + 1) * P) if g == 0 else slice(i, SEQ, DIL)
                        o = ps[i][:, 0:HEADS_ROUND * DH]
                        for k in range(4):
                            hi, lo = (w[slab % RING][:, k * 256:(k + 1) * 256] for w in (w_hi, w_lo))
                            t_hi, t_lo = (t[:, 4 * a + k, cols] for t in (xt_hi, xt_lo))
                            pe.matmul(o, t_hi, hi, start=(a == 0 and k == 0), stop=False)
                            pe.matmul(o, t_hi, lo, start=False, stop=False)
                            last = pe.matmul(o, t_lo, hi, start=False, stop=(a == 1 and k == 3))
                        if i == TILES - 1:
                            last.then_inc(w_used, 1)
                        elif a == 1:
                            last.then_inc(v_done, 1)

                    def turn_probs(h):
                        pe.wait_ge(probs_set, rnd * HEADS_ROUND + h + 1)
                        for q in range(4):
                            if h:
                                pe.wait_ge(*quarter_copied(rnd * HEADS_ROUND + h - 1, q))
                            for b in range(4 * q, min(4 * q + 4, BLOCKS)):
                                last = pe.transpose(ps[4 + q][:, (b % 4) * P:(b % 4 + 1) * P],
                                                    probs[:, h, b * P:(b + 1) * P], ident[:, :])
                            last.then_inc(pt_done, 1)

                    def values(h):
                        near, far = ps[2 * h], ps[2 * h + 1]
                        hd = slice(h * DH, (h + 1) * DH)
                        head = rnd * HEADS_ROUND + h
                        if h == 0:
                            pe.wait_ge(v_copied, (rnd + 1) * NG * TILES)
                        for j in range(TILES):
                            w = min(2, TILES - j) * P
                            if j % 2 == 0:
                                pe.wait_ge(*quarter_copied(head, j // 2))
                            last = pe.matmul(near[:, j * P:j * P + w], v_att[:, 0, j, hd],
                                             probs_t[:, h, 2 * j * P:2 * j * P + w], start=(j == 0),
                                             stop=(j == TILES - 1), skip_group_check=True)
                        for j in range(TILES):
                            b = BLOCKS_A + 2 * j
                            if j in (0, 2):
                                pe.wait_ge(*quarter_copied(head, 2 + j // 2))
                            for g in range(2):
                                last = pe.matmul(far[:, j * P:(j + 1) * P], v_att[:, 1 + g, j, hd],
                                                 probs_t[:, h, (b + g) * P:(b + g + 1) * P],
                                                 start=(j == 0 and g == 0), stop=(g == 1), skip_group_check=True)
                        last.then_inc(o_done, 1)

                    for g in range(NG):
                        for a in range(2):
                            slab_ready(first + 2 * n_qk + 2 * g + a, passed)
                            for i in range(TILES):
                                value_tile(g, a, i)
                                if g == 2 and a == 1 and i == 1:
                                    turn_probs(0)
                            if g == 0 and a == 0:
                                scores(n_qk - 1)
                            if g == 2 and a == 0:
                                pe.wait_ge(fac_set, rnd + 1)
                                for i in range(TILES):
                                    last = pe.matmul(ps[5][:, 0:2 * DIL], lm[:, i, :],
                                                     fac_sel[:, i, :, :].rearrange("p a b -> p (a b)"),
                                                     start=(i == 0), stop=(i == TILES - 1))
                                last.then_inc(fac_turned, 1)
                        if g == 1:
                            pe.wait_ge(exp_set, (rnd + 1) * 2 * HEADS_ROUND)
                            for i in range(TILES):
                                last = pe.matmul(ps[4][:, i * 16:(i + 1) * 16], lt[:, i, :],
                                                 st_far[:, :, :, :].rearrange("p a b c -> p (a b c)"),
                                                 start=True, stop=True)
                            last.then_inc(far_turned, 1)
                    turn_probs(1)
                    values(0)
                    values(1)
                    pe.wait_ge(o_set, (rnd + 1) * HEADS_ROUND)

            for k in range(HEADS - 3):
                pe.wait_ge(ot_set, k + 1)
                if k == 0:
                    whole_rows(S_OUT1, ot_hi, ot_lo, 0, first=True, banks_read=(o_set, HEADS + 1))
                else:
                    whole_rows(S_OUT1 + k, ot_hi, ot_lo, k)
            pe.wait_ge(ot_set, HEADS)
            finish_tiles(2, S_OUT1 + HEADS - 3, ot_hi, ot_lo, HEADS - 3)
            feed_forward(1, S_UP1, S_DOWN1, 3)

        @block.scalar
        def _(act):
            def split_high(slab, turns=0):
                act.wait_ge(w_loaded[slab % RING], 16 * (slab // RING + 1) + 16 * turns)
                if slab >= RING:
                    act.wait_ge(w_used, slab - RING + 1 + RING * turns)
                act.activation(w_hi[slab % RING][:, :], w_stage[slab % RING][:, :], ACT.Copy).then_inc(w_hi_ready, 1)

            def x_high(e, i):
                for half in range(2):
                    act.wait_ge(xt_turned, 2 * TILES * e + 2 * i + half + 1)
                    act.activation(xt_hi[:, 4 * half:4 * half + 4, i * P:(i + 1) * P],
                                   ps[i + 4 * half][:, :].rearrange("p (c n) -> p c n", n=P), ACT.Copy
                                   ).then_inc(xt_hi_set, 1)

            def norm(e, following):
                def root(i):
                    n = e * TILES + i
                    act.wait_ge(row_summed, n + 1)
                    act.activation(xt_lo[:, :, i * P:(i + 1) * P], x_res[:, i, :].rearrange("p (c n) -> p c n", n=P),
                                   ACT.Square, bias=neg_mean[:, i:i + 1], accum_out=sq_sum[:, i:i + 1]
                                   ).then_inc(ln_sq, 1)
                    act.wait_ge(ln_sq, n + 1)
                    act.activation(std[:, i:i + 1], sq_sum[:, i:i + 1], ACT.Sqrt, bias=eps[:, 0:1],
                                   scale=1.0 / D_MODEL).then_inc(ln_std, 1)

                def scale(i):
                    act.wait_ge(ln_scale, e * SHIFT_TILES + i + 1)
                    act.activation(x_res[:, i, :], x_res[:, i, :], ACT.Identity, bias=shift[:, i:i + 1],
                                   scale=rstd[:, i:i + 1]).then_inc(x_scaled, 1)

                def high(i):
                    if e < 3:
                        x_high(e + 1, i)

                def split(j):
                    if e < 3:
                        split_high(following + j)

                split(0)
                root(0)
                scale(0)
                root(1)
                scale(1)
                split(1)
                high(0)
                root(2)
                if e != 1:
                    high(1)
                if e < 3:
                    scale(2)
                if e != 1:
                    split(2)
                root(3)
                if e == 1:
                    high(1)
                    split(2)
                high(2)
                split(3)
                high(3)

            act.wait_ge(ones_set, 2)
            act.activation(std[:, 0:1], eps[:, 0:1], ACT.Copy)
            x_high(0, 0)
            x_high(0, 1)
            split_high(0)
            x_high(0, 2)
            x_high(0, 3)
            for slab in range(1, RING):
                split_high(slab)
            def multiply_taps(slab):
                for n, c, w in conv_taps(slab):
                    if w == dve_taps[c]:
                        act.wait_ge(a_set, c + 1)
                    if n >= 2:
                        act.wait_ge(tap_added, n - 1)
                    at = c * CONV_WIDTH + w
                    act.activation(mixed[:, n % 2, :], a_pad[:, c, w:w + SEQ], ACT.Copy, scale=par[:, at:at + 1]
                                   ).then_inc(tap_product, 1)

            def split_and_taps(slab):
                split_high(slab)
                multiply_taps(slab)

            for c in range(CC):
                act.wait_ge(w_used, S_IN + 2 * c + 2)
                if c >= 2:
                    act.wait_ge(a_set, c - 1)
                act.activation(sig[:, c % 2, :], ps[2 * (c % 2) + 1][:, :], ACT.Sigmoid).then_inc(sig_set, 1)
                if c == 0:
                    act.wait_ge(par_turned, 1)
                    act.activation(par[:, :], ps[4][:, 0:CC * CONV_WIDTH + 12], ACT.Copy).then_inc(par_set, 1)
                    act.wait_ge(par_set, 1)
                split_and_taps(2 * c + 4)
                split_and_taps(2 * c + 5)
            split_and_taps(12)
            split_and_taps(13)
            split_high(14)
            for i in range(TILES):
                if i < TILES - 1:
                    act.wait_ge(v_in, i + 1)
                else:
                    act.wait_ge(w_used, S_IN + 12)
                act.activation(v_tok[:, i, :], ps[4 + i][:, :], ACT.Gelu).then_inc(v_gelu, 1)
            multiply_taps(14)
            split_high(15)
            act.wait_ge(v_var, TILES)
            act.activation(std[:, 0:TILES], mean_var[:, :, 1], ACT.Sqrt, bias=eps[:, 0:1]).then_inc(v_std, 1)
            multiply_taps(15)
            for c in range(CC):
                act.wait_ge(w_used, S_IN + 12 + c + 1)
                act.activation(u_t[:, c, :], ps[c][:, :], ACT.Gelu).then_inc(u_set, 1)
                split_high(16 + c)
            for c in range(CC):
                act.wait_ge(g_set, c + 1)
                act.activation(mix_hi[:, CC + c, :], mixed[:, c % 2, :], ACT.Copy).then_inc(mixhi_set, 1)
                if c == 1:
                    for cc in range(CC):
                        act.wait_ge(xc_set, cc + 1)
                        act.activation(acc[:, cc, :], a_pad[:, cc, 0:SEQ], ACT.Square).then_inc(sq_set, 1)
            split_high(20)
            act.wait_ge(var_done, 1)
            act.activation(sig[:, 0, :], ps[4][:, :], ACT.Sqrt, bias=eps[:, 0:1]).then_inc(std_set, 1)
            gain, offset = CC * CONV_WIDTH + 4, CC * CONV_WIDTH + 8
            for c in range(CC):
                act.wait_ge(y_set, c + 1)
                if c >= 2:
                    act.wait_ge(mixlo_set, CC + c - 1)
                act.activation(mixed[:, c % 2, :], a_pad[:, c, 0:SEQ], ACT.Silu, scale=par[:, gain + c:gain + c + 1],
                               bias=par[:, offset + c:offset + c + 1]).then_inc(silu_set, 1)
                act.wait_ge(silu_set, c + 1)
                act.activation(mix_hi[:, c, :], mixed[:, c % 2, :], ACT.Copy).then_inc(mixhi_set, 1)
                if c < 3:
                    split_high(21 + c)
            norm(0, S_UP0)

            def rotary_tables():
                for n, table in enumerate((sin_t, cos_t)):
                    act.wait_ge(angles_set, n + 1)
                    for q in range(TILES):
                        last = act.activation(table[:, q * P:(q + 1) * P], rot_tmp[ROT * q:ROT * (q + 1), 3 - n, :], ACT.Sin)
                    last.then_inc(tables_set, 1)

            def feed_forward(layer, up, down, e):
                done = layer * KF

                def chunk(t, j):
                    n = done + 2 * t + j
                    act.wait_ge(w_used, up + 4 * t + 2 * j + 1)
                    if not (layer == 0 and isinstance(t, int) and t + j == 0):
                        act.wait_ge(ht_set, n)
                    act.activation(hidden[:, 0, :], ps[j][:, :], ACT.Silu).then_inc(gate_set, 1)
                    split_high(up + 4 + 2 * j, t)
                    act.wait_ge(hid_set, n + 1)
                    act.activation(ht_hi[:, bass.ds(2 * t + j, 1), :], hidden[:, :, :], ACT.Copy).then_inc(hthi_set, 1)
                    split_high(up + 5 + 2 * j, t)

                for j in range(2):
                    chunk(0, j)
                with act.Fori(1, N_UP // RING) as t:
                    for j in range(2):
                        chunk(t, j)
                with act.Fori(0, (N_DOWN - RING) // RING) as t:
                    for j in range(RING):
                        split_high(down + RING + j, t)
                if layer == 0:
                    rotary_tables()
                for slab in range(down + N_DOWN // RING * RING, down + N_DOWN):
                    split_high(slab)
                norm(e, down + N_DOWN)

            feed_forward(0, S_UP0, S_DOWN0, 1)

            with act.Fori(0, TURNS) as turn:
                for r in range(ROUNDS_BODY):
                    rnd = turn * ROUNDS_BODY + r
                    first = S_ATT + r * ROUND_SLABS
                    passed = turn * (ROUNDS_BODY * ROUND_SLABS // RING)
                    n_qk = HEADS_ROUND * NG

                    def copy_qk(s):
                        g = s % NG
                        act.wait_ge(w_used, first + 2 * s + 2 + RING * passed)
                        for c in range(2):
                            src = ps[2 * (s % 2) + c][:, :]
                            dst = qk[:, s % 2, c, :]
                            if g:
                                src = src.rearrange("p (m r) -> p r m", r=DIL)
                                dst = dst.rearrange("p (r m) -> p r m", r=DIL)
                            if s >= 2 and c == 0:
                                act.wait_ge(*((far_done, rnd * 2 * HEADS_ROUND + 2 * ((s - 2) // NG) + (s - 2) % NG)
                                              if (s - 2) % NG else
                                              (near_done, rnd * HEADS_ROUND + (s - 2) // NG + 1)))
                            last = act.activation(dst, src, ACT.Copy)
                        last.then_inc(qk_copied, 1)

                    def exps(h, far):
                        n = rnd * 2 * HEADS_ROUND + 2 * h + far
                        act.wait_ge(max_set, n + 1)
                        st = st_far if far else st_near
                        for i in range(TILES):
                            if far:
                                p = probs[:, h, (BLOCKS_A + 2 * i) * P:(BLOCKS_A + 2 * i + 2) * P]
                            else:
                                p = probs[:, h, max(0, 2 * i - 1) * P:(2 * i + 1) * P]
                            last = act.activation(p, p, ACT.Exp, bias=st[:, 0, h, i:i + 1], scale=SCALE,
                                                  accum_out=st[:, 1, h, i:i + 1])
                        last.then_inc(exp_set, 1)

                    for s in range(n_qk):
                        copy_qk(s)
                        split_high(first + 2 * s + 4, passed)
                        split_high(first + 2 * s + 5, passed)
                        if s in (1, 4):
                            exps(s // NG, 0)
                        if s == 3:
                            exps(0, 1)
                    exps(1, 1)
                    def copy_probs(h):
                        for q in (0, 2):
                            act.wait_ge(pt_done, (rnd * HEADS_ROUND + h) * 4 + q + 1)
                            act.activation(probs_t[:, h, q * 512:(q + 1) * 512], ps[4 + q][:, :], ACT.Copy
                                           ).then_inc(pt_act, 1)

                    for g in range(NG):
                        slab = first + 2 * n_qk + 2 * g
                        if g:
                            split_high(slab + 4, passed)
                        for i in range(TILES):
                            if i < TILES - 1:
                                act.wait_ge(v_done, (rnd * NG + g) * (TILES - 1) + i + 1)
                            else:
                                act.wait_ge(w_used, slab + 2 + RING * passed)
                            act.activation(v_att[:, g, i, :], ps[i][:, 0:HEADS_ROUND * DH], ACT.Copy
                                           ).then_inc(v_copied, 1)
                            if g == 2 and i == 1:
                                copy_probs(0)
                        if g == 0:
                            split_high(slab + 4, passed)
                        if g < 2:
                            split_high(slab + 5, passed)
                        if g == 1:
                            act.wait_ge(diff_set, rnd + 1)
                            act.activation(m_exp[:, :, :, :], m_diff[:, :, :, :], ACT.Exp).then_inc(diff_exp, 1)
                    copy_probs(1)
                    split_high(first + 2 * n_qk + 2 * NG + 3, passed)
                    for h in range(HEADS_ROUND):
                        act.wait_ge(o_done, rnd * HEADS_ROUND + h + 1)
                        act.activation(o_near[:, :], ps[2 * h][:, :], ACT.Copy).then_inc(near_copied, 1)
                        act.wait_ge(o_set, rnd * HEADS_ROUND + h + 2)
                        act.activation(ot_hi[:, bass.ds(rnd * HEADS_ROUND + h, 1), :],
                                       o_sum[:, :].rearrange("p (a n) -> p a n", a=1), ACT.Copy).then_inc(othi_set, 1)
            for slab in range(S_OUT1 + RING, S_UP1):
                split_high(slab)
            norm(2, S_UP1)
            feed_forward(1, S_UP1, S_DOWN1, 3)

        @block.vector
        def _(dve):
            link = Link(dve, dve_link)

            def x_low(e, i):
                for half in range(2):
                    n = 2 * TILES * e + 2 * i + half + 1
                    dve.wait_ge(xt_hi_set, n)
                    hi = xt_hi[:, 4 * half:4 * half + 4, i * P:(i + 1) * P]
                    dve.tensor_tensor(xt_lo[:, 4 * half:4 * half + 4, i * P:(i + 1) * P],
                                      ps[i + 4 * half][:, :].rearrange("p (c n) -> p c n", n=P), hi.bitcast(F32),
                                      ALU.subtract).then_inc(xt_set, 1)

            def norm_in(e, i):
                if i < TILES - 1:
                    dve.wait_ge(acc_done, e * (TILES - 1) + i + 1)
                else:
                    dve.wait_ge(w_used, (S_UP0, S_ATT, S_UP1, N_SLABS)[e])
                for half in range(2):
                    xh = x_res[:, i, half * 512:(half + 1) * 512]
                    link.mark(dve.scalar_tensor_tensor(out=xh, in0=xh, scalar=ALPHA, in1=ps[i + 4 * half][:, :],
                                                       op0=ALU.mult, op1=ALU.add, accum_out=row_sum[:, i, half:half + 1]))
                link.wait()
                dve.tensor_scalar(neg_mean[:, i:i + 1], row_sum[:, i, 0:1], row_sum[:, i, 1:2], -1.0 / D_MODEL,
                                  ALU.add, ALU.mult).then_inc(row_summed, 1)

            def norm_scale(e, i):
                dve.wait_ge(ln_std, e * TILES + i + 1)
                link.mark(dve.reciprocal(rstd[:, i:i + 1], std[:, i:i + 1]))
                link.wait()
                dve.tensor_tensor(shift[:, i:i + 1], neg_mean[:, i:i + 1], rstd[:, i:i + 1], ALU.mult
                                  ).then_inc(ln_scale, 1)

            def norm_gain(e, i):
                if i == 0:
                    dve.wait_ge(ln_loaded[e], 32)
                dve.wait_ge(x_scaled, e * SHIFT_TILES + i + 1)
                for half in range(2):
                    xh, cols = x_res[:, i, half * 512:(half + 1) * 512], slice(half * 512, (half + 1) * 512)
                    dve.tensor_tensor(xh, xh, norm_g[:, cols], ALU.mult).then_inc(x_gained, 1)

            def norm_short_gain(e, i):
                dve.wait_ge(ln_sq, e * TILES + i + 1)
                for cols in (slice(0, 512), slice(512, D_MODEL)):
                    link.mark(dve.scalar_tensor_tensor(out=x_res[:, i, cols], in0=x_res[:, i, cols],
                                                       scalar=neg_mean[:, i:i + 1], in1=norm_g[:, cols],
                                                       op0=ALU.add, op1=ALU.mult))

            def norm_short_end(e, i):
                dve.wait_ge(ln_std, e * TILES + i + 1)
                link.mark(dve.reciprocal(rstd[:, i:i + 1], std[:, i:i + 1]))
                link.wait()
                for cols in (slice(0, 512), slice(512, D_MODEL)):
                    dve.scalar_tensor_tensor(out=x_res[:, i, cols], in0=x_res[:, i, cols], scalar=rstd[:, i:i + 1],
                                             in1=norm_b[:, cols], op0=ALU.mult, op1=ALU.add).then_inc(x_normed_end, 1)

            def norm(e):
                def low(i):
                    x_low(e + 1, i)

                norm_in(e, 0)
                norm_scale(e, 0)
                norm_in(e, 1)
                norm_gain(e, 0)
                norm_scale(e, 1)
                if e == 3:
                    norm_in(e, 2)
                    norm_gain(e, 1)
                    norm_short_gain(e, 2)
                    norm_in(e, 3)
                    norm_short_end(e, 2)
                    norm_short_gain(e, 3)
                    norm_short_end(e, 3)
                    return
                norm_gain(e, 1)
                norm_in(e, 2)
                low(0)
                norm_scale(e, 2)
                if e != 1:
                    low(1)
                norm_in(e, 3)
                norm_gain(e, 2)
                norm_short_gain(e, 3)
                norm_short_end(e, 3)
                if e == 1:
                    low(1)
                low(2)
                low(3)

            for i in range(TILES):
                x_low(0, i)
            def gate_in(c):
                dve.wait_ge(sig_set, c + 1)
                dve.tensor_tensor(a_pad[:, c, PAD:PAD + SEQ], ps[2 * (c % 2)][:, :], sig[:, c % 2, :], ALU.mult
                                  ).then_inc(a_set, 1)

            self_tap = {}

            def taps(*steps):
                for c, w in steps:
                    src = a_pad[:, c, w:w + SEQ]
                    weight = par[:, c * CONV_WIDTH + w:c * CONV_WIDTH + w + 1]
                    bias = par[:, CC * CONV_WIDTH + c:CC * CONV_WIDTH + c + 1]
                    if w == 0:
                        ins = dve.tensor_scalar(acc[:, c, :], src, weight, bias, ALU.mult, ALU.add)
                    else:
                        link.wait(self_tap[c])
                        ins = dve.scalar_tensor_tensor(out=acc[:, c, :], in0=src, scalar=weight, in1=acc[:, c, :],
                                                       op0=ALU.mult, op1=ALU.add)
                    if c < 2 and w == dve_taps[c] - 1:
                        ins.then_inc(sum_begun, 1)
                    elif w == CONV_WIDTH - 1:
                        ins.then_inc(acc_set, 1)
                    else:
                        self_tap[c] = link.mark(ins)

            gate_in(0)
            dve.wait_ge(wsp_loaded, 16)
            for half in range(2):
                if half == 0:
                    dve.wait_ge(cst_loaded, 16)
                dve.wait_ge(wsp_turned, half + 1)
                dve.tensor_tensor(wsp_t[:, 4 * half:4 * half + 4, :],
                                  ps[5 + half][:, :].rearrange("p (h n) -> p h n", n=P),
                                  cst[:, C_UT:C_UT + P].unsqueeze(1).broadcast_to([P, 4, P]), ALU.mult).then_inc(wsp_set, 1)
            dve.wait_ge(a_set, 1)
            dve.wait_ge(par_set, 1)
            taps(*((0, w) for w in range(dve_taps[0])))
            gate_in(1)
            dve.wait_ge(a_set, 2)
            ahead = 8
            taps(*((1, w) for w in range(dve_taps[1] - ahead)))
            gate_in(2)
            dve.wait_ge(a_set, 3)
            taps(*(step for w in range(ahead) for step in ((1, dve_taps[1] - ahead + w), (2, w))))
            gate_in(3)
            dve.wait_ge(a_set, 4)
            rest = [(2, w) for w in range(ahead, CONV_WIDTH)] + [(3, w) for w in range(CONV_WIDTH)]
            rest.sort(key=lambda step: step[1] - (ahead if step[0] == 2 else 0))
            before, between = 42, 1
            taps(*rest[:before])
            rest = rest[before:]

            def some_taps():
                taps(*rest[:between])
                del rest[:between]

            dve.wait_ge(sgu_loaded, 16 * (2 + SGU_GROUPS))
            for i in range(TILES):
                dve.wait_ge(v_gelu, i + 1)
                link.mark(dve.bn_stats(stats[:, 6 * (i % 2):6 * (i % 2) + 6], v_tok[:, i, :]))
                link.wait()
                dve.bn_aggr(mean_var[:, i, :], stats[:, 6 * (i % 2):6 * (i % 2) + 6]).then_inc(v_var, 1)
                some_taps()
            for i in range(TILES):
                if i == 0:
                    dve.wait_ge(v_var, TILES)
                link.mark(dve.scalar_tensor_tensor(out=v_tok[:, i, :], in0=v_tok[:, i, :], scalar=mean_var[:, i, 0:1],
                                                   in1=sgu_g[:, :], op0=ALU.subtract, op1=ALU.mult))
            dve.wait_ge(v_std, 1)
            link.mark(dve.reciprocal(rstd[:, 0:TILES], std[:, 0:TILES]))
            link.wait()
            for i in range(TILES):
                dve.scalar_tensor_tensor(out=v_tok[:, i, :], in0=v_tok[:, i, :], scalar=rstd[:, i:i + 1],
                                         in1=sgu_b[:, :], op0=ALU.mult, op1=ALU.add).then_inc(v_set, 1)
            taps(*rest)
            dve.wait_ge(tap_added, len(pool_taps))

            def gated(c):
                dve.wait_ge(sv_done, c + 1)
                dve.wait_ge(u_set, c + 1)
                if c >= 2:
                    dve.wait_ge(mixhi_set, c - 1)
                    dve.wait_ge(mixlo_set, c - 1)
                link.mark(dve.tensor_tensor(mixed[:, c % 2, :].rearrange("p (n t) -> p n t", t=P),
                                            ps[4 + c][:, :].rearrange("p (n t) -> p n t", t=P),
                                            b_sp[:, c, :].unsqueeze(1).broadcast_to([P, TILES, P]), ALU.add))
                link.wait()
                dve.tensor_tensor(mixed[:, c % 2, :], mixed[:, c % 2, :], u_t[:, c, :], ALU.mult).then_inc(g_set, 1)

            def gated_low(c):
                dve.wait_ge(mixhi_set, c + 1)
                dve.tensor_tensor(mix_lo[:, CC + c, :], mixed[:, c % 2, :], mix_hi[:, CC + c, :].bitcast(F32),
                                  ALU.subtract).then_inc(mixlo_set, 1)

            gated(0)
            gated(1)
            gated_low(0)
            gated_low(1)
            dve.wait_ge(mean_done, 1)
            for c in range(CC):
                dve.tensor_tensor(a_pad[:, c, 0:SEQ], acc[:, c, :], ps[7][:, :], ALU.subtract).then_inc(xc_set, 1)
            gated(2)
            gated(3)
            gated_low(2)
            gated_low(3)
            dve.wait_ge(sq_set, CC)
            link.mark(dve.tensor_tensor(acc[:, 2, :], acc[:, 2, :], acc[:, 3, :], ALU.add))
            link.mark(dve.tensor_tensor(acc[:, 0, :], acc[:, 0, :], acc[:, 1, :], ALU.add))
            link.wait()
            dve.tensor_tensor(acc[:, 0, :], acc[:, 0, :], acc[:, 2, :], ALU.add).then_inc(sq_sum_set, 1)

            dve.wait_ge(std_set, 1)
            link.mark(dve.reciprocal(sig[:, 0, :], sig[:, 0, :]))
            link.wait()
            dve.wait_ge(sq_set, CC)
            for c in range(CC):
                dve.tensor_tensor(a_pad[:, c, 0:SEQ], a_pad[:, c, 0:SEQ], sig[:, 0, :], ALU.mult).then_inc(y_set, 1)
            for c in range(CC):
                dve.wait_ge(mixhi_set, CC + c + 1)
                dve.tensor_tensor(mix_lo[:, c, :], mixed[:, c % 2, :], mix_hi[:, c, :].bitcast(F32), ALU.subtract
                                  ).then_inc(mixlo_set, 1)
            norm(0)

            def rotary_angles():
                dve.wait_ge(rot_loaded, 16 * TILES)
                dve.wait_ge(cst_loaded, 16)
                ang, k, r_lo = rot_tmp[:, 0, :], rot_tmp[:, 1, :], rot_tmp[:, 2, :]

                def turns_of(src, scale, phase):
                    link.mark(dve.tensor_scalar(k, src, scale, phase, ALU.mult, ALU.add))
                    link.wait()
                    link.mark(dve.tensor_scalar(k, k, ROUND_MAGIC, None, ALU.add))
                    link.wait()
                    link.mark(dve.tensor_scalar(k, k, -ROUND_MAGIC, None, ALU.add))
                    link.wait()

                def take(dst, src, part):
                    link.mark(dve.scalar_tensor_tensor(out=dst, in0=k, scalar=-part, in1=src, op0=ALU.mult, op1=ALU.add))
                    link.wait()

                link.mark(dve.tensor_copy(ang, pos_i))
                link.wait()
                link.mark(dve.tensor_scalar(ang, ang, cst[:, C_FREQ:C_FREQ + 1], None, ALU.mult))
                link.wait()
                turns_of(ang, 1.0 / (BIG * TWO_PI), 0.0)
                for part in PI_A:
                    take(ang, ang, BIG * part)
                link.mark(dve.tensor_scalar(r_lo, k, -BIG * PI_A4, None, ALU.mult))
                link.wait()
                turns_of(ang, 1.0 / TWO_PI, 0.0)
                for part in (PI_B1, PI_B2, PI_B3):
                    take(ang, ang, part)
                link.mark(dve.tensor_tensor(ang, ang, r_lo, ALU.add))
                link.wait()
                for n, phase in enumerate((0.0, 0.25)):
                    r = rot_tmp[:, 3 - n, :]
                    turns_of(ang, 1.0 / TWO_PI, phase)
                    take(r, ang, PI_B1)
                    take(r, r, PI_B2)
                    take(r, r, PI_B3)
                    link.mark(dve.tensor_scalar(r, r, phase * TWO_PI, PI_SAFE, ALU.add, ALU.min))
                    link.wait()
                    dve.tensor_scalar(r, r, -PI_SAFE, None, ALU.max).then_inc(angles_set, 1)
                dve.wait_ge(tables_set, 2)
                dve.tensor_scalar(sin_t[:, :], sin_t[:, :], cst[0:ROT, C_SIGN:C_SIGN + 1], None, ALU.mult
                                  ).then_inc(o_set, 1)

            def feed_forward(layer, e):
                done = layer * KF
                with dve.Fori(0, N_UP // RING) as t:
                    for j in range(2):
                        n = done + 2 * t + j
                        dve.wait_ge(gate_set, n + 1)
                        dve.wait_ge(w_used, (S_UP1 if layer else S_UP0) + 4 * t + 2 * j + 2)
                        dve.tensor_tensor(hidden[:, 0, :], ps[4 + j][:, :], hidden[:, 0, :], ALU.mult
                                          ).then_inc(hid_set, 1)
                        dve.wait_ge(hthi_set, n + 1)
                        dve.tensor_tensor(ht_lo[:, bass.ds(2 * t + j, 1), :], hidden[:, :, :],
                                          ht_hi[:, bass.ds(2 * t + j, 1), :].bitcast(F32), ALU.subtract
                                          ).then_inc(ht_set, 1)
                if layer == 0:
                    dve.wait_ge(ht_set, KF)
                    rotary_angles()
                norm(e)

            feed_forward(0, 1)

            rot_links = HEADS_ROUND * NG * 3
            max_links = HEADS_ROUND * 2 * 2
            merge_links = 7
            round_links = rot_links + max_links + merge_links
            base = link.n
            with dve.Fori(0, TURNS) as turn:
                for r in range(ROUNDS_BODY):
                    rnd = turn * ROUNDS_BODY + r
                    n_qk = HEADS_ROUND * NG
                    link.n = base + rnd * round_links

                    def rotate(s):
                        g = s % NG
                        if s:
                            dve.wait_ge(qk_set, rnd * n_qk + s)
                        dve.wait_ge(qk_copied, rnd * n_qk + s + 1)
                        x3 = qk[0:ROT, s % 2, :, :]
                        cosv, sinv = cos_t[:, :], sin_t[:, :]

                        def order(a):
                            return a.rearrange("p (m r) -> p r m", r=DIL) if g else a

                        def dst(a):
                            return a.rearrange("p (r m) -> p r m", r=DIL) if g else a

                        for c in range(2):
                            ins = dve.tensor_tensor(dst(rot_a[:, c, :]), dst(qk[0:ROT, s % 2, c, :]), order(cosv), ALU.mult)
                        ins = dve.stream_shuffle(rot_b[:, :, :].rearrange("p a b -> p (a b)"),
                                                 x3.rearrange("p a b -> p (a b)"),
                                                 [(p + ROT // 2) % ROT for p in range(ROT)])
                        link.mark(ins)
                        link.wait()
                        for c in range(2):
                            ins = dve.tensor_tensor(dst(rot_b[:, c, :]), dst(rot_b[:, c, :]), order(sinv), ALU.mult)
                            link.mark(ins)
                        link.wait()
                        dve.tensor_tensor(x3, rot_a[:, :, :], rot_b[:, :, :], ALU.add).then_inc(qk_set, 1)

                    def maxima(h, far):
                        st = st_far if far else st_near
                        if far:
                            dve.wait_ge(far_done, rnd * 2 * HEADS_ROUND + 2 * (h + 1))
                            dst = probs[:, h, BLOCKS_A * P:BLOCKS * P]
                            ins = dve.tensor_tensor(dst[:, 0:512], ps[6][:, :], cst[:, C_MASKB:C_MASKB + 512], ALU.add)
                            ins = dve.tensor_tensor(dst[:, 512:1024], ps[7][:, :], cst[:, C_MASKB:C_MASKB + 512], ALU.add)
                            link.mark(ins)
                            link.wait()
                            ins = dve.tensor_reduce(st[:, 0, h, :], dst.rearrange("p (t n) -> p t n", n=2 * P), AXX, ALU.max)
                            link.mark(ins)
                        else:
                            dve.wait_ge(near_done, rnd * HEADS_ROUND + h + 1)
                            dst = probs[:, h, 0:BLOCKS_A * P]
                            dve.tensor_tensor(dst[:, 0:384], ps[4][:, P:512], cst[:, C_MASKA + P:C_MASKA + 512], ALU.add)
                            ins = dve.tensor_tensor(dst[:, 384:896], ps[5][:, :], cst[:, C_MASKA:C_MASKA + 512], ALU.add)
                            link.mark(ins)
                            link.wait()
                            dve.tensor_reduce(st[:, 0, h, 0:1], dst[:, 0:P], AXX, ALU.max)
                            ins = dve.tensor_reduce(st[:, 0, h, 1:4], dst[:, P:7 * P].rearrange("p (t n) -> p t n", n=2 * P),
                                                    AXX, ALU.max)
                            link.mark(ins)
                        link.wait()
                        dve.tensor_scalar(st[:, 0, h, :], st[:, 0, h, :], -SCALE, None, ALU.mult).then_inc(max_set, 1)

                    rotate(0)
                    rotate(1)
                    maxima(0, 0)
                    rotate(2)
                    rotate(3)
                    maxima(0, 1)
                    rotate(4)
                    maxima(1, 0)
                    rotate(5)
                    maxima(1, 1)

                    dve.wait_ge(far_turned, rnd + 1)
                    rsel = cst[:, C_R:C_R + DIL]
                    link.mark(dve.tensor_tensor(far_sel[:, :, :], ps[4][:, 0:64].rearrange("p (a r) -> p a r", r=DIL),
                                                rsel.unsqueeze(1).broadcast_to([P, 16, DIL]), ALU.mult))
                    link.wait()
                    link.mark(dve.tensor_reduce(far_nat[:, :, :, :].rearrange("p a b c -> p (a b c)"), far_sel[:, :, :],
                                                AXX, ALU.add))
                    link.wait()
                    far_m, far_d = (far_nat[:, :, kind, :].rearrange("p i h -> p h i") for kind in range(2))
                    link.mark(dve.tensor_tensor(m_low[:, :, :], st_near[:, 0, :, :], far_m, ALU.min))
                    link.wait()
                    dve.tensor_tensor(m_diff[:, 0, :, :], m_low[:, :, :], st_near[:, 0, :, :], ALU.subtract)
                    dve.tensor_tensor(m_diff[:, 1, :, :], m_low[:, :, :], far_m, ALU.subtract).then_inc(diff_set, 1)
                    dve.wait_ge(diff_exp, rnd + 1)
                    dve.tensor_tensor(m_w[:, 0, :, :], m_exp[:, 0, :, :], st_near[:, 1, :, :], ALU.mult)
                    link.mark(dve.tensor_tensor(m_w[:, 1, :, :], m_exp[:, 1, :, :], far_d, ALU.mult))
                    link.wait()
                    link.mark(dve.tensor_tensor(m_den[:, :, :], m_w[:, 0, :, :], m_w[:, 1, :, :], ALU.add))
                    link.wait()
                    link.mark(dve.reciprocal(m_den[:, :, :], m_den[:, :, :]))
                    link.wait()
                    dve.tensor_tensor(m_fac[:, 0, :, :], m_exp[:, 0, :, :], m_den[:, :, :], ALU.mult)
                    link.mark(dve.tensor_tensor(m_fac[:, 1, :, :], m_exp[:, 1, :, :], m_den[:, :, :], ALU.mult))
                    link.wait()
                    for h in range(HEADS_ROUND):
                        ins = dve.tensor_tensor(fac_sel[:, :, h, :],
                                                m_fac[:, 1, h, :].unsqueeze(2).broadcast_to([P, TILES, DIL]),
                                                rsel.unsqueeze(1).broadcast_to([P, TILES, DIL]), ALU.mult)
                    ins.then_inc(fac_set, 1)
                    dve.wait_ge(fac_turned, rnd + 1)
                    link_done = dve.tensor_copy(fac_far[:, :, :], ps[5][:, 0:2 * DIL].rearrange("p (h r) -> p h r", h=2))
                    link_done.then_inc(fac_copied, 1)
                    dve.wait_ge(fac_copied, rnd + 1)
                    for h in range(HEADS_ROUND):
                        for i in range(TILES):
                            near = probs[:, h, max(0, 2 * i - 1) * P:(2 * i + 1) * P]
                            far = probs[:, h, (BLOCKS_A + 2 * i) * P:(BLOCKS_A + 2 * i + 2) * P]
                            dve.tensor_scalar(near, near, m_fac[:, 0, h, i:i + 1], None, ALU.mult)
                            ins = dve.tensor_scalar(far, far, fac_far[:, h, i:i + 1], None, ALU.mult)
                        ins.then_inc(probs_set, 1)
                    for h in range(HEADS_ROUND):
                        n = (rnd * HEADS_ROUND + h) * 4
                        for q in range(1, 4, 2):
                            width = 512 if q < 3 else BLOCKS * P - 3 * 512
                            dve.wait_ge(pt_done, n + q + 1)
                            dve.tensor_copy(probs_t[:, h, q * 512:q * 512 + width], ps[4 + q][:, 0:width]
                                            ).then_inc(pt_dve, 1)
                    for h in range(HEADS_ROUND):
                        if h:
                            dve.wait_ge(ot_set, rnd * HEADS_ROUND + h)
                        dve.wait_ge(near_copied, rnd * HEADS_ROUND + h + 1)
                        dve.tensor_tensor(o_sum[:, :].rearrange("p (m r) -> p m r", r=DIL),
                                          ps[2 * h + 1][:, :].rearrange("p (r m) -> p m r", r=DIL),
                                          o_near[:, :].rearrange("p (m r) -> p m r", r=DIL), ALU.add).then_inc(o_set, 1)
                        dve.wait_ge(othi_set, rnd * HEADS_ROUND + h + 1)
                        at = bass.ds(rnd * HEADS_ROUND + h, 1)
                        dve.tensor_tensor(ot_lo[:, at, :], o_sum[:, :].rearrange("p (a n) -> p a n", a=1),
                                          ot_hi[:, at, :].bitcast(F32), ALU.subtract).then_inc(ot_set, 1)
            link.n = base + TURNS * ROUNDS_BODY * round_links
            norm(2)
            feed_forward(1, 3)


_INS = ["x", "positions", "ev_w_in", "ev_conv_w", "ev_conv_b", "ev_conv_ln_g", "ev_conv_ln_b", "ev_sgu_ln_g",
        "ev_sgu_ln_b", "ev_w_spatial", "ev_b_spatial", "ev_w_out", "od_w_qkv", "od_w_out", "ffn_w_gate",
        "ffn_w_up", "ffn_w_down", "ln_g", "ln_b"]


def kernel(**inputs):
    import concourse.bacc as _bacc
    from concourse.bass_utils import run_bass_kernel_spmd as _run

    nc = _bacc.Bacc("TRN2", target_bir_lowering=False, num_devices=1)
    arrays, args = {}, []
    given = [(n, inputs[n]) for n in _INS] + [("ident", np.eye(P, dtype=np.float32)), ("const", constant_table())]
    for name, value in given:
        a = np.ascontiguousarray(value)
        arrays[f"in_{name}_dram"] = a
        args.append(nc.dram_tensor(f"in_{name}_dram", a.shape, mybir.dt.from_np(a.dtype), kind="ExternalInput").ap())
    args.append(nc.dram_tensor("out_0_dram", (1, SEQ, D_MODEL), F32, kind="ExternalOutput").ap())
    trunk(nc, *args)
    r = _run(nc, [arrays], core_ids=[0])
    return r.results[0]["out_0_dram"]
```
